# Optimizing a Trainium2 kernel written in Bass

```python
import math
import jax, jax.numpy as jnp
from jax import lax
import numpy as np

D_MODEL = 2048
BATCH = 1
SEQ = 256
DEPTH = 1

MIX_WIDTH = D_MODEL
SSM_WIDTH = MIX_WIDTH // 2
ATTN_WIDTH = MIX_WIDTH - SSM_WIDTH
SSM_GROUP = 16
SSM_GROUPS = SSM_WIDTH // SSM_GROUP
SSM_STATE = 64
HEAD_DIM = 64
N_HEADS = ATTN_WIDTH // HEAD_DIM
Q_BLOCK = 128
D_FF = ((8 * D_MODEL // 3 + 255) // 256) * 256
N_MOD = 6
EPS = 1e-6
DT_MIN = 1e-3
DT_MAX = 1e-1
IN_COLS = SSM_WIDTH + 3 * ATTN_WIDTH

kernel_name = "hybrid_s5_stickbreaking_adaln_block"

def rmsnorm(x, gain):
    xf = x.astype(jnp.float32)
    xf = xf * lax.rsqrt(jnp.mean(xf * xf, axis=-1, keepdims=True) + EPS)
    return (xf * gain.astype(jnp.float32)).astype(x.dtype)

def s5_mixer(u, a_re, a_im, log_dt, b_re, b_im, c_re, c_im, d_skip, w_glu):
    bsz, seqlen, _ = u.shape
    f32 = jnp.float32
    uf = u.astype(f32).reshape(bsz, seqlen, SSM_GROUPS, SSM_GROUP)
    lam = lax.complex(a_re.astype(f32), a_im.astype(f32))
    dt = jnp.exp(log_dt.astype(f32))[:, None]
    lam_bar = jnp.exp(lam * dt)
    b = lax.complex(b_re.astype(f32), b_im.astype(f32))
    b_bar = ((lam_bar - 1.0) / lam)[..., None] * b
    bu = jnp.einsum('blgh,gph->blgp', uf.astype(jnp.complex64), b_bar)
    a = jnp.broadcast_to(lam_bar, bu.shape)

    def combine(left, right):
        a_l, b_l = left
        a_r, b_r = right
        return a_r * a_l, a_r * b_l + b_r

    _, states = lax.associative_scan(combine, (a, bu), axis=1)
    c = lax.complex(c_re.astype(f32), c_im.astype(f32))
    y = jnp.einsum('ghp,blgp->blgh', c, states).real + d_skip.astype(f32) * uf
    y = jax.nn.gelu(y.reshape(bsz, seqlen, SSM_WIDTH))
    y = y * jax.nn.sigmoid(y @ w_glu.astype(f32))
    return y.astype(u.dtype)

def stick_breaking_attention(q, k, v):
    bsz, seqlen, nh, dh = q.shape
    nblk = seqlen // Q_BLOCK
    f32 = jnp.float32
    qf = q.astype(f32) * (1.0 / math.sqrt(dh))
    kf = k.astype(f32)
    vf = v.astype(f32)
    qb = qf.reshape(bsz, nblk, Q_BLOCK, nh, dh).transpose(1, 0, 3, 2, 4)
    key_pos = jnp.arange(seqlen)

    def one_block(args):
        q_blk, blk_idx = args
        q_pos = blk_idx * Q_BLOCK + jnp.arange(Q_BLOCK)
        z = jnp.einsum('bhqd,bkhd->bhqk', q_blk, kf)
        past = key_pos[None, :] < q_pos[:, None]
        log_keep = jnp.where(past, jax.nn.log_sigmoid(-z), 0.0)
        after = lax.cumsum(log_keep, axis=3, reverse=True) - log_keep
        log_w = jax.nn.log_sigmoid(z) + after
        w = jnp.where(past, jnp.exp(log_w), 0.0)
        return jnp.einsum('bhqk,bkhd->bhqd', w, vf)

    out = lax.map(one_block, (qb, jnp.arange(nblk)))
    out = out.transpose(1, 0, 3, 2, 4).reshape(bsz, seqlen, nh * dh)
    return out.astype(q.dtype)

def setup_inputs(seed: int = 0) -> dict:
    key = jax.random.key(seed)
    ks = jax.random.split(key, 24)
    f32 = jnp.float32
    nrm = lambda k, shape, s: (jax.random.normal(k, shape, f32) * s)
    x = jax.random.normal(ks[0], (BATCH, SEQ, D_MODEL), f32)
    c = jax.random.normal(ks[1], (BATCH, D_MODEL), f32)
    w_ada = nrm(ks[2], (DEPTH, D_MODEL, N_MOD * D_MODEL), D_MODEL ** -0.5)
    b_ada = nrm(ks[3], (DEPTH, N_MOD * D_MODEL), 0.01)
    g_mix = 1.0 + nrm(ks[4], (DEPTH, D_MODEL), 0.02)
    w_in = nrm(ks[5], (DEPTH, D_MODEL, IN_COLS), D_MODEL ** -0.5)
    a_re = -0.5 + nrm(ks[6], (DEPTH, SSM_GROUPS, SSM_STATE), 0.01)
    a_im = (math.pi * jnp.arange(SSM_STATE, dtype=f32))[None, None, :] + nrm(ks[7], (DEPTH, SSM_GROUPS, SSM_STATE), 0.01)
    log_dt = jax.random.uniform(ks[8], (DEPTH, SSM_GROUPS), f32, math.log(DT_MIN), math.log(DT_MAX))
    b_re = nrm(ks[9], (DEPTH, SSM_GROUPS, SSM_STATE, SSM_GROUP), (2 * SSM_GROUP) ** -0.5)
    b_im = nrm(ks[10], (DEPTH, SSM_GROUPS, SSM_STATE, SSM_GROUP), (2 * SSM_GROUP) ** -0.5)
    c_re = nrm(ks[11], (DEPTH, SSM_GROUPS, SSM_GROUP, SSM_STATE), SSM_STATE ** -0.5)
    c_im = nrm(ks[12], (DEPTH, SSM_GROUPS, SSM_GROUP, SSM_STATE), SSM_STATE ** -0.5)
    d_skip = nrm(ks[13], (DEPTH, SSM_GROUPS, SSM_GROUP), 1.0)
    w_glu = nrm(ks[14], (DEPTH, SSM_WIDTH, SSM_WIDTH), SSM_WIDTH ** -0.5)
    q_gain = 1.0 + nrm(ks[15], (DEPTH, HEAD_DIM), 0.02)
    k_gain = 1.0 + nrm(ks[16], (DEPTH, HEAD_DIM), 0.02)
    g_ssm_out = 1.0 + nrm(ks[17], (DEPTH, SSM_WIDTH), 0.02)
    g_attn_out = 1.0 + nrm(ks[18], (DEPTH, ATTN_WIDTH), 0.02)
    w_out = nrm(ks[19], (DEPTH, MIX_WIDTH, D_MODEL), MIX_WIDTH ** -0.5)
    g_ffn = 1.0 + nrm(ks[20], (DEPTH, D_MODEL), 0.02)
    w_gate = nrm(ks[21], (DEPTH, D_MODEL, D_FF), D_MODEL ** -0.5)
    w_up = nrm(ks[22], (DEPTH, D_MODEL, D_FF), D_MODEL ** -0.5)
    w_down = nrm(ks[23], (DEPTH, D_FF, D_MODEL), D_FF ** -0.5)
    return {"x": x, "c": c, "w_ada": w_ada, "b_ada": b_ada, "g_mix": g_mix, "w_in": w_in,
            "a_re": a_re, "a_im": a_im, "log_dt": log_dt, "b_re": b_re, "b_im": b_im,
            "c_re": c_re, "c_im": c_im, "d_skip": d_skip, "w_glu": w_glu,
            "q_gain": q_gain, "k_gain": k_gain, "g_ssm_out": g_ssm_out, "g_attn_out": g_attn_out,
            "w_out": w_out, "g_ffn": g_ffn, "w_gate": w_gate, "w_up": w_up, "w_down": w_down}

def reference(x, c, w_ada, b_ada, g_mix, w_in, a_re, a_im, log_dt, b_re, b_im, c_re, c_im,
              d_skip, w_glu, q_gain, k_gain, g_ssm_out, g_attn_out, w_out, g_ffn, w_gate,
              w_up, w_down):
    bsz, seqlen, _ = x.shape
    h = x
    cond = jax.nn.silu(c.astype(jnp.float32))
    for layer in range(DEPTH):
        mod = (cond @ w_ada[layer].astype(jnp.float32) + b_ada[layer].astype(jnp.float32)).astype(x.dtype)
        shift_m, scale_m, gate_m, shift_f, scale_f, gate_f = jnp.split(mod[:, None, :], N_MOD, axis=-1)

        xm = rmsnorm(h, g_mix[layer]) * (1.0 + scale_m) + shift_m
        proj = xm @ w_in[layer]
        u, q, k, v = jnp.split(proj, [SSM_WIDTH, SSM_WIDTH + ATTN_WIDTH, SSM_WIDTH + 2 * ATTN_WIDTH], axis=-1)
        y_ssm = s5_mixer(u, a_re[layer], a_im[layer], log_dt[layer], b_re[layer], b_im[layer],
                         c_re[layer], c_im[layer], d_skip[layer], w_glu[layer])
        q = rmsnorm(q.reshape(bsz, seqlen, N_HEADS, HEAD_DIM), q_gain[layer])
        k = rmsnorm(k.reshape(bsz, seqlen, N_HEADS, HEAD_DIM), k_gain[layer])
        v = v.reshape(bsz, seqlen, N_HEADS, HEAD_DIM)
        y_attn = stick_breaking_attention(q, k, v)
        mixed = jnp.concatenate([rmsnorm(y_ssm, g_ssm_out[layer]),
                                 rmsnorm(y_attn, g_attn_out[layer])], axis=-1)
        h = h + gate_m * (mixed @ w_out[layer])

        xf = rmsnorm(h, g_ffn[layer]) * (1.0 + scale_f) + shift_f
        ffn = (jax.nn.silu(xf @ w_gate[layer]) * (xf @ w_up[layer])) @ w_down[layer]
        h = h + gate_f * ffn
    return h


_drawn_inputs = setup_inputs


def setup_inputs(seed=0):
    import zlib

    import numpy as np

    out = dict(_drawn_inputs(seed))
    spreads = {}
    factors = {'b_ada': 3.413,
     'g_mix': 5.591,
     'a_re': 8.0,
     'q_gain': 8.0,
     'k_gain': 8.0,
     'g_ssm_out': 7.675,
     'g_attn_out': 7.515,
     'g_ffn': 4.33}
    for name, (base, spread) in spreads.items():
        noise = np.random.default_rng([zlib.crc32(name.encode()), seed]).standard_normal(out[name].shape)
        drawn = base * np.exp(spread * noise) if base else spread * noise
        out[name] = __import__('jax').numpy.asarray(drawn.astype(out[name].dtype))
    for name, factor in factors.items():
        out[name] = (out[name] * factor).astype(out[name].dtype)
    return out
```

```python
import math
from contextlib import ExitStack

import numpy as np
import concourse.bass as bass
from concourse import mybir

P = 128
D = 2048
T = 256
KD = D // P
SW = 1024
KS = SW // P
GROUPS, GH, NS = 64, 16, 64
ST = GROUPS * NS // P
DH = 64
FF = 5632
KF = FF // P
NMOD = 6 * D
EPS = 1e-6
TC = 128
NC = T // TC
CK, CW = 2, 512
RAW, SPL, ADA = 8, 4, 4
FB = CW // P

IN_B, IN_C = 4 * SW // CW, KD // CK
GLU_B, GLU_C = SW // CW, KS // CK
OUT_B, OUT_C = D // CW, KD // CK
UP_B, UP_C = 2 * FF // CW, KD // CK
DN_B, DN_C = D // CW, KF // CK
GLU_C0 = IN_B * IN_C
OUT_C0 = GLU_C0 + GLU_B * GLU_C
UP_C0 = OUT_C0 + OUT_B * OUT_C
DN_C0 = UP_C0 + UP_B * UP_C
ALL_C = DN_C0 + DN_B * DN_C
GLU_B0 = IN_B
OUT_B0 = GLU_B0 + GLU_B
UP_B0 = OUT_B0 + OUT_B
DN_B0 = UP_B0 + UP_B
ADA_G = NMOD // CW
ADA_C = KD // CK
ADA_IN0 = 2 * D // CW
ADA_MID0 = ADA_IN0 + IN_B
ADA_UP0 = ADA_MID0 + 4


def build(nc, a):
    f32, f32r, bf16, i32 = mybir.dt.float32, mybir.dt.float32r, mybir.dt.bfloat16, mybir.dt.int32
    ALU, ACT, AX = mybir.AluOpType, mybir.ActivationFunctionType, mybir.AxisListType
    ds = bass.ds

    def chunks(w):
        return w.rearrange("(c t p) n -> c p t n", t=CK, p=P)

    w_in, w_glu, w_out = chunks(a["w_in"]), chunks(a["w_glu"]), chunks(a["w_out"])
    w_gate, w_up, w_down = chunks(a["w_gate"]), chunks(a["w_up"]), chunks(a["w_down"])
    w_ada = chunks(a["w_ada"])

    ctx = ExitStack()
    with ctx:
        def sb(name, shape, dt=f32):
            return ctx.enter_context(nc.sbuf_tensor(name, shape, dt))

        def sem(name):
            return ctx.enter_context(nc.semaphore(name))

        raw = sb("raw", [P, RAW, CK, CW])
        hi = sb("hi", [P, SPL, CK, CW], f32r)
        lo = sb("lo", [P, SPL, CK, CW], f32r)
        resid = sb("resid", [P, KD, T])
        xs_at = (nc.sbuf_base + 31) // 32 * 32
        xs = sb("xs", [P, KD, 2 * T], f32r)
        ar_at = (nc.sbuf_base + 31) // 32 * 32
        hid = sb("hid", [P, KF, 2 * T], f32r)
        ident = sb("ident", [P, P])
        ones = sb("ones", [P, P])
        head_ones = sb("head_ones", [P, P])
        neg_tri = sb("neg_tri", [P, P])
        neg_ones = sb("neg_ones", [P, P])
        ident_b = sb("ident_b", [P, P], bf16)
        mask_b = sb("mask_b", [P, P], bf16)
        vec1 = sb("vec1", [P, P])
        vec2 = sb("vec2", [P, 106])
        mods = sb("mods", [P, NMOD // P])
        a_mix = sb("a_mix", [P, KD])
        a_ffn = sb("a_ffn", [P, KD])
        cs = sb("cs", [P, KD])
        eps = sb("eps", [P, 5])
        grp = sb("grp", [P, 2])
        rstd = sb("rstd", [P, T])
        act_tmp = sb("act_tmp", [P, 2, T])

        def over(name, base, at, shape, dt=f32):
            return nc.alloc_sbuf_tensor_at(name, shape, dt, offset=base + 4 * at)

        tabs = over("tabs", ar_at, 0, [P, 2, ST, TC])
        uqkv = over("uqkv", ar_at, 8192, [P, 32, T])
        b_bar = over("b_bar", ar_at, 16384, [P, 2, ST, GH])
        ada_acc = over("ada_acc", ar_at, 17408, [P, 2, CW])
        ada_raw = over("ada_raw", ar_at, 18432, [P, ADA, CK, CW])
        x_tok = over("x_tok", ar_at, 8192, [P, 2, D])
        x_n = over("x_n", ar_at, 8192, [P, KD, T])
        b_raw = over("b_raw", ar_at, 12288, [P, 2, ST, GH])
        rows = over("rows", ar_at, 13312, [P, 2, P])
        ldt = over("ldt", ar_at, 13568, [P, GROUPS])
        tiny = over("tiny", ar_at, 13632, [P, 24, ST])
        tiny_i = over("tiny_i", ar_at, 14400, [P, ST], i32)
        nrm = over("nrm", ar_at, 14432, [P, T])
        sqx = over("sqx", ar_at, 14720, [P, 2, 2, T])
        ptmp = over("ptmp", xs_at, 0, [P, 2, ST, TC // 2])
        ptiny = over("ptiny", xs_at, 4096, [P, 3, ST])
        btmp = over("btmp", xs_at, 4224, [P, 2, ST, GH])
        c_raw = over("c_raw", xs_at, 0, [P, KS, 2, NS])
        bx = over("bx", xs_at, 1024, [P, 2, 4, 2, GH])
        cx = over("cx", xs_at, 1280, [P, 2, 2, NS])
        bc = over("bc", xs_at, 1536, [P, 2, 4, P])
        dem = over("dem", xs_at, 2560, [P, 4, T])
        v_y = over("v_y", xs_at, 3584, [P, 2, T])
        carry = over("carry", xs_at, 4096, [P, 4])
        rem = over("rem", xs_at, 4128, [P, 4, T])
        u_st = over("u_st", xs_at, 5152, [P, 2, T])
        qk_n = over("qk_n", xs_at, 5664, [P, 2, T])
        v_st = over("v_st", xs_at, 6176, [P, T])
        v_t = over("v_t", xs_at, 6432, [P, 2, P])
        qk_a = over("qk_a", xs_at, 6688, [P, 2, T])
        qk_r = over("qk_r", xs_at, 7200, [P, 2, T])
        sp = over("sp", xs_at, 6688, [P, 3, P])
        w_t = over("w_t", xs_at, 7200, [P, 3, P])
        glu_z = over("glu_z", ar_at, 12288, [P, 2, T])
        glu_s = over("glu_s", ar_at, 12800, [P, 2, T])
        mix_f = over("mix_f", ar_at, 13312, [P, 2, T])
        msq = over("msq", ar_at, 13824, [P, 2, T])
        rs2 = over("rs2", ar_at, 14336, [P, 2, 2, T])
        ffn_f = over("ffn_f", ar_at, 15360, [P, 2, T])
        out_s = over("out_s", xs_at, 0, [P, 2, 2, CW])
        h_out = over("h_out", xs_at, 2048, [P, 2, FB, T])

        acc = ctx.enter_context(nc.psum_tensor("acc", [P, 8, 512], f32))

        def ps(bank, lo_=0, n=512):
            return acc[:, bank, lo_:lo_ + n]

        rows_in, x_in, b_in, c_in, out_done = sem("rows_in"), sem("x_in"), sem("b_in"), sem("c_in"), sem("out_done")
        raw_full = [sem(f"raw_full{s}") for s in range(RAW)]
        ada_full = [sem(f"ada_full{s}") for s in range(ADA)]
        hi_ready, lo_ready = sem("hi_ready"), sem("lo_ready")
        chunk_done = sem("chunk_done")
        acc_ready = sem("acc_ready")
        acc_free = sem("acc_free")
        ada_mac, ada_sum, mod_ready = sem("ada_mac"), sem("ada_sum"), sem("mod_ready")
        cols_ready = sem("cols_ready")
        dve_const = sem("dve_const")
        rows_t, vec_ready, cs_ready, lam_ready = sem("rows_t"), sem("vec_ready"), sem("cs_ready"), sem("lam_ready")
        dve_chain, pool_chain, act_chain = sem("dve_chain"), sem("pool_chain"), sem("act_chain")
        tab_ready, bbar_ready = sem("tab_ready"), sem("bbar_ready")
        xt_ps, xt_ready, sqx_ready, ssx_ready = sem("xt_ps"), sem("xt_ready"), sem("sqx_ready"), sem("ssx_ready")
        sqx_used, rx_ready = sem("sqx_used"), sem("rx_ready")
        xf_ready, xhi_ready, xlo_ready = sem("xf_ready"), sem("xhi_ready"), sem("xlo_ready")
        cneg = sem("cneg")
        bcx_ready, bc_ps, bc_ready, u_ready = sem("bcx_ready"), sem("bc_ps"), sem("bc_ready"), sem("u_ready")
        bu_ready, bu_used, s5_chain = sem("bu_ready"), sem("bu_used"), sem("s5_chain")
        rem_ready, rem_used, y_ready = sem("rem_ready"), sem("rem_used"), sem("y_ready")
        qsq_ready, qss_ready, qr_ready, qn_chain = sem("qsq_ready"), sem("qss_ready"), sem("qr_ready"), sem("qn_chain")
        qt_ready, qrn_ready, qkn_ready = sem("qt_ready"), sem("qrn_ready"), sem("qkn_ready")
        vst_ready, vt_ps, vt_ready = sem("vst_ready"), sem("vt_ps"), sem("vt_ready")
        z_ready, ln_ready, sp_ready, zs_ready, w_ready = sem("z_ready"), sem("ln_ready"), sem("sp_ready"), sem("zs_ready"), sem("w_ready")
        act_z = sem("act_z")
        av_ready, attn_ready = sem("av_ready"), sem("attn_ready")
        gelu_ready, yhi_ready, ylo_ready = sem("gelu_ready"), sem("yhi_ready"), sem("ylo_ready")
        sig_ready, y2_ready = sem("sig_ready"), sem("y2_ready")
        msq_ready, msq_used, mr_ready = sem("msq_ready"), sem("msq_used"), sem("mr_ready")
        mr_done = sem("mr_done")
        mf_ready, mhi_ready, mlo_ready = sem("mf_ready"), sem("mhi_ready"), sem("mlo_ready")
        h_ready, fsq_ready, fsq_used, fss_ready, fr_ready = sem("h_ready"), sem("fsq_ready"), sem("fsq_used"), sem("fss_ready"), sem("fr_ready")
        ff_ready, fhi_ready, flo_ready = sem("ff_ready"), sem("fhi_ready"), sem("flo_ready")
        g_act, h_prod, hid_hi, hid_lo = sem("g_act"), sem("h_prod"), sem("hid_hi"), sem("hid_lo")
        d_red, o_ready, ot_ps, ot_ready = sem("d_red"), sem("o_ready"), sem("ot_ps"), sem("ot_ready")

        block = ctx.enter_context(nc.Block())

        def store(eng, b):
            for i in range(2):
                eng.wait_ge(ot_ready, 2 * b + i + 3)
                eng.dma_start(a["out"][i * P:(i + 1) * P, b * CW:(b + 1) * CW], out_s[:, b % 2, i, :]).then_inc(out_done, 16)

        @block.sync
        def _(sp_):
            def weights(first_chunk, k, slot, src, cols):
                sp_.dma_start(raw[:, slot, :, cols[0]:cols[1]], src).then_inc(raw_full[slot], 16)

            def ada_chunk(chunk, c, s, group, wait=True):
                if wait:
                    sp_.wait_ge(ada_mac, CK * (chunk - ADA) + CK)
                sp_.dma_start(ada_raw[:, s, :, :], w_ada[c, :, :, ds(group * CW, CW)]).then_inc(ada_full[s], 16)

            def row(i, at, n, src):
                sp_.dma_start(rows[at:at + n, i, :], src).then_inc(rows_in, 16)

            row(0, 0, 96, a["b_ada"].rearrange("(r c) -> r c", c=P))
            row(0, 96, 16, a["c"].rearrange("(r c) -> r c", c=P))
            row(0, 112, 16, a["g_mix"].rearrange("(r c) -> r c", c=P))
            row(1, 0, 16, a["g_ffn"].rearrange("(r c) -> r c", c=P))
            row(1, 16, 8, a["g_ssm_out"].rearrange("(r c) -> r c", c=P))
            row(1, 24, 8, a["g_attn_out"].rearrange("(r c) -> r c", c=P))
            row(1, 32, 8, a["d_skip"].rearrange("(r g) h -> r (g h)", g=8))
            row(1, 40, 32, a["a_re"].rearrange("(r g) n -> r (g n)", g=2))
            row(1, 72, 32, a["a_im"].rearrange("(r g) n -> r (g n)", g=2))
            for i, name in enumerate(("q_gain", "k_gain")):
                sp_.dma_start(rows[104 + i:105 + i, 1, :].rearrange("o (g n) -> o g n", g=2),
                              a[name].rearrange("(o g n) -> o g n", o=1, g=1).to_broadcast([1, 2, DH])
                              ).then_inc(rows_in, 16)
            sp_.dma_start(ldt[:, :], a["log_dt"].rearrange("(o n) -> o n", o=1).to_broadcast([P, GROUPS])
                          ).then_inc(rows_in, 16)
            for c in range(ADA_C):
                ada_chunk(c, c, c % ADA, 0, wait=c >= ADA)
            for i in range(2):
                sp_.dma_start(x_tok[:, i, :], a["x"][i * P:(i + 1) * P, :]).then_inc(x_in, 16)
            for i, name in enumerate(("b_re", "b_im")):
                sp_.dma_start(b_raw[:, i, :, :], a[name].rearrange("(t g) n h -> (g n) t h", g=2)).then_inc(b_in, 16)
            with sp_.Fori(1, ADA_IN0) as g:
                for c in range(ADA_C):
                    ada_chunk(g * ADA_C + c, c, c % ADA, g)
            for c in range(IN_C):
                sp_.dma_start(raw[:, c, :, :], w_in[c, :, :, 0:CW]).then_inc(raw_full[c], 16)
                ada_chunk(ADA_IN0 * ADA_C + c, c, c % ADA, ADA_IN0)
            with sp_.Fori(1, IN_B) as b:
                for c in range(IN_C):
                    sp_.wait_ge(lo_ready, b * IN_C + c - RAW + 1)
                    sp_.dma_start(raw[:, c, :, :], w_in[c, :, :, ds(b * CW, CW)]).then_inc(raw_full[c], 16)
                    ada_chunk((b + ADA_IN0) * ADA_C + c, c, c % ADA, b + ADA_IN0)
            for c in range(GLU_B * GLU_C):
                sp_.wait_ge(lo_ready, GLU_C0 + c - RAW + 1)
                sp_.dma_start(raw[:, c % RAW, :, :],
                              w_glu[c % GLU_C, :, :, (c // GLU_C) * CW:(c // GLU_C + 1) * CW]).then_inc(raw_full[c % RAW], 16)
            sp_.wait_ge(chunk_done, SPL + GLU_C0)
            for i, name in enumerate(("c_re", "c_im")):
                sp_.dma_start(c_raw[:, :, i, :], a[name].rearrange("(f g) h n -> (g h) f n", f=KS)).then_inc(c_in, 16)
            with sp_.Fori(0, 4) as g:
                for c in range(ADA_C):
                    ada_chunk((g + ADA_MID0) * ADA_C + c, c, c % ADA, g + ADA_MID0)
            for n in range(OUT_B * OUT_C):
                b, c = divmod(n, OUT_C)
                sp_.wait_ge(lo_ready, OUT_C0 + n - RAW + 1)
                sp_.dma_start(raw[:, c, :, :], w_out[(c + KS // CK) % OUT_C, :, :, b * CW:(b + 1) * CW]).then_inc(raw_full[c], 16)

            def up_block(b):
                for c in range(UP_C):
                    sp_.wait_ge(lo_ready, b * UP_C + (UP_C0 + c - RAW + 1))
                    for w, cols in ((w_gate, (0, 256)), (w_up, (256, 512))):
                        sp_.dma_start(raw[:, c, :, cols[0]:cols[1]], w[c, :, :, ds(b * 256, 256)]).then_inc(raw_full[c], 16)

            with sp_.Fori(0, 4) as g:
                for half in range(2):
                    up_block(g * 2 + half)
                    for c in range(ADA_C // 2 * half, ADA_C // 2 * (half + 1)):
                        ada_chunk((g + ADA_UP0) * ADA_C + c, c, c % ADA, g + ADA_UP0)
            with sp_.Fori(8, UP_B) as b:
                up_block(b)
            for b in range(DN_B):
                for c in range(DN_C):
                    n = b * DN_C + c
                    sp_.wait_ge(lo_ready, DN_C0 + n - RAW + 1)
                    sp_.dma_start(raw[:, n % RAW, :, :], w_down[c, :, :, b * CW:(b + 1) * CW]).then_inc(raw_full[n % RAW], 16)
                if b >= 1:
                    store(sp_, b - 1)
            store(sp_, DN_B - 1)
            sp_.wait_ge(out_done, 16 * 2 * DN_B)

        @block.gpsimd
        def _(pool):
            n = [0]

            def link(ins):
                n[0] += 1
                ins.then_inc(pool_chain, 1)
                pool.wait_ge(pool_chain, n[0])

            g = nc.gpsimd
            link(g.memset(ident[:, :], 0.0))
            link(g.affine_select(out=ident[:, :], in_=ident[:, :], compare_op=ALU.not_equal, fill=1.0, base=0,
                                 pattern=[[-1, P]], channel_multiplier=1))
            g.memset(ones[:, :], 1.0).then_inc(cols_ready, 1)
            link(g.memset(neg_ones[:, :], -1.0))
            link(g.affine_select(out=neg_tri[:, :], in_=neg_ones[:, :], compare_op=ALU.is_ge, fill=0.0, base=0,
                                 pattern=[[-1, P]], channel_multiplier=1))
            link(g.affine_select(out=head_ones[:, 0:DH], in_=ones[:, 0:DH], compare_op=ALU.is_ge, fill=0.0, base=DH - 1,
                                 pattern=[[0, DH]], channel_multiplier=-1))
            link(g.affine_select(out=head_ones[:, DH:P], in_=ones[:, DH:P], compare_op=ALU.is_ge, fill=0.0, base=-DH,
                                 pattern=[[0, DH]], channel_multiplier=1))
            link(g.tensor_copy(ident_b[:, :], ident[:, :]))
            link(g.memset(mask_b[:, :], -1e30))
            link(g.affine_select(out=mask_b[:, :], in_=mask_b[:, :], compare_op=ALU.is_ge, fill=0.0, base=0,
                                 pattern=[[-1, P]], channel_multiplier=1))
            link(g.memset(grp[:, :], 1.0))
            for q in range(6, -1, -1):
                link(g.affine_select(out=grp[:, 1:2], in_=grp[:, 1:2], compare_op=ALU.is_ge, fill=float(q % 2),
                                     base=-16 * (q + 1), pattern=[[0, 1]], channel_multiplier=1))
            link(g.tensor_tensor(grp[:, 0:1], ones[:, 0:1], grp[:, 1:2], ALU.subtract))
            for i, v in enumerate((D * EPS, DH * EPS, SW * EPS, -0.5 * math.log(2))):
                link(g.memset(eps[:, i:i + 1], v))
            g.memset(eps[:, 4:5], 1.5).then_inc(cols_ready, 1)

            pool.wait_ge(lam_ready, 1)
            cosp, sinp = tabs[:, 0, :, :], tabs[:, 1, :, :]

            def unit(j):
                c_, s_ = cosp[:, :, j], sinp[:, :, j]
                t0, t1 = ptiny[:, 0, :], ptiny[:, 1, :]
                link(g.tensor_tensor(t0, c_, c_, ALU.mult))
                link(g.tensor_tensor(t1, s_, s_, ALU.mult))
                link(g.tensor_tensor(t0, t0, t1, ALU.add))
                link(g.tensor_scalar(t0, t0, -0.5, 1.5, ALU.mult, ALU.add))
                link(g.tensor_tensor(c_, c_, t0, ALU.mult))
                link(g.tensor_tensor(s_, s_, t0, ALU.mult))

            link(g.tensor_copy(cosp[:, :, 0], tiny[:, 0, :]))
            link(g.tensor_copy(sinp[:, :, 0], tiny[:, 1, :]))
            unit(0)
            w = 1
            while w < TC:
                def col(x):
                    return x[:, :, w - 1:w].to_broadcast([P, ST, w])
                p0, p1 = ptmp[:, 0, :, 0:w], ptmp[:, 1, :, 0:w]
                c0, s0, c1, s1 = cosp[:, :, 0:w], sinp[:, :, 0:w], cosp[:, :, w:2 * w], sinp[:, :, w:2 * w]
                link(g.tensor_tensor(p0, c0, col(cosp), ALU.mult))
                link(g.tensor_tensor(p1, s0, col(sinp), ALU.mult))
                link(g.tensor_tensor(c1, p0, p1, ALU.subtract))
                link(g.tensor_tensor(p0, c0, col(sinp), ALU.mult))
                link(g.tensor_tensor(p1, s0, col(cosp), ALU.mult))
                link(g.tensor_tensor(s1, p0, p1, ALU.add))
                w *= 2
                unit(w - 1)
            g.tensor_copy(ptiny[:, 2, :], ptiny[:, 0, :]).then_inc(tab_ready, 1)

            pool.wait_ge(b_in, 32)
            f_re = tiny[:, 2, :].unsqueeze(2).to_broadcast([P, ST, GH])
            f_im = tiny[:, 3, :].unsqueeze(2).to_broadcast([P, ST, GH])
            b0, b1 = btmp[:, 0, :, :], btmp[:, 1, :, :]
            link(g.tensor_tensor(b0, b_raw[:, 0, :, :], f_re, ALU.mult))
            link(g.tensor_tensor(b1, b_raw[:, 1, :, :], f_im, ALU.mult))
            link(g.tensor_tensor(b_bar[:, 0, :, :], b0, b1, ALU.subtract))
            link(g.tensor_tensor(b0, b_raw[:, 1, :, :], f_re, ALU.mult))
            link(g.tensor_tensor(b1, b_raw[:, 0, :, :], f_im, ALU.mult))
            g.tensor_tensor(b_bar[:, 1, :, :], b0, b1, ALU.add).then_inc(bbar_ready, 1)

            def low(value, slot, s):
                pool.wait_ge(hi_ready, value + 1)
                g.tensor_tensor(lo[:, s, :, :], raw[:, slot, :, :], hi[:, s, :, :].bitcast(f32), ALU.subtract).then_inc(lo_ready, 1)

            with pool.Fori(0, IN_B) as b:
                for c in range(IN_C):
                    low(b * IN_C + c, c % RAW, c % SPL)

            for c in range(SPL):
                low(GLU_C0 + c, c, c)
            pool.wait_ge(chunk_done, SPL + GLU_C0)
            pool.wait_ge(c_in, 32)
            link(g.tensor_scalar(c_raw[:, :, 1, :], c_raw[:, :, 1, :], -1.0, None, ALU.mult))
            pool.wait_ge(bbar_ready, 1)
            with pool.Fori(0, KS) as ft:
                pool.wait_ge(bc_ps, ft + 1)
                pool.wait_ge(cols_ready, 2)
                for q in range(2):
                    g.tensor_tensor(bx[:, :, :, q, :], b_bar[:, :, ds(ft * 4, 4), :],
                                    head_ones[:, 127 * q:127 * q + 1].unsqueeze(2).unsqueeze(3).to_broadcast([P, 2, 4, GH]),
                                    ALU.mult).then_inc(bcx_ready, 1)
                for q in range(2):
                    g.tensor_tensor(cx[:, :, q, :], c_raw[:, ds(ft, 1), :, :].rearrange("p o r n -> p (o r) n"),
                                          grp[:, q:q + 1].unsqueeze(2).to_broadcast([P, 2, NS]), ALU.mult).then_inc(bcx_ready, 1)
                pool.wait_ge(qt_ready, ft + 1)
                g.tensor_tensor(qk_a[:, :, :], qk_a[:, :, :], qk_r[:, :, :], ALU.mult).then_inc(qn_chain, 1)
                pool.wait_ge(qn_chain, ft * 2 + 1)
                g.tensor_tensor(qk_a[:, :, :], eps[:, 4:5].unsqueeze(2).to_broadcast([P, 2, T]), qk_a[:, :, :],
                                ALU.subtract).then_inc(qn_chain, 1)
                pool.wait_ge(qn_chain, ft * 2 + 2)
                g.tensor_tensor(qk_r[:, :, :], qk_r[:, :, :], qk_a[:, :, :], ALU.mult).then_inc(qrn_ready, 1)

            for c in range(SPL, RAW):
                low(GLU_C0 + c, c, c % SPL)
            for first, count in ((OUT_C0, OUT_B), (UP_C0, UP_B), (DN_C0, DN_B * DN_C // RAW)):
                with pool.Fori(0, count) as b:
                    for c in range(RAW):
                        low(b * RAW + (first + c), c, c % SPL)

        @block.scalar
        def _(act):
            s = nc.scalar
            n = [0]

            def link(ins):
                n[0] += 1
                ins.then_inc(act_chain, 1)
                act.wait_ge(act_chain, n[0])

            def high(value, c, full):
                act.wait_ge(raw_full[c], full)
                act.wait_ge(chunk_done, value + 1)
                s.activation(hi[:, c % SPL, :, :], raw[:, c, :, :], ACT.Copy).then_inc(hi_ready, 1)

            act.wait_ge(rows_t, 1)
            s.activation(vec1[:, :], ps(0, 0, P), ACT.Copy).then_inc(vec_ready, 1)
            act.wait_ge(rows_t, 2)
            s.activation(vec2[:, :], ps(1, 0, 106), ACT.Copy).then_inc(vec_ready, 1)
            act.wait_ge(vec_ready, 2)
            s.activation(cs[:, :], vec1[:, 96:112], ACT.Silu).then_inc(cs_ready, 1)

            act.wait_ge(cols_ready, 2)
            for j in range(KD // 2):
                act.wait_ge(xt_ps, j + 1)
                s.activation(resid[:, 2 * j:2 * j + 2, :], ps(j % 4), ACT.Copy).then_inc(xt_ready, 1)
                if j >= 2:
                    act.wait_ge(sqx_used, j - 1)
                act.wait_ge(xt_ready, j + 1)
                s.activation(sqx[:, j % 2, :, :], resid[:, 2 * j:2 * j + 2, :], ACT.Square).then_inc(sqx_ready, 1)
            act.wait_ge(ssx_ready, 1)
            link(s.activation(rstd[:, :], ps(4, 0, T), ACT.Ln, bias=eps[:, 0:1]))
            s.activation(rstd[:, :], rstd[:, :], ACT.Exp, scale=-0.5).then_inc(rx_ready, 1)

            for j in range(4):
                act.wait_ge(xf_ready, j + 1)
                s.activation(xs[:, 4 * j:4 * j + 4, 0:T], x_n[:, 4 * j:4 * j + 4, :], ACT.Copy).then_inc(xhi_ready, 1)

            with act.Fori(0, IN_B) as b:
                for c in range(IN_C):
                    high(b * IN_C + c, c, b * 16 + 16)

            for c in range(SPL):
                high(GLU_C0 + c, c, 16 * (GLU_C0 // RAW + 1))

            heads = uqkv[:, :, :].rearrange("p (m f) t -> p m f t", m=4)
            act.wait_ge(acc_free, FB + IN_B * FB)
            act.wait_ge(chunk_done, SPL + GLU_C0)
            with act.Fori(0, KS // 2) as pair:
                for par in range(2):
                    ft = pair * 2 + par
                    act.wait_ge(av_ready, ft * 2 + 1)
                    act.wait_ge(cols_ready, 2)
                    s.activation(qk_a[:, :, :].unsqueeze(2), heads[:, 1:3, ds(ft, 1), :], ACT.Square).then_inc(qsq_ready, 1)
                    s.activation(u_st[:, par, :].unsqueeze(1), uqkv[:, ds(ft, 1), :], ACT.Copy).then_inc(u_ready, 1)
                    s.activation(v_st[:, :].unsqueeze(1), uqkv[:, ds(ft + 3 * KS, 1), :], ACT.Copy).then_inc(vst_ready, 1)
                    act.wait_ge(bc_ps, ft + 2)
                    s.activation(bc[:, par, :, :], ps(2), ACT.Copy).then_inc(bc_ready, 1)
                    act.wait_ge(qss_ready, ft + 1)
                    s.activation(qk_r[:, :, :], ps(3), ACT.Ln, bias=eps[:, 1:2]).then_inc(act_z, 1)
                    act.wait_ge(act_z, ft * 5 + 1)
                    s.activation(qk_r[:, :, :], qk_r[:, :, :], ACT.Exp, bias=eps[:, 3:4], scale=-0.5).then_inc(qr_ready, 1)
                    act.wait_ge(vt_ps, ft + 1)
                    s.activation(v_t[:, :, :], ps(6, 256, 256), ACT.Copy).then_inc(vt_ready, 1)
                    for h in range(2):
                        zh = ps(h, 0, 384)
                        e = ps(2, 0, 384)
                        act.wait_ge(z_ready, ft * 2 + (h + 1))
                        s.activation(e, zh, ACT.Abs).then_inc(act_z, 1)
                        act.wait_ge(act_z, ft * 5 + (2 * h + 2))
                        s.activation(e, e, ACT.Exp, scale=-1.0).then_inc(act_z, 1)
                        act.wait_ge(act_z, ft * 5 + (2 * h + 3))
                        s.activation(sp[:, :, :], e, ACT.Ln, bias=1.0).then_inc(ln_ready, 1)
                        act.wait_ge(zs_ready, ft * 2 + (h + 1))
                        s.activation(w_t[:, :, :], zh, ACT.Exp).then_inc(w_ready, 1)
                    act.wait_ge(av_ready, ft * 2 + 3)
                    s.activation(uqkv[:, ds(ft + KS, 1), :], ps(3, 0, T).unsqueeze(1), ACT.Copy).then_inc(attn_ready, 1)

            for j in range(4):
                act.wait_ge(y_ready, 2 * j + 3)
                s.activation(uqkv[:, 2 * j:2 * j + 2, :], uqkv[:, 2 * j:2 * j + 2, :], ACT.Gelu_apprx_tanh).then_inc(gelu_ready, 1)
            for j in range(4):
                act.wait_ge(gelu_ready, j + 1)
                s.activation(xs[:, 2 * j:2 * j + 2, 0:T], uqkv[:, 2 * j:2 * j + 2, :], ACT.Copy).then_inc(yhi_ready, 1)
            for c in range(SPL, GLU_B * GLU_C):
                high(GLU_C0 + c, c, 16 * (GLU_C0 // RAW + 1))
            act.wait_ge(attn_ready, KS + 1)

            def square(j, src):
                if j >= 1:
                    act.wait_ge(msq_used, j)
                s.activation(msq[:, :, :], src, ACT.Square).then_inc(msq_ready, 1)

            for j in range(4):
                square(j, uqkv[:, KS + 2 * j:KS + 2 * j + 2, :])
            act.wait_ge(msq_used, 4)
            link(s.activation(rs2[:, 1, 0, :], ps(4, 0, T), ACT.Ln, bias=eps[:, 2:3]))
            s.activation(rs2[:, 1, 0, :], rs2[:, 1, 0, :], ACT.Exp, scale=-0.5).then_inc(mr_ready, 1)
            for j in range(4):
                act.wait_ge(acc_free, FB + GLU_B0 * FB + 2 * j + 2)
                s.activation(glu_s[:, :, :], glu_z[:, :, :], ACT.Sigmoid).then_inc(sig_ready, 1)
                act.wait_ge(y2_ready, j + 1)
                square(4 + j, uqkv[:, 2 * j:2 * j + 2, :])
            act.wait_ge(msq_used, 8)
            link(s.activation(rs2[:, 0, 0, :], ps(5, 0, T), ACT.Ln, bias=eps[:, 2:3]))
            s.activation(rs2[:, 0, 0, :], rs2[:, 0, 0, :], ACT.Exp, scale=-0.5).then_inc(mr_ready, 1)
            for j in range(8):
                t0 = (2 * j + KS) % KD
                act.wait_ge(mf_ready, j + 1)
                s.activation(xs[:, t0:t0 + 2, 0:T], mix_f[:, :, :], ACT.Copy).then_inc(mhi_ready, 1)

            with act.Fori(0, OUT_B) as b:
                for c in range(OUT_C):
                    high(b * OUT_C + (OUT_C0 + c), c, b * 16 + 16 * (OUT_C0 // RAW + 1))

            for j in range(KD // 2):
                act.wait_ge(h_ready, 2 * j + 2)
                if j >= 1:
                    act.wait_ge(fsq_used, j)
                s.activation(msq[:, :, :], resid[:, 2 * j:2 * j + 2, :], ACT.Square).then_inc(fsq_ready, 1)
            act.wait_ge(fss_ready, 1)
            link(s.activation(rstd[:, :], ps(4, 0, T), ACT.Ln, bias=eps[:, 0:1]))
            s.activation(rstd[:, :], rstd[:, :], ACT.Exp, scale=-0.5).then_inc(fr_ready, 1)
            for j in range(KD // 2):
                act.wait_ge(ff_ready, j + 1)
                s.activation(xs[:, 2 * j:2 * j + 2, 0:T], ffn_f[:, :, :], ACT.Copy).then_inc(fhi_ready, 1)

            UP_FULL = 16 * (UP_C0 // RAW)

            def hidden_silu(blk):
                act.wait_ge(acc_free, blk * FB + (FB + UP_B0 * FB + 2))
                s.activation(act_tmp[:, :, :], ps(4), ACT.Silu).then_inc(g_act, 1)

            def hidden_high(blk, tile):
                act.wait_ge(h_prod, blk + 1)
                act.wait_ge(cols_ready, 2)
                s.activation(hid[:, tile, 0:T], act_tmp[:, :, :], ACT.Copy).then_inc(hid_hi, 1)

            for c in range(UP_C):
                high(UP_C0 + c, c, UP_FULL + 32)
            with act.Fori(1, UP_B) as b:
                for c in range(UP_C):
                    high(b * UP_C + (UP_C0 + c), c, b * 32 + (UP_FULL + 32))
                    if c == 3:
                        hidden_silu(b - 1)
                    if c == 5:
                        hidden_high(b - 1, ds(b * 2 - 2, 2))
            hidden_silu(UP_B - 1)
            hidden_high(UP_B - 1, slice(KF - 2, KF))

            DN_FULL = UP_FULL + 32 * UP_B
            def out_copy(b):
                for i in range(2):
                    act.wait_ge(ot_ps, 2 * b + i + 5)
                    if b >= 2:
                        act.wait_ge(out_done, 32 * (b - 1))
                    s.activation(out_s[:, b % 2, i, :], ps(6 + i), ACT.Copy).then_inc(ot_ready, 1)

            for b in range(DN_B):
                for c in range(DN_C):
                    m = b * DN_C + c
                    high(DN_C0 + m, m % RAW, DN_FULL + 16 * (m // RAW + 1))
                    if b and c == 10:
                        out_copy(b - 1)
            out_copy(DN_B - 1)

        @block.tensor
        def _(pe):
            mm = nc.tensor.matmul
            pe.sem_inc(chunk_done, SPL)
            pe.sem_inc(bc_ps, 1)
            pe.sem_inc(av_ready, 1)
            pe.sem_inc(ot_ps, 4)

            def chunk(value, c, rhs, blk=None, last=False):
                pe.wait_ge(lo_ready, value + 1)
                for f in range(FB):
                    if blk is not None:
                        pe.wait_ge(acc_free, blk * FB + f + 1)
                    for t in range(CK):
                        w_ = slice(f * P, (f + 1) * P)
                        mm(ps(f), hi[:, c % SPL, t, w_], rhs(t, 2 * T), start=blk is not None and t == 0, stop=False)
                        ins = mm(ps(f, 0, T), lo[:, c % SPL, t, w_], rhs(t, T), start=False, stop=last and t == CK - 1)
                    if last and f < FB - 1:
                        ins.then_inc(acc_ready, 1)
                ins.then_inc(chunk_done, 1)

            def of(src, kt):
                return lambda t, n: src[:, kt + t, 0:n]

            def mod_group(g, mid=0):
                pe.wait_ge(ada_mac, g * (CK * ADA_C) + CK * ADA_C)
                for j in range(FB):
                    for q in range(2):
                        ins = mm(ps(7, j, 1), ada_acc[:, q, j * P:(j + 1) * P], ones[:, 0:1], start=q == 0, stop=q == 1)
                ins.then_inc(ada_sum, 1)

            pe.wait_ge(cols_ready, 1)
            pe.wait_ge(rows_in, 16 * 12)
            nc.tensor.transpose(ps(0, 0, P), rows[:, 0, :], ident[:, :]).then_inc(rows_t, 1)
            nc.tensor.transpose(ps(1, 0, 106), rows[0:106, 1, :], ident[0:106, 0:106]).then_inc(rows_t, 1)
            pe.wait_ge(cols_ready, 2)
            pe.wait_ge(vec_ready, 2)
            pe.wait_ge(x_in, 32)
            def x_squares(j):
                pe.wait_ge(sqx_ready, j + 1)
                for q in range(2):
                    ins = mm(ps(4, 0, T), ones[:, :], sqx[:, j % 2, q, :], start=j + q == 0, stop=j == KD // 2 - 1 and q == 1)
                ins.then_inc(ssx_ready if j == KD // 2 - 1 else sqx_used, 1)

            for j in range(KD // 2):
                if j >= 4:
                    pe.wait_ge(xt_ready, j - 3)
                for q in range(2):
                    for i in range(2):
                        kt = 2 * j + q
                        ins = nc.tensor.transpose(ps(j % 4, (2 * q + i) * P, P), x_tok[:, i, kt * P:(kt + 1) * P], ident[:, :])
                ins.then_inc(xt_ps, 1)
                if j >= 2:
                    x_squares(j - 2)
            x_squares(KD // 2 - 2)
            x_squares(KD // 2 - 1)
            mod_group(0)
            with pe.Fori(1, ADA_IN0) as g:
                pe.wait_ge(mod_ready, g)
                mod_group(g)

            pe.wait_ge(xlo_ready, 4)
            with pe.Fori(0, IN_B) as b:
                for c in range(IN_C):
                    chunk(b * IN_C + c, c, of(xs, 2 * c), blk=b if c == 0 else None, last=c == IN_C - 1)
                pe.wait_ge(mod_ready, b + ADA_IN0)
                mod_group(b + ADA_IN0)

            pe.wait_ge(acc_free, FB + IN_B * FB)
            pe.wait_ge(tab_ready, 1)

            def bu(par, i, ft):
                pe.wait_ge(bu_used, ft * 4 + (i + 1))
                r = slice(32 * i, 32 * i + 32)
                for q in range(2):
                    ins = mm(ps(4 + i % 2, q * T, T), bc[r, par, q, :], u_st[r, par, :], start=q == 0, stop=True, skip_group_check=True)
                ins.then_inc(bu_ready, 1)

            def c_y(par, i, ft):
                pe.wait_ge(rem_ready, ft * 4 + (i + 1))
                for q in range(4):
                    ins = mm(acc[32 * i:32 * i + 32, 6, 0:T], bc[:, par, 2 + q // 2, 32 * i:32 * i + 32], rem[:, q, :],
                             start=q == 0, stop=q == 3)
                ins.then_inc(rem_used, 1)

            def scores(h, ft):
                hr = slice(DH * h, DH * h + DH)
                if h == 0:
                    pe.wait_ge(qkn_ready, ft + 1)
                pe.wait_ge(w_ready, ft * 2 + (h + 1))
                zz = lambda a_, n_: ps(h, a_, n_)
                mm(zz(0, 256), qk_n[hr, 1, 0:P], qk_n[hr, 0, :], start=True, stop=False, skip_group_check=True)
                mm(zz(256, P), qk_n[hr, 1, P:T], qk_n[hr, 0, P:T], start=False, stop=False, skip_group_check=True)
                mm(zz(0, P), ident_b[:, :], mask_b[:, :], start=False, stop=False, skip_group_check=True)
                mm(zz(256, P), ident_b[:, :], mask_b[:, :], start=False, stop=True, skip_group_check=True).then_inc(z_ready, 1)

            def keep(h, ft):
                pe.wait_ge(sp_ready, ft * 2 + (h + 1))
                mm(ps(h, 0, 256), neg_tri[:, :], sp[:, 0:2, :], start=False, stop=False, skip_group_check=True)
                mm(ps(h, P, P), neg_ones[:, :], sp[:, 2, :], start=False, stop=False, skip_group_check=True)
                mm(ps(h, 256, P), neg_tri[:, :], sp[:, 2, :], start=False, stop=True, skip_group_check=True).then_inc(zs_ready, 1)

            def values(h, ft):
                hr = slice(DH * h, DH * h + DH)
                pe.wait_ge(w_ready, ft * 2 + (h + 3))
                mm(acc[hr, 3, 0:T], v_t[:, 0, hr], w_t[:, 0:2, :], start=True, stop=False)
                mm(acc[hr, 3, P:T], v_t[:, 1, hr], w_t[:, 2, :], start=False, stop=True).then_inc(av_ready, 1)

            pe.sem_inc(w_ready, 2)
            with pe.Fori(0, KS // 2) as pair:
                for par in range(2):
                    ft = pair * 2 + par
                    pe.wait_ge(bcx_ready, ft * 4 + 4)
                    for q in range(2):
                        nc.tensor.transpose(ps(2, q * P, P), bx[:, q, :, :, :].rearrange("p i g h -> p (i g h)"), ident[:, :])
                    for q in range(2):
                        ins = nc.tensor.transpose(ps(2, (2 + q) * P, P), cx[:, q, :, :].rearrange("p g n -> p (g n)"), ident[:, :])
                    ins.then_inc(bc_ps, 1)
                    pe.wait_ge(qsq_ready, ft + 1)
                    pe.wait_ge(attn_ready, ft + 1)
                    mm(ps(3), head_ones[:, :], qk_a[:, :, :], start=True, stop=True).then_inc(qss_ready, 1)
                    pe.wait_ge(vst_ready, ft + 1)
                    pe.wait_ge(y_ready, ft + 1)
                    for i in range(2):
                        ins = nc.tensor.transpose(ps(6, 256 + i * P, P), v_st[:, i * P:(i + 1) * P], ident[:, :])
                    ins.then_inc(vt_ps, 1)
                    pe.wait_ge(u_ready, ft + 1)
                    pe.wait_ge(bc_ready, ft + 1)
                    bu(par, 0, ft)
                    bu(par, 1, ft)
                    pe.wait_ge(vt_ready, ft + 1)
                    c_y(par, 0, ft)
                    bu(par, 2, ft)
                    scores(0, ft)
                    c_y(par, 1, ft)
                    bu(par, 3, ft)
                    keep(0, ft)
                    c_y(par, 2, ft)
                    values(0, ft)
                    scores(1, ft)
                    c_y(par, 3, ft)
                    keep(1, ft)
                    values(1, ft)
                pe.wait_ge(mod_ready, pair + ADA_MID0)
                mod_group(pair + ADA_MID0)

            def sum_sq(bank, j, j0):
                pe.wait_ge(msq_ready, j0 + j + 1)
                for q in range(2):
                    ins = mm(ps(bank, 0, T), ones[:, :], msq[:, q, :], start=j + q == 0, stop=j == 3 and q == 1)
                ins.then_inc(msq_used, 1)

            for c in range(GLU_B * GLU_C):
                b = c // GLU_C
                if c < GLU_C:
                    pe.wait_ge(ylo_ready, c + 1)
                chunk(GLU_C0 + c, c, of(xs, 2 * (c % GLU_C)), blk=GLU_B0 + b if c % GLU_C == 0 else None,
                      last=c % GLU_C == GLU_C - 1)
                if c == GLU_C - 1:
                    for j in range(4):
                        sum_sq(4, j, 0)
            for j in range(4):
                sum_sq(5, j, 4)

            for c in range(OUT_C):
                pe.wait_ge(mlo_ready, c + 1)
                chunk(OUT_C0 + c, c, of(xs, (2 * c + KS) % KD), blk=OUT_B0 if c == 0 else None, last=c == OUT_C - 1)
            with pe.Fori(1, OUT_B) as b:
                for c in range(OUT_C):
                    chunk(b * OUT_C + (OUT_C0 + c), c, of(xs, (2 * c + KS) % KD), blk=b + OUT_B0 if c == 0 else None,
                          last=c == OUT_C - 1)
            pe.wait_ge(mr_done, 2)
            for j in range(KD // 2):
                pe.wait_ge(fsq_ready, j + 1)
                for q in range(2):
                    ins = mm(ps(4, 0, T), ones[:, :], msq[:, q, :], start=j + q == 0, stop=j == KD // 2 - 1 and q == 1)
                ins.then_inc(fss_ready if j == KD // 2 - 1 else fsq_used, 1)

            def up_block(b):
                for c in range(UP_C):
                    chunk(b * UP_C + (UP_C0 + c), c, of(xs, 2 * c), blk=b + UP_B0 if c == 0 else None, last=c == UP_C - 1)

            for c in range(UP_C):
                pe.wait_ge(flo_ready, c + 1)
                chunk(UP_C0 + c, c, of(xs, 2 * c), blk=UP_B0 if c == 0 else None, last=c == UP_C - 1)
            for c in range(UP_C):
                chunk(UP_C + UP_C0 + c, c, of(xs, 2 * c), blk=UP_B0 + 1 if c == 0 else None, last=c == UP_C - 1)
            pe.wait_ge(mod_ready, ADA_UP0)
            mod_group(ADA_UP0)
            with pe.Fori(1, 4) as g:
                up_block(g * 2)
                up_block(g * 2 + 1)
                pe.wait_ge(mod_ready, g + ADA_UP0)
                mod_group(g + ADA_UP0)
            with pe.Fori(8, UP_B) as b:
                up_block(b)

            def rows_out(b, par):
                pe.wait_ge(o_ready, b + 1)
                pe.wait_ge(ot_ready, b * 2 + 2)
                for i in range(2):
                    for f in range(FB):
                        ins = nc.tensor.transpose(ps(6 + i, f * P, P), h_out[:, par, f, i * P:(i + 1) * P], ident[:, :])
                    ins.then_inc(ot_ps, 1)

            with pe.Fori(0, DN_B // 2) as pair:
                for par in range(2):
                    b = pair * 2 + par
                    for c in range(DN_C):
                        m = par * DN_C + c
                        pe.wait_ge(hid_lo, c + 1)
                        chunk(pair * (2 * DN_C) + (DN_C0 + m), m, of(hid, 2 * c), blk=b + DN_B0 if c == 0 else None,
                              last=c == DN_C - 1)
                    rows_out(b, par)

        @block.vector
        def _(dve):
            v = nc.vector
            n = [0]

            def link(ins):
                n[0] += 1
                ins.then_inc(dve_chain, 1)
                dve.wait_ge(dve_chain, n[0])

            dve.sem_inc(acc_free, FB)
            dve.sem_inc(bu_used, 2)
            dve.sem_inc(attn_ready, 1)
            dve.sem_inc(y_ready, 1)
            dve.sem_inc(ot_ready, 2)

            def ada_kt(chunk_, c, full, t, first):
                kt = CK * c + t
                if t == 0:
                    dve.wait_ge(ada_full[c % ADA], full)
                src, col, dst = ada_raw[:, c % ADA, t, :], cs[:, kt:kt + 1], ada_acc[:, kt % 2, :]
                if first:
                    v.tensor_scalar(dst, src, col, None, ALU.mult).then_inc(ada_mac, 1)
                else:
                    dve.wait_ge(ada_mac, chunk_ * CK + (t - 1))
                    v.scalar_tensor_tensor(dst, src, col, dst, ALU.mult, ALU.add).then_inc(ada_mac, 1)

            def ada_chunks(g, c0, c1):
                if c0 == 0 and not (isinstance(g, int) and g == 0):
                    dve.wait_ge(ada_sum, g)
                for c in range(c0, c1):
                    for t in range(CK):
                        ada_kt(g * ADA_C + c, c, g * (16 * ADA_C // ADA) + 16 * (c // ADA + 1), t, c == 0)

            def ada_mods(g):
                dve.wait_ge(ada_sum, g + 1)
                dve.wait_ge(cs_ready, 1)
                v.tensor_tensor(mods[:, ds(g * FB, FB)], vec1[:, ds(g * FB, FB)], ps(7, 0, FB), ALU.add).then_inc(mod_ready, 1)

            dve.wait_ge(vec_ready, 2)
            tn = [4]

            def new():
                tn[0] += 1
                assert tn[0] <= 24
                return tiny[:, tn[0] - 1, :]

            def ts(o, i_, s1, s2, o1, o2):
                link(v.tensor_scalar(o, i_, s1, s2, o1, o2))

            def tt(o, i0, i1, op):
                link(v.tensor_tensor(o, i0, i1, op))

            def stt(o, i0, s1, i1, o1, o2):
                link(v.scalar_tensor_tensor(o, i0, s1, i1, o1, o2))

            MAGIC = 12582912.0
            LN2_HI, LN2_LO = 0.693359375, -2.12194440e-4
            kf, fr, ex, sc = new(), new(), new(), new()

            def expm1(x, em1):
                ts(kf, x, 1.4426950408889634, MAGIC, ALU.mult, ALU.add)
                ts(kf, kf, MAGIC, 126.0, ALU.subtract, ALU.min)
                ts(kf, kf, -126.0, None, ALU.max, ALU.bypass)
                stt(fr, kf, -LN2_HI, x, ALU.mult, ALU.add)
                stt(fr, kf, -LN2_LO, fr, ALU.mult, ALU.add)
                ts(ex, fr, 1 / 5040, None, ALU.mult, ALU.bypass)
                for c_ in (1 / 720, 1 / 120, 1 / 24, 1 / 6, 0.5, 1.0):
                    stt(ex, ex, c_, fr, ALU.add, ALU.mult)
                ts(tiny_i[:, :], kf, 127.0, 8388608.0, ALU.add, ALU.mult)
                link(v.tensor_copy(sc, tiny_i[:, :].bitcast(f32)))
                tt(ex, ex, sc, ALU.mult)
                stt(em1, sc, -1.0, ex, ALU.add, ALU.add)

            a_re, a_im = vec2[:, 40:72], vec2[:, 72:104]
            dt_ = new()
            for q in range(2):
                rq = slice(DH * q, DH * (q + 1))
                link(v.tensor_copy(dt_[rq, :], ldt[rq, q::2]))
            expm1(dt_, dt_)
            ts(dt_, dt_, 1.0, None, ALU.add, ALU.bypass)
            em, th, cm, sn, z2, zz = new(), new(), new(), new(), new(), new()
            tt(em, a_re, dt_, ALU.mult)
            expm1(em, em)
            tt(th, a_im, dt_, ALU.mult)
            ts(kf, th, 1 / (2 * math.pi), MAGIC, ALU.mult, ALU.add)
            ts(kf, kf, MAGIC, None, ALU.subtract, ALU.bypass)
            C1 = 6.28125
            C2 = float(np.float32(math.floor((2 * math.pi - C1) * 2 ** 21) / 2 ** 21))
            C3 = 2 * math.pi - C1 - C2
            for c_ in (C1, C2, C3):
                stt(th, kf, -c_, th, ALU.mult, ALU.add)
            ts(th, th, 0.5, None, ALU.mult, ALU.bypass)
            tt(z2, th, th, ALU.mult)
            ts(sn, z2, 1 / math.factorial(13), None, ALU.mult, ALU.bypass)
            for k_ in (11, 9, 7, 5, 3):
                stt(sn, sn, (-1.0) ** (k_ // 2) / math.factorial(k_), z2, ALU.add, ALU.mult)
            stt(sn, sn, 1.0, th, ALU.add, ALU.mult)
            ts(cm, z2, -1 / math.factorial(14), None, ALU.mult, ALU.bypass)
            for k_ in (12, 10, 8, 6, 4, 2):
                stt(cm, cm, (-1.0) ** (k_ // 2) / math.factorial(k_), z2, ALU.add, ALU.mult)
            tt(zz, sn, sn, ALU.mult)
            ts(zz, zz, -2.0, None, ALU.mult, ALU.bypass)
            stt(cm, cm, 1.0, sn, ALU.add, ALU.mult)
            ts(sn, cm, 2.0, None, ALU.mult, ALU.bypass)
            ts(tiny[:, 0, :], zz, 1.0, None, ALU.add, ALU.bypass)
            ts(tiny[:, 1, :], sn, -1.0, None, ALU.mult, ALU.bypass)
            re_, im_, den, t0 = new(), new(), new(), new()
            tt(re_, em, tiny[:, 0, :], ALU.mult)
            tt(re_, re_, zz, ALU.add)
            stt(im_, em, 1.0, sn, ALU.add, ALU.mult)
            tt(den, a_re, a_re, ALU.mult)
            tt(t0, a_im, a_im, ALU.mult)
            tt(den, den, t0, ALU.add)
            link(v.reciprocal(den, den))
            tt(tiny[:, 2, :], re_, a_re, ALU.mult)
            tt(t0, im_, a_im, ALU.mult)
            tt(tiny[:, 2, :], tiny[:, 2, :], t0, ALU.add)
            tt(tiny[:, 2, :], tiny[:, 2, :], den, ALU.mult)
            tt(tiny[:, 3, :], im_, a_re, ALU.mult)
            tt(t0, re_, a_im, ALU.mult)
            tt(tiny[:, 3, :], tiny[:, 3, :], t0, ALU.subtract)
            tt(tiny[:, 3, :], tiny[:, 3, :], den, ALU.mult)
            decay = vec2[:, 40:72]
            v.tensor_scalar(decay, em, 1.0, None, ALU.add, ALU.bypass).then_inc(lam_ready, 1)

            dve.wait_ge(cs_ready, 1)
            def newton(r, scratch, total, e):
                link(v.scalar_tensor_tensor(scratch, total, e, r, ALU.add, ALU.mult))
                link(v.tensor_tensor(scratch, scratch, r, ALU.mult))
                link(v.tensor_scalar(scratch, scratch, -0.5, 1.5, ALU.mult, ALU.add))
                return v.tensor_tensor(r, r, scratch, ALU.mult)

            ada_chunks(0, 0, ADA_C)
            ada_mods(0)
            dve.wait_ge(rx_ready, 1)
            link(newton(rstd[:, :], nrm[:, :], ps(4, 0, T), D * EPS))
            dve.wait_ge(ssx_ready, 1)
            for j in range(4):
                link(v.tensor_tensor(x_n[:, 4 * j:4 * j + 4, :], resid[:, 4 * j:4 * j + 4, :],
                                     rstd[:, :].unsqueeze(1).to_broadcast([P, 4, T]), ALU.mult))
            with dve.Fori(1, ADA_IN0) as g:
                ada_chunks(g, 0, ADA_C)
                ada_mods(g)
            dve.wait_ge(mod_ready, ADA_IN0)
            def modulate(dst, gain, scale):
                link(v.tensor_scalar(dst, gain, math.sqrt(D), None, ALU.mult, ALU.bypass))
                link(v.scalar_tensor_tensor(dst, scale, 1.0, dst, ALU.add, ALU.mult))

            modulate(a_mix[:, :], vec1[:, 112:128], mods[:, KD:2 * KD])
            dve.wait_ge(bbar_ready, 1)
            for j in range(5):
                if j < 4:
                    for kt in range(4 * j, 4 * j + 4):
                        v.tensor_scalar(x_n[:, kt, :], x_n[:, kt, :], a_mix[:, kt:kt + 1], mods[:, kt:kt + 1],
                                        ALU.mult, ALU.add).then_inc(xf_ready if kt % 4 == 3 else dve_const, 1)
                if j:
                    dve.wait_ge(xhi_ready, j)
                    sl = slice(4 * j - 4, 4 * j)
                    v.tensor_tensor(xs[:, sl, T:2 * T], x_n[:, sl, :], xs[:, sl, 0:T].bitcast(f32), ALU.subtract).then_inc(xlo_ready, 1)

            def bank_wait(f, blk, end_chunk):
                if f < FB - 1:
                    dve.wait_ge(acc_ready, blk * (FB - 1) + (f + 1))
                else:
                    dve.wait_ge(chunk_done, end_chunk + SPL)

            def halves(bank):
                return ps(bank).rearrange("p (h t) -> p t h", h=2)

            with dve.Fori(0, IN_B) as b:
                ada_chunks(b + ADA_IN0, 0, ADA_C)
                for f in range(FB):
                    bank_wait(f, b, b * IN_C + IN_C)
                    dve.wait_ge(cs_ready, 1)
                    v.tensor_reduce(uqkv[:, ds(b * FB + f, 1), :].rearrange("p o t -> p (o t)"), halves(f), AX.X, ALU.add).then_inc(acc_free, 1)
                ada_mods(b + ADA_IN0)

            dve.wait_ge(tab_ready, 1)
            gains = vec2[:, 104:106]
            link(v.tensor_scalar(gains[:, 0:1], gains[:, 0:1], math.sqrt(2), None, ALU.mult, ALU.bypass))
            link(v.tensor_scalar(gains[:, 1:2], gains[:, 1:2], math.sqrt(2 * DH), None, ALU.mult, ALU.bypass))
            NCH = 15

            def s5_tile(ft, i):
                tile = ft * 4 + i
                base = tile * NCH
                k = [0]

                def step(ins):
                    k[0] += 1
                    ins.then_inc(s5_chain, 1)

                def need(m):
                    dve.wait_ge(s5_chain, base + m)

                tb = [tabs[:, q, ds(tile, 1), :].rearrange("p o t -> p (o t)") for q in range(2)]
                cosb, nsinb = (x.unsqueeze(1).to_broadcast([P, NC, TC]) for x in tb)
                chunked = lambda ap: ap.rearrange("p (c t) -> p c t", c=NC)
                bre, bim = chunked(ps(4 + i % 2, 0, T)), chunked(ps(4 + i % 2, T, T))
                dm = [chunked(dem[:, q, :]) for q in range(4)]
                vre, vim = v_y[:, 0, :], v_y[:, 1, :]
                dve.wait_ge(bu_ready, tile + 1)
                step(v.tensor_tensor(dm[0], bre, cosb, ALU.mult))
                step(v.tensor_tensor(dm[1], bim, nsinb, ALU.mult))
                step(v.tensor_tensor(dm[2], bim, cosb, ALU.mult))
                v.tensor_tensor(dm[3], bre, nsinb, ALU.mult).then_inc(bu_used, 1)
                need(2)
                step(v.tensor_tensor(vre, dem[:, 0, :], dem[:, 1, :], ALU.subtract))
                dve.wait_ge(bu_used, tile + 3)
                step(v.tensor_tensor(vim, dem[:, 2, :], dem[:, 3, :], ALU.add))
                rr = decay[:, ds(tile, 1)].to_broadcast([P, TC])
                need(4)
                step(v.tensor_tensor_scan(vre[:, 0:TC], rr, vre[:, 0:TC], 0.0, ALU.mult, ALU.add))
                need(5)
                step(v.tensor_tensor_scan(vim[:, 0:TC], rr, vim[:, 0:TC], 0.0, ALU.mult, ALU.add))
                c128, s128 = tb[0][:, TC - 1:TC], tb[1][:, TC - 1:TC]
                lre, lim = vre[:, TC - 1:TC], vim[:, TC - 1:TC]
                need(6)
                step(v.tensor_scalar(carry[:, 1:2], lre, s128, None, ALU.mult, ALU.bypass))
                need(7)
                step(v.tensor_scalar(carry[:, 0:1], lim, s128, None, ALU.mult, ALU.bypass))
                need(8)
                step(v.scalar_tensor_tensor(carry[:, 3:4], lim, c128, carry[:, 1:2], ALU.mult, ALU.subtract))
                need(9)
                step(v.scalar_tensor_tensor(carry[:, 2:3], lre, c128, carry[:, 0:1], ALU.mult, ALU.add))
                need(10)
                step(v.tensor_tensor_scan(vim[:, TC:T], rr, vim[:, TC:T], carry[:, 3:4], ALU.mult, ALU.add))
                need(11)
                step(v.tensor_tensor_scan(vre[:, TC:T], rr, vre[:, TC:T], carry[:, 2:3], ALU.mult, ALU.add))
                dve.wait_ge(rem_used, tile + 1)
                yre, yim = chunked(vre), chunked(vim)
                rm = [chunked(rem[:, q, :]) for q in range(4)]
                need(12)
                step(v.tensor_tensor(rm[1], yim, nsinb, ALU.mult))
                step(v.tensor_tensor(rm[3], yim, cosb, ALU.mult))
                need(13)
                v.scalar_tensor_tensor(rm[2], yre, -1.0, nsinb, ALU.mult, ALU.mult)
                v.tensor_tensor(rm[0], yre, cosb, ALU.mult).then_inc(rem_ready, 1)
                assert k[0] == NCH, k

            dve.sem_inc(rem_used, 1)
            with dve.Fori(0, KS // 2) as pair:
                for par in range(2):
                    ft = pair * 2 + par
                    ada_chunks(pair + ADA_MID0, 4 * par, 4 * par + 4)
                    s5_tile(ft, 0)
                    dve.wait_ge(qr_ready, ft + 1)
                    v.scalar_tensor_tensor(qk_a[:, :, :], ps(3).rearrange("p (m t) -> p m t", m=2), DH * EPS, qk_r[:, :, :],
                                           ALU.add, ALU.mult).then_inc(qt_ready, 1)
                    s5_tile(ft, 1)
                    dve.wait_ge(qrn_ready, ft + 1)
                    for m in range(2):
                        ins = v.scalar_tensor_tensor(qk_n[:, m, :].unsqueeze(1), uqkv[:, ds(ft + KS * (m + 1), 1), :], gains[:, m:m + 1],
                                                     qk_r[:, m, :].unsqueeze(1), ALU.mult, ALU.mult)
                        ins.then_inc(qkn_ready if m else dve_const, 1)
                    s5_tile(ft, 2)
                    for h in range(2):
                        dve.wait_ge(ln_ready, ft * 2 + (h + 1))
                        v.scalar_tensor_tensor(sp[:, :, :], ps(h, 0, 384).rearrange("p (m t) -> p m t", m=3), 0.0, sp[:, :, :],
                                               ALU.max, ALU.add).then_inc(sp_ready, 1)
                        if h == 0:
                            s5_tile(ft, 3)
                    dve.wait_ge(rem_used, ft * 4 + 5)
                    ut = uqkv[:, ds(ft, 1), :].rearrange("p o t -> p (o t)")
                    v.scalar_tensor_tensor(ut, ut, vec2[:, ds(ft + 32, 1)], ps(6, 0, T), ALU.mult, ALU.add).then_inc(y_ready, 1)
                ada_mods(pair + ADA_MID0)

            for j in range(4):
                dve.wait_ge(yhi_ready, j + 1)
                sl = slice(2 * j, 2 * j + 2)
                v.tensor_tensor(xs[:, sl, T:2 * T], uqkv[:, sl, :], xs[:, sl, 0:T].bitcast(f32), ALU.subtract).then_inc(ylo_ready, 1)
            dve.wait_ge(mr_ready, 1)
            newton(rs2[:, 1, 0, :], rs2[:, 1, 1, :], ps(4, 0, T), SW * EPS).then_inc(mr_done, 1)
            for j in range(4):
                b = j // 2
                if j:
                    dve.wait_ge(sig_ready, j)
                for q in range(2):
                    f = (2 * j + q) % FB
                    bank_wait(f, GLU_B0 + b, GLU_C0 + (b + 1) * GLU_C)
                    v.tensor_reduce(glu_z[:, q, :], halves(f), AX.X, ALU.add).then_inc(acc_free, 1)
                dve.wait_ge(sig_ready, j + 1)
                sl = slice(2 * j, 2 * j + 2)
                v.tensor_tensor(uqkv[:, sl, :], uqkv[:, sl, :], glu_s[:, :, :], ALU.mult).then_inc(y2_ready, 1)
            gw = vec2[:, 16:32]
            link(v.tensor_scalar(gw, gw, math.sqrt(SW), None, ALU.mult, ALU.bypass))

            def mixed(j):
                if j < 8:
                    t0 = (2 * j + KS) % KD
                    kind = 1 if j < 4 else 0
                    if j == 0:
                        dve.wait_ge(mr_done, 1)
                    if j == 4:
                        dve.wait_ge(mr_ready, 2)
                        newton(rs2[:, 0, 0, :], rs2[:, 0, 1, :], ps(5, 0, T), SW * EPS).then_inc(mr_done, 1)
                        dve.wait_ge(mr_done, 2)
                    if j:
                        dve.wait_ge(mlo_ready, j)
                    for q in range(2):
                        v.scalar_tensor_tensor(mix_f[:, q, :], uqkv[:, t0 + q, :], gw[:, t0 + q:t0 + q + 1], rs2[:, kind, 0, :],
                                               ALU.mult, ALU.mult).then_inc(mf_ready if q else dve_const, 1)
                    dve.wait_ge(mhi_ready, j + 1)
                    v.tensor_tensor(xs[:, t0:t0 + 2, T:2 * T], mix_f[:, :, :], xs[:, t0:t0 + 2, 0:T].bitcast(f32),
                                    ALU.subtract).then_inc(mlo_ready, 1)

            for j in range(8):
                mixed(j)

            for b in range(OUT_B):
                for f in range(FB):
                    kt = b * FB + f
                    bank_wait(f, OUT_B0 + b, OUT_C0 + (b + 1) * OUT_C)
                    v.tensor_reduce(act_tmp[:, f % 2, :], halves(f), AX.X, ALU.add).then_inc(acc_free, 1)
                    dve.wait_ge(acc_free, FB + (OUT_B0 + b) * FB + f + 1)
                    v.scalar_tensor_tensor(resid[:, kt, :], act_tmp[:, f % 2, :], mods[:, 2 * KD + kt:2 * KD + kt + 1], resid[:, kt, :],
                                           ALU.mult, ALU.add).then_inc(h_ready, 1)
            modulate(a_ffn[:, :], vec2[:, 0:16], mods[:, 4 * KD:5 * KD])
            dve.wait_ge(fr_ready, 1)
            link(newton(rstd[:, :], rs2[:, 0, 1, :], ps(4, 0, T), D * EPS))
            for j in range(KD // 2):
                if j:
                    dve.wait_ge(flo_ready, j)
                for q in range(2):
                    kt = 2 * j + q
                    link(v.scalar_tensor_tensor(ffn_f[:, q, :], resid[:, kt, :], a_ffn[:, kt:kt + 1], rstd[:, :], ALU.mult, ALU.mult))
                    v.tensor_scalar(ffn_f[:, q, :], ffn_f[:, q, :], mods[:, 3 * KD + kt:3 * KD + kt + 1], None,
                                    ALU.add, ALU.bypass).then_inc(ff_ready if q else dve_const, 1)
                dve.wait_ge(fhi_ready, j + 1)
                v.tensor_tensor(xs[:, 2 * j:2 * j + 2, T:2 * T], ffn_f[:, :, :], xs[:, 2 * j:2 * j + 2, 0:T].bitcast(f32),
                                ALU.subtract).then_inc(flo_ready, 1)

            def hidden(b):
                end = b * UP_C + (UP_C0 + UP_C)
                blk = b + UP_B0
                for f in range(FB):
                    bank_wait(f, blk, end)
                    ins = v.tensor_reduce(ps(4 + f // 2, (f % 2) * T, T), halves(f), AX.X, ALU.add)
                    ins.then_inc(acc_free, 1)
                dve.wait_ge(g_act, b + 1)
                dve.wait_ge(acc_free, blk * FB + (FB + 4))
                v.tensor_tensor(act_tmp[:, :, :], ps(5).rearrange("p (m t) -> p m t", m=2), act_tmp[:, :, :], ALU.mult).then_inc(h_prod, 1)
                dve.wait_ge(hid_hi, b + 1)
                dve.wait_ge(cs_ready, 1)
                tl = ds(b * 2, 2)
                v.tensor_tensor(hid[:, tl, T:2 * T], act_tmp[:, :, :], hid[:, tl, 0:T].bitcast(f32), ALU.subtract).then_inc(hid_lo, 1)

            with dve.Fori(0, 4) as g:
                ada_chunks(g + ADA_UP0, 0, 4)
                hidden(g * 2)
                ada_chunks(g + ADA_UP0, 4, 8)
                hidden(g * 2 + 1)
                ada_mods(g + ADA_UP0)
            with dve.Fori(8, UP_B) as b:
                hidden(b)

            with dve.Fori(0, DN_B // 2) as pair:
                for par in range(2):
                    for f in range(FB):
                        blk = pair * 2 + par
                        kt = blk * FB + f
                        bank_wait(f, blk + DN_B0, blk * DN_C + (DN_C0 + DN_C))
                        v.tensor_reduce(act_tmp[:, f % 2, :], halves(f), AX.X, ALU.add).then_inc(acc_free, 1)
                        dve.wait_ge(ot_ps, blk * 2 + 2)
                        dve.wait_ge(acc_free, blk * FB + (FB + DN_B0 * FB + f + 1))
                        v.scalar_tensor_tensor(h_out[:, par, f:f + 1, :], act_tmp[:, f % 2, :].unsqueeze(1),
                                               mods[:, ds(kt + 5 * KD, 1)], resid[:, ds(kt, 1), :],
                                               ALU.mult, ALU.add).then_inc(o_ready if f == FB - 1 else dve_const, 1)


_VEC = ["c", "b_ada", "g_mix", "log_dt", "q_gain", "k_gain", "g_ssm_out", "g_attn_out", "g_ffn"]
_MAT = ["x", "w_ada", "w_in", "a_re", "a_im", "b_re", "b_im", "c_re", "c_im", "d_skip", "w_glu", "w_out",
        "w_gate", "w_up", "w_down"]


def kernel(**inputs):
    import numpy as _np
    import concourse.bacc as _bacc
    from concourse import mybir as _mybir
    from concourse.bass_utils import run_bass_kernel_spmd as _run

    nc = _bacc.Bacc("TRN2", target_bir_lowering=False, num_devices=1)
    arrays, args = {}, {}
    for name in _VEC + _MAT:
        v = _np.ascontiguousarray(inputs[name])
        v = v.reshape(v.shape[1:])
        arrays[f"in_{name}"] = v
        args[name] = nc.dram_tensor(f"in_{name}", v.shape, _mybir.dt.from_np(v.dtype), kind="ExternalInput").ap()
    args["out"] = nc.dram_tensor("out_h", (T, D), _mybir.dt.float32, kind="ExternalOutput").ap()
    build(nc, args)
    r = _run(nc, [arrays], core_ids=[0])
    return r.results[0]["out_h"].reshape(1, T, D)
```

```python
import math
from contextlib import ExitStack

import numpy as np
import concourse.bass as bass
from concourse import mybir

P = 128
D = 2048
T = 256
KD = D // P
SW = 1024
KS = SW // P
GROUPS, GH, NS = 64, 16, 64
ST = GROUPS * NS // P
DH = 64
FF = 5632
KF = FF // P
NMOD = 6 * D
EPS = 1e-6
TC = 128
NC = T // TC
CK, CW = 2, 512
RAW, SPL, ADA = 8, 4, 4
FB = CW // P

IN_B, IN_C = 4 * SW // CW, KD // CK
GLU_B, GLU_C = SW // CW, KS // CK
OUT_B, OUT_C = D // CW, KD // CK
UP_B, UP_C = 2 * FF // CW, KD // CK
DN_B, DN_C = D // CW, KF // CK
GLU_C0 = IN_B * IN_C
OUT_C0 = GLU_C0 + GLU_B * GLU_C
UP_C0 = OUT_C0 + OUT_B * OUT_C
DN_C0 = UP_C0 + UP_B * UP_C
ALL_C = DN_C0 + DN_B * DN_C
GLU_B0 = IN_B
OUT_B0 = GLU_B0 + GLU_B
UP_B0 = OUT_B0 + OUT_B
DN_B0 = UP_B0 + UP_B
ADA_G = NMOD // CW
ADA_C = KD // CK
ADA_T = (3, 6)


class Ada:

    def __init__(self, g0, count, shared, before=None):
        self.g0, self.count = g0, count
        self.tensor = ADA_T if shared else ()
        self.vper, self.tper = CK * (ADA_C - len(self.tensor)), len(self.tensor)
        self.v0 = before.v0 + before.count * before.vper if before else 0
        self.t0 = before.t0 + before.count * before.tper if before else 0

    def used(self, i, c):
        if c in self.tensor:
            return True, i * self.tper + (self.t0 + sum(x <= c for x in self.tensor))
        return False, i * self.vper + (self.v0 + CK * sum(x not in self.tensor for x in range(c + 1)))


PRE = Ada(0, 2 * D // CW, True)
INP = Ada(PRE.count, IN_B, False, PRE)
MID = Ada(INP.g0 + INP.count, OUT_B, False, INP)
UPG = Ada(MID.g0 + MID.count, 4, False, MID)


def build(nc, a):
    f32, f32r, bf16, i32 = mybir.dt.float32, mybir.dt.float32r, mybir.dt.bfloat16, mybir.dt.int32
    ALU, ACT, AX = mybir.AluOpType, mybir.ActivationFunctionType, mybir.AxisListType
    ds = bass.ds

    def chunks(w):
        return w.rearrange("(c t p) n -> c p t n", t=CK, p=P)

    w_in, w_glu, w_out = chunks(a["w_in"]), chunks(a["w_glu"]), chunks(a["w_out"])
    w_gate, w_up, w_down = chunks(a["w_gate"]), chunks(a["w_up"]), chunks(a["w_down"])
    w_ada = chunks(a["w_ada"])

    ctx = ExitStack()
    with ctx:
        def sb(name, shape, dt=f32):
            return ctx.enter_context(nc.sbuf_tensor(name, shape, dt))

        def sem(name):
            return ctx.enter_context(nc.semaphore(name))

        raw = sb("raw", [P, RAW, CK, CW])
        hi = sb("hi", [P, SPL, CK, CW], f32r)
        lo_at = (nc.sbuf_base + 31) // 32 * 32
        lo = sb("lo", [P, SPL, CK, CW], f32r)
        resid = sb("resid", [P, KD, T])
        xs_at = (nc.sbuf_base + 31) // 32 * 32
        xs = sb("xs", [P, KD, 2 * T], f32r)
        ar_at = (nc.sbuf_base + 31) // 32 * 32
        hid = sb("hid", [P, KF, 2 * T], f32r)
        ident = sb("ident", [P, P])
        ones = sb("ones", [P, P])
        head_ones = sb("head_ones", [P, P])
        neg_tri = sb("neg_tri", [P, P])
        neg_ones = sb("neg_ones", [P, P])
        ident_b = sb("ident_b", [P, P], bf16)
        mask_b = sb("mask_b", [P, P], bf16)
        vec1 = sb("vec1", [P, P])
        vec2 = sb("vec2", [P, 106])
        mods = sb("mods", [P, NMOD // P])
        a_mix = sb("a_mix", [P, KD])
        a_ffn = sb("a_ffn", [P, KD])
        cs = sb("cs", [P, KD])
        eps = sb("eps", [P, 5])
        grp = sb("grp", [P, 2])
        rstd = sb("rstd", [P, T])
        act_tmp = sb("act_tmp", [P, 2, T])

        def over(name, base, at, shape, dt=f32):
            return nc.alloc_sbuf_tensor_at(name, shape, dt, offset=base + 4 * at)

        tabs = over("tabs", ar_at, 0, [P, 2, ST, TC])
        uqkv = over("uqkv", ar_at, 8192, [P, 32, T])
        b_bar = over("b_bar", ar_at, 16384, [P, 2, ST, GH])
        ada_acc = over("ada_acc", ar_at, 17408, [P, 2, CW])
        ada_raw = over("ada_raw", ar_at, 18432, [P, ADA, CK, CW])
        x_tok = over("x_tok", ar_at, 8192, [P, 2, D])
        x_n = over("x_n", ar_at, 8192, [P, KD, T])
        b_raw = over("b_raw", ar_at, 12288, [P, 2, ST, GH])
        rows = over("rows", ar_at, 13312, [P, 2, P])
        ldt = over("ldt", ar_at, 13568, [P, GROUPS])
        tiny = over("tiny", ar_at, 13632, [P, 24, ST])
        tiny_i = over("tiny_i", ar_at, 14400, [P, ST], i32)
        nrm = over("nrm", ar_at, 14432, [P, T])
        sqx = over("sqx", ar_at, 14720, [P, 2, 2, T])
        ptiny = over("ptiny", ar_at, 15744, [P, 2, ST])
        btmp = over("btmp", ar_at, 10240, [P, 2, ST, GH])
        ptmp = over("ptmp", lo_at, 0, [P, 2, ST, TC // 2])
        pre_raw = over("pre_raw", xs_at, 0, [P, ADA_C, CK, CW])
        c_raw = over("c_raw", xs_at, 0, [P, KS, 2, NS])
        bx = over("bx", xs_at, 1024, [P, 2, 4, 2, GH])
        cx = over("cx", xs_at, 1280, [P, 2, 2, NS])
        bc = over("bc", xs_at, 1536, [P, 2, 4, P])
        dem = over("dem", xs_at, 2560, [P, 4, T])
        v_y = over("v_y", xs_at, 3584, [P, 2, T])
        carry = over("carry", xs_at, 4096, [P, 4])
        rem = over("rem", xs_at, 4128, [P, 4, T])
        u_st = over("u_st", xs_at, 5152, [P, 2, T])
        qk_n = over("qk_n", xs_at, 5664, [P, 2, T])
        v_st = over("v_st", xs_at, 6176, [P, T])
        qk_a = over("qk_a", xs_at, 6688, [P, 2, T])
        qk_r = over("qk_r", xs_at, 7200, [P, 2, T])
        sp = over("sp", ar_at, 18432, [P, 2, 3, P])
        w_t = over("w_t", ar_at, 19200, [P, 2, 3, P])
        v_t = over("v_t", ar_at, 19968, [P, 2, 2, P])
        glu_z = over("glu_z", ar_at, 12288, [P, 2, T])
        glu_s = over("glu_s", ar_at, 12800, [P, 2, T])
        mix_f = over("mix_f", ar_at, 13312, [P, 2, T])
        msq = over("msq", ar_at, 13824, [P, 2, T])
        rs2 = over("rs2", ar_at, 14336, [P, 2, 2, T])
        ffn_f = over("ffn_f", ar_at, 15360, [P, 2, T])
        out_s = over("out_s", xs_at, 0, [P, 2, 2, CW])
        h_out = over("h_out", xs_at, 2048, [P, 2, FB, T])

        acc = ctx.enter_context(nc.psum_tensor("acc", [P, 8, 512], f32))

        def ps(bank, lo_=0, n=512):
            return acc[:, bank, lo_:lo_ + n]

        rows_in, x_in, b_in, c_in, out_done = sem("rows_in"), sem("x_in"), sem("b_in"), sem("c_in"), sem("out_done")
        raw_full = [sem(f"raw_full{s}") for s in range(RAW)]
        pre_full = [sem(f"pre_full{c}") for c in range(ADA_C)]
        ada_full = [sem(f"ada_full{s}") for s in range(ADA)]
        hi_ready, lo_ready = sem("hi_ready"), sem("lo_ready")
        chunk_done = sem("chunk_done")
        acc_ready = sem("acc_ready")
        acc_free = sem("acc_free")
        ada_mac, ada_pe = sem("ada_mac"), sem("ada_pe")
        ada_sum, mod_ready = sem("ada_sum"), sem("mod_ready")
        cols_ready = sem("cols_ready")
        dve_const = sem("dve_const")
        rows_t, vec_ready, cs_ready, lam_ready = sem("rows_t"), sem("vec_ready"), sem("cs_ready"), sem("lam_ready")
        dve_chain, pool_chain, act_chain = sem("dve_chain"), sem("pool_chain"), sem("act_chain")
        tab_ready, bbar_ready, den_ready = sem("tab_ready"), sem("bbar_ready"), sem("den_ready")
        xt_ps, xt_ready, sqx_ready, ssx_ready = sem("xt_ps"), sem("xt_ready"), sem("sqx_ready"), sem("ssx_ready")
        sqx_used, rx_ready = sem("sqx_used"), sem("rx_ready")
        xf_ready, xhi_ready, xlo_ready = sem("xf_ready"), sem("xhi_ready"), sem("xlo_ready")
        cneg = sem("cneg")
        bcx_ready, bc_ps, bc_ready, u_ready = sem("bcx_ready"), sem("bc_ps"), sem("bc_ready"), sem("u_ready")
        bu_ready, bu_used, s5_chain = sem("bu_ready"), sem("bu_used"), sem("s5_chain")
        rem_ready, rem_used, y_ready = sem("rem_ready"), sem("rem_used"), sem("y_ready")
        qsq_ready, qss_ready, qr_ready, qn_chain = sem("qsq_ready"), sem("qss_ready"), sem("qr_ready"), sem("qn_chain")
        qt_ready, qrn_ready, qkn_ready = sem("qt_ready"), sem("qrn_ready"), sem("qkn_ready")
        vst_ready, vt_ps, vt_ready = sem("vst_ready"), sem("vt_ps"), sem("vt_ready")
        z_ready, ln_ready, sp_ready, zs_ready, w_ready = sem("z_ready"), sem("ln_ready"), sem("sp_ready"), sem("zs_ready"), sem("w_ready")
        act_z = sem("act_z")
        av_ready, attn_ready = sem("av_ready"), sem("attn_ready")
        gelu_ready, yhi_ready, ylo_ready = sem("gelu_ready"), sem("yhi_ready"), sem("ylo_ready")
        sig_ready, y2_ready = sem("sig_ready"), sem("y2_ready")
        msq_ready, msq_used, mr_ready = sem("msq_ready"), sem("msq_used"), sem("mr_ready")
        mr_done = sem("mr_done")
        mf_ready, mhi_ready, mlo_ready = sem("mf_ready"), sem("mhi_ready"), sem("mlo_ready")
        h_ready, fsq_ready, fsq_used, fss_ready, fr_ready = sem("h_ready"), sem("fsq_ready"), sem("fsq_used"), sem("fss_ready"), sem("fr_ready")
        ff_ready, fhi_ready, flo_ready = sem("ff_ready"), sem("fhi_ready"), sem("flo_ready")
        g_act, h_prod, hid_hi, hid_lo = sem("g_act"), sem("h_prod"), sem("hid_hi"), sem("hid_lo")
        d_red, o_ready, ot_ps, ot_ready = sem("d_red"), sem("o_ready"), sem("ot_ps"), sem("ot_ready")

        block = ctx.enter_context(nc.Block())

        def store(eng, b):
            for i in range(2):
                eng.wait_ge(ot_ready, 2 * b + i + 3)
                eng.dma_start(a["out"][i * P:(i + 1) * P, b * CW:(b + 1) * CW], out_s[:, b % 2, i, :]).then_inc(out_done, 16)

        def ada_slot(ph, i, c):
            if ph is PRE:
                return pre_raw[:, c, :, :], pre_full[c], i * 16 + 16
            return ada_raw[:, c % ADA, :, :], ada_full[c % ADA], \
                (i + (ph.g0 - PRE.count)) * (16 * ADA_C // ADA) + 16 * (c // ADA + 1)

        @block.sync
        def _(sp_):
            def weights(first_chunk, k, slot, src, cols):
                sp_.dma_start(raw[:, slot, :, cols[0]:cols[1]], src).then_inc(raw_full[slot], 16)

            def ada_chunk(ph, i, c):
                ring = ADA_C if ph is PRE else ADA
                first = isinstance(i, int) and i == 0
                if c < ring and ph in (MID, UPG):
                    sp_.wait_ge(ada_mac, ph.v0)
                    sp_.wait_ge(ada_pe, ph.t0)
                if c >= ring or not first:
                    tensor, value = ph.used(i, c - ring) if c >= ring else ph.used(i - 1, c - ring + ADA_C)
                    sp_.wait_ge(ada_pe if tensor else ada_mac, value)
                dst, full = (pre_raw[:, c, :, :], pre_full[c]) if ph is PRE else (ada_raw[:, c % ADA, :, :], ada_full[c % ADA])
                sp_.dma_start(dst, w_ada[c, :, :, ds((i + ph.g0) * CW, CW)]).then_inc(full, 16)

            def row(i, at, n, src):
                sp_.dma_start(rows[at:at + n, i, :], src).then_inc(rows_in, 16)

            row(0, 0, 96, a["b_ada"].rearrange("(r c) -> r c", c=P))
            row(0, 96, 16, a["c"].rearrange("(r c) -> r c", c=P))
            row(0, 112, 16, a["g_mix"].rearrange("(r c) -> r c", c=P))
            row(1, 0, 16, a["g_ffn"].rearrange("(r c) -> r c", c=P))
            row(1, 16, 8, a["g_ssm_out"].rearrange("(r c) -> r c", c=P))
            row(1, 24, 8, a["g_attn_out"].rearrange("(r c) -> r c", c=P))
            row(1, 32, 8, a["d_skip"].rearrange("(r g) h -> r (g h)", g=8))
            row(1, 40, 32, a["a_re"].rearrange("(r g) n -> r (g n)", g=2))
            row(1, 72, 32, a["a_im"].rearrange("(r g) n -> r (g n)", g=2))
            for i, name in enumerate(("q_gain", "k_gain")):
                sp_.dma_start(rows[104 + i:105 + i, 1, :].rearrange("o (g n) -> o g n", g=2),
                              a[name].rearrange("(o g n) -> o g n", o=1, g=1).to_broadcast([1, 2, DH])
                              ).then_inc(rows_in, 16)
            sp_.dma_start(ldt[:, :], a["log_dt"].rearrange("(o n) -> o n", o=1).to_broadcast([P, GROUPS])
                          ).then_inc(rows_in, 16)
            for i in range(2):
                sp_.dma_start(x_tok[:, i, :], a["x"][i * P:(i + 1) * P, :]).then_inc(x_in, 16)
            for c in range(ADA_C):
                ada_chunk(PRE, 0, c)
            for i, name in enumerate(("b_re", "b_im")):
                sp_.dma_start(b_raw[:, i, :, :], a[name].rearrange("(t g) n h -> (g n) t h", g=2)).then_inc(b_in, 16)
            with sp_.Fori(1, PRE.count) as g:
                for c in range(ADA_C):
                    ada_chunk(PRE, g, c)
            for c in range(IN_C):
                sp_.dma_start(raw[:, c, :, :], w_in[c, :, :, 0:CW]).then_inc(raw_full[c], 16)
            for c in range(ADA_C):
                ada_chunk(INP, 0, c)
            with sp_.Fori(1, IN_B) as b:
                for c in range(IN_C):
                    sp_.wait_ge(lo_ready, b * IN_C + c - RAW + 1)
                    sp_.dma_start(raw[:, c, :, :], w_in[c, :, :, ds(b * CW, CW)]).then_inc(raw_full[c], 16)
                    ada_chunk(INP, b, c)
            for c in range(GLU_B * GLU_C):
                sp_.wait_ge(lo_ready, GLU_C0 + c - RAW + 1)
                sp_.dma_start(raw[:, c % RAW, :, :],
                              w_glu[c % GLU_C, :, :, (c // GLU_C) * CW:(c // GLU_C + 1) * CW]).then_inc(raw_full[c % RAW], 16)
            sp_.wait_ge(chunk_done, SPL + GLU_C0)
            for i, name in enumerate(("c_re", "c_im")):
                sp_.dma_start(c_raw[:, :, i, :], a[name].rearrange("(f g) h n -> (g h) f n", f=KS)).then_inc(c_in, 16)
            for n in range(OUT_B * OUT_C):
                b, c = divmod(n, OUT_C)
                sp_.wait_ge(lo_ready, OUT_C0 + n - RAW + 1)
                sp_.dma_start(raw[:, c, :, :], w_out[(c + KS // CK) % OUT_C, :, :, b * CW:(b + 1) * CW]).then_inc(raw_full[c], 16)
                if n == 0:
                    sp_.wait_ge(attn_ready, KS + 1)
                ada_chunk(MID, b, c)

            def up_block(b):
                for c in range(UP_C):
                    sp_.wait_ge(lo_ready, b * UP_C + (UP_C0 + c - RAW + 1))
                    for w, cols in ((w_gate, (0, 256)), (w_up, (256, 512))):
                        sp_.dma_start(raw[:, c, :, cols[0]:cols[1]], w[c, :, :, ds(b * 256, 256)]).then_inc(raw_full[c], 16)

            with sp_.Fori(0, 4) as g:
                for half in range(2):
                    up_block(g * 2 + half)
                    for c in range(ADA_C // 2 * half, ADA_C // 2 * (half + 1)):
                        ada_chunk(UPG, g, c)
            with sp_.Fori(8, UP_B) as b:
                up_block(b)
            for b in range(DN_B):
                for c in range(DN_C):
                    n = b * DN_C + c
                    sp_.wait_ge(lo_ready, DN_C0 + n - RAW + 1)
                    sp_.dma_start(raw[:, n % RAW, :, :], w_down[c, :, :, b * CW:(b + 1) * CW]).then_inc(raw_full[n % RAW], 16)
                if b >= 1:
                    store(sp_, b - 1)
            store(sp_, DN_B - 1)
            sp_.wait_ge(out_done, 16 * 2 * DN_B)

        @block.gpsimd
        def _(pool):
            n = [0]

            def link(ins):
                n[0] += 1
                ins.then_inc(pool_chain, 1)
                pool.wait_ge(pool_chain, n[0])

            g = nc.gpsimd
            link(g.memset(ident[:, :], 0.0))
            link(g.affine_select(out=ident[:, :], in_=ident[:, :], compare_op=ALU.not_equal, fill=1.0, base=0,
                                 pattern=[[-1, P]], channel_multiplier=1))
            g.memset(ones[:, :], 1.0).then_inc(cols_ready, 1)
            link(g.memset(neg_ones[:, :], -1.0))
            link(g.affine_select(out=neg_tri[:, :], in_=neg_ones[:, :], compare_op=ALU.is_ge, fill=0.0, base=0,
                                 pattern=[[-1, P]], channel_multiplier=1))
            link(g.affine_select(out=head_ones[:, 0:DH], in_=ones[:, 0:DH], compare_op=ALU.is_ge, fill=0.0, base=DH - 1,
                                 pattern=[[0, DH]], channel_multiplier=-1))
            link(g.affine_select(out=head_ones[:, DH:P], in_=ones[:, DH:P], compare_op=ALU.is_ge, fill=0.0, base=-DH,
                                 pattern=[[0, DH]], channel_multiplier=1))
            link(g.tensor_copy(ident_b[:, :], ident[:, :]))
            link(g.memset(mask_b[:, :], -1e30))
            link(g.affine_select(out=mask_b[:, :], in_=mask_b[:, :], compare_op=ALU.is_ge, fill=0.0, base=0,
                                 pattern=[[-1, P]], channel_multiplier=1))
            link(g.memset(grp[:, :], 1.0))
            for q in range(6, -1, -1):
                link(g.affine_select(out=grp[:, 1:2], in_=grp[:, 1:2], compare_op=ALU.is_ge, fill=float(q % 2),
                                     base=-16 * (q + 1), pattern=[[0, 1]], channel_multiplier=1))
            link(g.tensor_tensor(grp[:, 0:1], ones[:, 0:1], grp[:, 1:2], ALU.subtract))
            for i, v in enumerate((D * EPS, DH * EPS, SW * EPS, -0.5 * math.log(2))):
                link(g.memset(eps[:, i:i + 1], v))
            g.memset(eps[:, 4:5], 1.5).then_inc(cols_ready, 1)

            pool.wait_ge(vec_ready, 2)
            tn = [4]

            def new():
                tn[0] += 1
                assert tn[0] <= 21
                return tiny[:, tn[0] - 1, :]

            def ts(o, i_, s1, s2, o1, o2):
                link(g.tensor_scalar(o, i_, s1, s2, o1, o2))

            def tt(o, i0, i1, op):
                link(g.tensor_tensor(o, i0, i1, op))

            def stt(o, i0, s1, i1, o1, o2):
                link(g.tensor_scalar(tiny[:, 21, :], i0, s1, None, o1, ALU.bypass))
                link(g.tensor_tensor(o, tiny[:, 21, :], i1, o2))

            MAGIC = 12582912.0
            LN2_HI, LN2_LO = 0.693359375, -2.12194440e-4
            kf, fr, ex, sc = new(), new(), new(), new()

            def expm1(x, em1):
                ts(kf, x, 1.4426950408889634, MAGIC, ALU.mult, ALU.add)
                ts(kf, kf, MAGIC, 126.0, ALU.subtract, ALU.min)
                ts(kf, kf, -126.0, None, ALU.max, ALU.bypass)
                stt(fr, kf, -LN2_HI, x, ALU.mult, ALU.add)
                stt(fr, kf, -LN2_LO, fr, ALU.mult, ALU.add)
                ts(ex, fr, 1 / 5040, None, ALU.mult, ALU.bypass)
                for c_ in (1 / 720, 1 / 120, 1 / 24, 1 / 6, 0.5, 1.0):
                    stt(ex, ex, c_, fr, ALU.add, ALU.mult)
                ts(tiny_i[:, :], kf, 127.0, 8388608.0, ALU.add, ALU.mult)
                link(g.tensor_copy(sc, tiny_i[:, :].bitcast(f32)))
                tt(ex, ex, sc, ALU.mult)
                stt(em1, sc, -1.0, ex, ALU.add, ALU.add)

            a_re, a_im = vec2[:, 40:72], vec2[:, 72:104]
            dt_ = new()
            for q in range(2):
                rq = slice(DH * q, DH * (q + 1))
                link(g.tensor_copy(dt_[rq, :], ldt[rq, q::2]))
            expm1(dt_, dt_)
            ts(dt_, dt_, 1.0, None, ALU.add, ALU.bypass)
            em, th, cm, sn, z2, zz = new(), new(), new(), new(), new(), new()
            tt(em, a_re, dt_, ALU.mult)
            expm1(em, em)
            tt(th, a_im, dt_, ALU.mult)
            ts(kf, th, 1 / (2 * math.pi), MAGIC, ALU.mult, ALU.add)
            ts(kf, kf, MAGIC, None, ALU.subtract, ALU.bypass)
            C1 = 6.28125
            C2 = float(np.float32(math.floor((2 * math.pi - C1) * 2 ** 21) / 2 ** 21))
            C3 = 2 * math.pi - C1 - C2
            for c_ in (C1, C2, C3):
                stt(th, kf, -c_, th, ALU.mult, ALU.add)
            ts(th, th, 0.5, None, ALU.mult, ALU.bypass)
            tt(z2, th, th, ALU.mult)
            ts(sn, z2, 1 / math.factorial(13), None, ALU.mult, ALU.bypass)
            for k_ in (11, 9, 7, 5, 3):
                stt(sn, sn, (-1.0) ** (k_ // 2) / math.factorial(k_), z2, ALU.add, ALU.mult)
            stt(sn, sn, 1.0, th, ALU.add, ALU.mult)
            ts(cm, z2, -1 / math.factorial(14), None, ALU.mult, ALU.bypass)
            for k_ in (12, 10, 8, 6, 4, 2):
                stt(cm, cm, (-1.0) ** (k_ // 2) / math.factorial(k_), z2, ALU.add, ALU.mult)
            tt(zz, sn, sn, ALU.mult)
            ts(zz, zz, -2.0, None, ALU.mult, ALU.bypass)
            stt(cm, cm, 1.0, sn, ALU.add, ALU.mult)
            ts(sn, cm, 2.0, None, ALU.mult, ALU.bypass)
            ts(tiny[:, 0, :], zz, 1.0, None, ALU.add, ALU.bypass)
            ts(tiny[:, 1, :], sn, -1.0, None, ALU.mult, ALU.bypass)
            re_, im_, t0, den = new(), new(), new(), tiny[:, 23, :]
            tt(re_, em, tiny[:, 0, :], ALU.mult)
            tt(re_, re_, zz, ALU.add)
            stt(im_, em, 1.0, sn, ALU.add, ALU.mult)
            pool.wait_ge(den_ready, 1)
            tt(tiny[:, 2, :], re_, a_re, ALU.mult)
            tt(t0, im_, a_im, ALU.mult)
            tt(tiny[:, 2, :], tiny[:, 2, :], t0, ALU.add)
            tt(tiny[:, 2, :], tiny[:, 2, :], den, ALU.mult)
            tt(tiny[:, 3, :], im_, a_re, ALU.mult)
            tt(t0, re_, a_im, ALU.mult)
            tt(tiny[:, 3, :], tiny[:, 3, :], t0, ALU.subtract)
            tt(tiny[:, 3, :], tiny[:, 3, :], den, ALU.mult)
            decay = vec2[:, 40:72]
            g.tensor_scalar(decay, em, 1.0, None, ALU.add, ALU.bypass).then_inc(lam_ready, 1)


            cosp, sinp = tabs[:, 0, :, :], tabs[:, 1, :, :]

            def unit(j):
                c_, s_ = cosp[:, :, j], sinp[:, :, j]
                t0, t1 = ptiny[:, 0, :], ptiny[:, 1, :]
                link(g.tensor_tensor(t0, c_, c_, ALU.mult))
                link(g.tensor_tensor(t1, s_, s_, ALU.mult))
                link(g.tensor_tensor(t0, t0, t1, ALU.add))
                link(g.tensor_scalar(t0, t0, -0.5, 1.5, ALU.mult, ALU.add))
                link(g.tensor_tensor(c_, c_, t0, ALU.mult))
                link(g.tensor_tensor(s_, s_, t0, ALU.mult))

            link(g.tensor_copy(cosp[:, :, 0], tiny[:, 0, :]))
            link(g.tensor_copy(sinp[:, :, 0], tiny[:, 1, :]))
            unit(0)
            w = 1
            while w < TC:
                p0, p1 = ptmp[:, 0, :, 0:w], ptmp[:, 1, :, 0:w]
                c0, s0, c1, s1 = cosp[:, :, 0:w], sinp[:, :, 0:w], cosp[:, :, w:2 * w], sinp[:, :, w:2 * w]
                cn, sn = (x[:, :, w - 1:w].to_broadcast([P, ST, w]) for x in (cosp, sinp))
                link(g.tensor_tensor(p0, c0, cn, ALU.mult))
                link(g.tensor_tensor(p1, s0, sn, ALU.mult))
                link(g.tensor_tensor(c1, p0, p1, ALU.subtract))
                link(g.tensor_tensor(p0, c0, sn, ALU.mult))
                link(g.tensor_tensor(p1, s0, cn, ALU.mult))
                link(g.tensor_tensor(s1, p0, p1, ALU.add))
                w *= 2
                unit(w - 1)
            pool.sem_inc(tab_ready, 1)

            def low(value, slot, s):
                pool.wait_ge(hi_ready, value + 1)
                g.tensor_tensor(lo[:, s, :, :], raw[:, slot, :, :], hi[:, s, :, :].bitcast(f32), ALU.subtract).then_inc(lo_ready, 1)

            with pool.Fori(0, IN_B) as b:
                for c in range(IN_C):
                    low(b * IN_C + c, c % RAW, c % SPL)

            for c in range(SPL):
                low(GLU_C0 + c, c, c)
            pool.wait_ge(chunk_done, SPL + GLU_C0)
            pool.wait_ge(c_in, 32)
            link(g.tensor_scalar(c_raw[:, :, 1, :], c_raw[:, :, 1, :], -1.0, None, ALU.mult))
            pool.wait_ge(bbar_ready, 1)
            with pool.Fori(0, KS) as ft:
                pool.wait_ge(bc_ps, ft + 1)
                pool.wait_ge(cols_ready, 2)
                for q in range(2):
                    g.tensor_tensor(bx[:, :, :, q, :], b_bar[:, :, ds(ft * 4, 4), :],
                                    head_ones[:, 127 * q:127 * q + 1].unsqueeze(2).unsqueeze(3).to_broadcast([P, 2, 4, GH]),
                                    ALU.mult).then_inc(bcx_ready, 1)
                for q in range(2):
                    g.tensor_tensor(cx[:, :, q, :], c_raw[:, ds(ft, 1), :, :].rearrange("p o r n -> p (o r) n"),
                                          grp[:, q:q + 1].unsqueeze(2).to_broadcast([P, 2, NS]), ALU.mult).then_inc(bcx_ready, 1)
                pool.wait_ge(qt_ready, ft + 1)
                g.tensor_tensor(qk_a[:, :, :], qk_a[:, :, :], qk_r[:, :, :], ALU.mult).then_inc(qn_chain, 1)
                pool.wait_ge(qn_chain, ft * 2 + 1)
                g.tensor_tensor(qk_a[:, :, :], eps[:, 4:5].unsqueeze(2).to_broadcast([P, 2, T]), qk_a[:, :, :],
                                ALU.subtract).then_inc(qn_chain, 1)
                pool.wait_ge(qn_chain, ft * 2 + 2)
                g.tensor_tensor(qk_r[:, :, :], qk_r[:, :, :], qk_a[:, :, :], ALU.mult).then_inc(qrn_ready, 1)

            for c in range(SPL, RAW):
                low(GLU_C0 + c, c, c % SPL)
            for first, count in ((OUT_C0, OUT_B), (UP_C0, UP_B), (DN_C0, DN_B * DN_C // RAW)):
                with pool.Fori(0, count) as b:
                    for c in range(RAW):
                        low(b * RAW + (first + c), c, c % SPL)

        @block.scalar
        def _(act):
            s = nc.scalar
            n = [0]

            def link(ins):
                n[0] += 1
                ins.then_inc(act_chain, 1)
                act.wait_ge(act_chain, n[0])

            def high(value, c, full):
                act.wait_ge(raw_full[c], full)
                act.wait_ge(chunk_done, value + 1)
                s.activation(hi[:, c % SPL, :, :], raw[:, c, :, :], ACT.Copy).then_inc(hi_ready, 1)

            act.wait_ge(rows_t, 1)
            s.activation(vec1[:, :], ps(0, 0, P), ACT.Copy).then_inc(vec_ready, 1)
            act.wait_ge(rows_t, 2)
            s.activation(vec2[:, :], ps(1, 0, 106), ACT.Copy).then_inc(vec_ready, 1)
            act.wait_ge(vec_ready, 2)
            s.activation(cs[:, :], vec1[:, 96:112], ACT.Silu).then_inc(cs_ready, 1)

            act.wait_ge(cols_ready, 2)
            for j in range(KD // 2):
                act.wait_ge(xt_ps, j + 1)
                s.activation(resid[:, 2 * j:2 * j + 2, :], ps(j % 4), ACT.Copy).then_inc(xt_ready, 1)
                if j >= 2:
                    act.wait_ge(sqx_used, j - 1)
                act.wait_ge(xt_ready, j + 1)
                s.activation(sqx[:, j % 2, :, :], resid[:, 2 * j:2 * j + 2, :], ACT.Square).then_inc(sqx_ready, 1)
            act.wait_ge(ssx_ready, 1)
            link(s.activation(rstd[:, :], ps(4, 0, T), ACT.Ln, bias=eps[:, 0:1]))
            s.activation(rstd[:, :], rstd[:, :], ACT.Exp, scale=-0.5).then_inc(rx_ready, 1)

            for j in range(4):
                act.wait_ge(xf_ready, j + 1)
                s.activation(xs[:, 4 * j:4 * j + 4, 0:T], x_n[:, 4 * j:4 * j + 4, :], ACT.Copy).then_inc(xhi_ready, 1)

            with act.Fori(0, IN_B) as b:
                for c in range(IN_C):
                    high(b * IN_C + c, c, b * 16 + 16)

            for c in range(SPL):
                high(GLU_C0 + c, c, 16 * (GLU_C0 // RAW + 1))

            heads = uqkv[:, :, :].rearrange("p (m f) t -> p m f t", m=4)
            act.wait_ge(acc_free, FB + IN_B * FB)
            act.wait_ge(chunk_done, SPL + GLU_C0)

            def copies(ft, par):
                s.activation(u_st[:, par, :].unsqueeze(1), uqkv[:, ds(ft, 1), :], ACT.Copy).then_inc(u_ready, 1)
                s.activation(v_st[:, :].unsqueeze(1), uqkv[:, ds(ft + 3 * KS, 1), :], ACT.Copy).then_inc(vst_ready, 1)
                if not (isinstance(ft, int) and ft == 0):
                    act.wait_ge(qrn_ready, ft)
                s.activation(qk_a[:, :, :].unsqueeze(2), heads[:, 1:3, ds(ft, 1), :], ACT.Square).then_inc(qsq_ready, 1)

            def bc_copy(ft, par):
                act.wait_ge(bc_ps, ft + 2)
                s.activation(bc[:, par, :, :], ps(2), ACT.Copy).then_inc(bc_ready, 1)

            def norm_ln(ft, links):
                act.wait_ge(qss_ready, ft + 1)
                if not (isinstance(ft, int) and ft == 0):
                    act.wait_ge(qkn_ready, ft)
                s.activation(qk_r[:, :, :], ps(7), ACT.Ln, bias=eps[:, 1:2]).then_inc(act_z, 1)

            def norm_exp(ft, par, links):
                act.wait_ge(act_z, links)
                s.activation(qk_r[:, :, :], qk_r[:, :, :], ACT.Exp, bias=eps[:, 3:4], scale=-0.5).then_inc(qr_ready, 1)
                act.wait_ge(vt_ps, ft + 1)
                s.activation(v_t[:, par, :, :], ps(2, 0, T), ACT.Copy).then_inc(vt_ready, 1)

            def mixer(ft, par, last=False):
                z = acc[:, 0:2, 0:384]
                spv = sp[:, :, :, :].rearrange("p h m t -> p h (m t)")
                if not last:
                    copies(ft + 1, 1 - par)
                act.wait_ge(z_ready, ft + 1)
                s.activation(spv, z, ACT.Abs).then_inc(act_z, 1)
                act.wait_ge(act_z, ft * 3 + 2)
                s.activation(spv, spv, ACT.Exp, scale=-1.0).then_inc(act_z, 1)
                act.wait_ge(act_z, ft * 3 + 3)
                s.activation(spv, spv, ACT.Ln, bias=1.0).then_inc(ln_ready, 1)
                if not last:
                    bc_copy(ft + 1, 1 - par)
                    norm_ln(ft + 1, None)
                    norm_exp(ft + 1, 1 - par, ft * 3 + 4)
                act.wait_ge(zs_ready, ft + 1)
                s.activation(w_t[:, :, :, :].rearrange("p h m t -> p h (m t)"), z, ACT.Exp).then_inc(w_ready, 1)
                act.wait_ge(av_ready, ft * 2 + 3)
                s.activation(uqkv[:, ds(ft + KS, 1), :], ps(3, 0, T).unsqueeze(1), ACT.Copy).then_inc(attn_ready, 1)

            act.wait_ge(cols_ready, 2)
            copies(0, 0)
            bc_copy(0, 0)
            norm_ln(0, None)
            norm_exp(0, 0, 1)
            mixer(0, 0)
            mixer(1, 1)
            with act.Fori(1, KS // 2 - 1) as pair:
                for par in range(2):
                    mixer(pair * 2 + par, par)
            mixer(KS - 2, 0)
            mixer(KS - 1, 1, last=True)

            for j in range(4):
                act.wait_ge(y_ready, 2 * j + 3)
                s.activation(uqkv[:, 2 * j:2 * j + 2, :], uqkv[:, 2 * j:2 * j + 2, :], ACT.Gelu_apprx_tanh).then_inc(gelu_ready, 1)
            for j in range(4):
                act.wait_ge(gelu_ready, j + 1)
                s.activation(xs[:, 2 * j:2 * j + 2, 0:T], uqkv[:, 2 * j:2 * j + 2, :], ACT.Copy).then_inc(yhi_ready, 1)
            for c in range(SPL, GLU_B * GLU_C):
                high(GLU_C0 + c, c, 16 * (GLU_C0 // RAW + 1))
            act.wait_ge(attn_ready, KS + 1)

            def square(j, src):
                if j >= 1:
                    act.wait_ge(msq_used, j)
                s.activation(msq[:, :, :], src, ACT.Square).then_inc(msq_ready, 1)

            for j in range(4):
                square(j, uqkv[:, KS + 2 * j:KS + 2 * j + 2, :])
            act.wait_ge(msq_used, 4)
            link(s.activation(rs2[:, 1, 0, :], ps(4, 0, T), ACT.Ln, bias=eps[:, 2:3]))
            s.activation(rs2[:, 1, 0, :], rs2[:, 1, 0, :], ACT.Exp, scale=-0.5).then_inc(mr_ready, 1)
            for j in range(4):
                act.wait_ge(acc_free, FB + GLU_B0 * FB + 2 * j + 2)
                s.activation(glu_s[:, :, :], glu_z[:, :, :], ACT.Sigmoid).then_inc(sig_ready, 1)
                act.wait_ge(y2_ready, j + 1)
                square(4 + j, uqkv[:, 2 * j:2 * j + 2, :])
            act.wait_ge(msq_used, 8)
            link(s.activation(rs2[:, 0, 0, :], ps(5, 0, T), ACT.Ln, bias=eps[:, 2:3]))
            s.activation(rs2[:, 0, 0, :], rs2[:, 0, 0, :], ACT.Exp, scale=-0.5).then_inc(mr_ready, 1)
            for j in range(8):
                t0 = (2 * j + KS) % KD
                act.wait_ge(mf_ready, j + 1)
                s.activation(xs[:, t0:t0 + 2, 0:T], mix_f[:, :, :], ACT.Copy).then_inc(mhi_ready, 1)

            with act.Fori(0, OUT_B) as b:
                for c in range(OUT_C):
                    high(b * OUT_C + (OUT_C0 + c), c, b * 16 + 16 * (OUT_C0 // RAW + 1))

            for j in range(KD // 2):
                act.wait_ge(h_ready, 2 * j + 2)
                if j >= 1:
                    act.wait_ge(fsq_used, j)
                s.activation(msq[:, :, :], resid[:, 2 * j:2 * j + 2, :], ACT.Square).then_inc(fsq_ready, 1)
            act.wait_ge(fss_ready, 1)
            link(s.activation(rstd[:, :], ps(4, 0, T), ACT.Ln, bias=eps[:, 0:1]))
            s.activation(rstd[:, :], rstd[:, :], ACT.Exp, scale=-0.5).then_inc(fr_ready, 1)
            for j in range(KD // 2):
                act.wait_ge(ff_ready, j + 1)
                s.activation(xs[:, 2 * j:2 * j + 2, 0:T], ffn_f[:, :, :], ACT.Copy).then_inc(fhi_ready, 1)

            UP_FULL = 16 * (UP_C0 // RAW)

            def hidden_silu(blk):
                act.wait_ge(acc_free, blk * FB + (FB + UP_B0 * FB + 2))
                s.activation(act_tmp[:, :, :], ps(4), ACT.Silu).then_inc(g_act, 1)

            def hidden_high(blk, tile):
                act.wait_ge(h_prod, blk + 1)
                act.wait_ge(cols_ready, 2)
                s.activation(hid[:, tile, 0:T], act_tmp[:, :, :], ACT.Copy).then_inc(hid_hi, 1)

            for c in range(UP_C):
                high(UP_C0 + c, c, UP_FULL + 32)
            with act.Fori(1, UP_B) as b:
                for c in range(UP_C):
                    high(b * UP_C + (UP_C0 + c), c, b * 32 + (UP_FULL + 32))
                    if c == 3:
                        hidden_silu(b - 1)
                    if c == 5:
                        hidden_high(b - 1, ds(b * 2 - 2, 2))
            hidden_silu(UP_B - 1)
            hidden_high(UP_B - 1, slice(KF - 2, KF))

            DN_FULL = UP_FULL + 32 * UP_B
            def out_copy(b):
                for i in range(2):
                    act.wait_ge(ot_ps, 2 * b + i + 5)
                    if b >= 2:
                        act.wait_ge(out_done, 32 * (b - 1))
                    s.activation(out_s[:, b % 2, i, :], ps(6 + i), ACT.Copy).then_inc(ot_ready, 1)

            for b in range(DN_B):
                for c in range(DN_C):
                    m = b * DN_C + c
                    high(DN_C0 + m, m % RAW, DN_FULL + 16 * (m // RAW + 1))
                    if b and c == 10:
                        out_copy(b - 1)
            out_copy(DN_B - 1)

        @block.tensor
        def _(pe):
            mm = nc.tensor.matmul
            pe.sem_inc(chunk_done, SPL)
            pe.sem_inc(bc_ps, 1)
            pe.sem_inc(av_ready, 1)
            pe.sem_inc(ot_ps, 4)

            def chunk(value, c, rhs, blk=None, last=False):
                pe.wait_ge(lo_ready, value + 1)
                for f in range(FB):
                    if blk is not None:
                        pe.wait_ge(acc_free, blk * FB + f + 1)
                    for t in range(CK):
                        w_ = slice(f * P, (f + 1) * P)
                        mm(ps(f), hi[:, c % SPL, t, w_], rhs(t, 2 * T), start=blk is not None and t == 0, stop=False)
                        ins = mm(ps(f, 0, T), lo[:, c % SPL, t, w_], rhs(t, T), start=False, stop=last and t == CK - 1)
                    if last and f < FB - 1:
                        ins.then_inc(acc_ready, 1)
                ins.then_inc(chunk_done, 1)

            def of(src, kt):
                return lambda t, n: src[:, kt + t, 0:n]

            def ada_direct(ph, i, c, col=0, start=False):
                src, full, value = ada_slot(ph, i, c)
                pe.wait_ge(full, value)
                for t in range(CK):
                    for j in range(FB):
                        ins = mm(acc[:, 7, ds(col + j, 1)], src[:, t, j * P:(j + 1) * P], cs[:, CK * c + t:CK * c + t + 1],
                                 start=start and t + j == 0, stop=False, skip_group_check=True)
                ins.then_inc(ada_pe, 1)

            def mod_group(ph, i, buf=0, col=0, start=False):
                pe.wait_ge(ada_mac, i * ph.vper + (ph.v0 + ph.vper))
                for j in range(FB):
                    ins = mm(acc[:, 7, ds(col + j, 1)], ada_acc[:, buf, j * P:(j + 1) * P], ones[:, 0:1],
                             start=start and j == 0, stop=True, skip_group_check=True)
                ins.then_inc(ada_sum, 1)

            pe.wait_ge(cols_ready, 1)
            pe.wait_ge(rows_in, 16 * 12)
            nc.tensor.transpose(ps(0, 0, P), rows[:, 0, :], ident[:, :]).then_inc(rows_t, 1)
            nc.tensor.transpose(ps(1, 0, 106), rows[0:106, 1, :], ident[0:106, 0:106]).then_inc(rows_t, 1)
            pe.wait_ge(cols_ready, 2)
            pe.wait_ge(vec_ready, 2)
            pe.wait_ge(x_in, 32)
            def x_squares(j):
                pe.wait_ge(sqx_ready, j + 1)
                for q in range(2):
                    ins = mm(ps(4, 0, T), ones[:, :], sqx[:, j % 2, q, :], start=j + q == 0, stop=j == KD // 2 - 1 and q == 1)
                ins.then_inc(ssx_ready if j == KD // 2 - 1 else sqx_used, 1)

            for j in range(KD // 2):
                if j >= 4:
                    pe.wait_ge(xt_ready, j - 3)
                for q in range(2):
                    for i in range(2):
                        kt = 2 * j + q
                        ins = nc.tensor.transpose(ps(j % 4, (2 * q + i) * P, P), x_tok[:, i, kt * P:(kt + 1) * P], ident[:, :])
                ins.then_inc(xt_ps, 1)
                if j >= 2:
                    x_squares(j - 2)
                if j == 0:
                    pe.wait_ge(cs_ready, 1)
                if j in PRE.tensor:
                    ada_direct(PRE, 0, j, start=j == PRE.tensor[0])
            x_squares(KD // 2 - 2)
            x_squares(KD // 2 - 1)
            mod_group(PRE, 0)

            def pre_group(g, buf):
                for c in PRE.tensor:
                    ada_direct(PRE, g, c, g * FB)
                mod_group(PRE, g, buf, g * FB)

            pre_group(1, 1)
            with pe.Fori(1, PRE.count // 2) as pair:
                for q in range(2):
                    pre_group(pair * 2 + q, q)

            pe.wait_ge(xlo_ready, 4)
            with pe.Fori(0, IN_B) as b:
                for c in range(IN_C):
                    chunk(b * IN_C + c, c, of(xs, 2 * c), blk=b if c == 0 else None, last=c == IN_C - 1)
                pe.wait_ge(mod_ready, b + INP.g0)
                mod_group(INP, b, start=True)

            pe.wait_ge(acc_free, FB + IN_B * FB)
            pe.wait_ge(tab_ready, 1)

            def bu(par, i, ft):
                pe.wait_ge(bu_used, ft * 4 + (i + 1))
                r = slice(32 * i, 32 * i + 32)
                for q in range(2):
                    ins = mm(ps(4 + i % 2, q * T, T), bc[r, par, q, :], u_st[r, par, :], start=q == 0, stop=True, skip_group_check=True)
                ins.then_inc(bu_ready, 1)

            def c_y(par, i, ft):
                pe.wait_ge(rem_ready, ft * 4 + (i + 1))
                for q in range(4):
                    ins = mm(acc[32 * i:32 * i + 32, 6, 0:T], bc[:, par, 2 + q // 2, 32 * i:32 * i + 32], rem[:, q, :],
                             start=q == 0, stop=q == 3)
                ins.then_inc(rem_used, 1)

            def scores(h, ft):
                hr = slice(DH * h, DH * h + DH)
                zz = lambda a_, n_: ps(h, a_, n_)
                mm(zz(0, 256), qk_n[hr, 1, 0:P], qk_n[hr, 0, :], start=True, stop=False, skip_group_check=True)
                mm(zz(256, P), qk_n[hr, 1, P:T], qk_n[hr, 0, P:T], start=False, stop=False, skip_group_check=True)
                mm(zz(0, P), ident_b[:, :], mask_b[:, :], start=False, stop=False, skip_group_check=True)
                return mm(zz(256, P), ident_b[:, :], mask_b[:, :], start=False, stop=True, skip_group_check=True)

            def keep(h):
                mm(ps(h, 0, 256), neg_tri[:, :], sp[:, h, 0:2, :], start=False, stop=False, skip_group_check=True)
                mm(ps(h, P, P), neg_ones[:, :], sp[:, h, 2, :], start=False, stop=False, skip_group_check=True)
                return mm(ps(h, 256, P), neg_tri[:, :], sp[:, h, 2, :], start=False, stop=True, skip_group_check=True)

            def values(h, par):
                hr = slice(DH * h, DH * h + DH)
                mm(acc[hr, 3, 0:T], v_t[:, par, 0, hr], w_t[:, h, 0:2, :], start=True, stop=False)
                mm(acc[hr, 3, P:T], v_t[:, par, 1, hr], w_t[:, h, 2, :], start=False, stop=True).then_inc(av_ready, 1)

            def prepare(ft):
                pe.wait_ge(bcx_ready, ft * 4 + 4)
                if not (isinstance(ft, int) and ft == 0):
                    pe.wait_ge(vt_ready, ft)
                    pe.wait_ge(qt_ready, ft)
                for q in range(2):
                    nc.tensor.transpose(ps(2, q * P, P), bx[:, q, :, :, :].rearrange("p i g h -> p (i g h)"), ident[:, :])
                for q in range(2):
                    ins = nc.tensor.transpose(ps(2, (2 + q) * P, P), cx[:, q, :, :].rearrange("p g n -> p (g n)"), ident[:, :])
                ins.then_inc(bc_ps, 1)
                pe.wait_ge(qsq_ready, ft + 1)
                mm(ps(7), head_ones[:, :], qk_a[:, :, :], start=True, stop=True).then_inc(qss_ready, 1)

            def value_rows(ft):
                pe.wait_ge(vst_ready, ft + 1)
                pe.wait_ge(bc_ready, ft + 1)
                for i in range(2):
                    ins = nc.tensor.transpose(ps(2, i * P, P), v_st[:, i * P:(i + 1) * P], ident[:, :])
                ins.then_inc(vt_ps, 1)

            def mixer(ft, par, last=False):
                pe.wait_ge(qkn_ready, ft + 1)
                pe.wait_ge(w_ready, ft + 1)
                scores(0, ft)
                scores(1, ft).then_inc(z_ready, 1)
                if not last:
                    prepare(ft + 1)
                pe.wait_ge(y_ready, ft + 1)
                c_y(par, 0, ft)
                bu(par, 2, ft)
                if not last:
                    value_rows(ft + 1)
                c_y(par, 1, ft)
                bu(par, 3, ft)
                pe.wait_ge(sp_ready, ft + 1)
                keep(0)
                keep(1).then_inc(zs_ready, 1)
                pe.wait_ge(w_ready, ft + 2)
                pe.wait_ge(vt_ready, ft + 1)
                pe.wait_ge(attn_ready, ft + 1)
                for h in range(2):
                    values(h, par)
                c_y(par, 2, ft)
                if not last:
                    pe.wait_ge(u_ready, ft + 2)
                    bu(1 - par, 0, ft + 1)
                    bu(1 - par, 1, ft + 1)
                c_y(par, 3, ft)

            pe.sem_inc(w_ready, 1)
            pe.wait_ge(mod_ready, MID.g0)
            prepare(0)
            value_rows(0)
            pe.wait_ge(u_ready, 1)
            bu(0, 0, 0)
            bu(0, 1, 0)
            mixer(0, 0)
            mixer(1, 1)
            with pe.Fori(1, KS // 2 - 1) as pair:
                for par in range(2):
                    mixer(pair * 2 + par, par)
            mixer(KS - 2, 0)
            mixer(KS - 1, 1, last=True)

            def sum_sq(bank, j, j0):
                pe.wait_ge(msq_ready, j0 + j + 1)
                for q in range(2):
                    ins = mm(ps(bank, 0, T), ones[:, :], msq[:, q, :], start=j + q == 0, stop=j == 3 and q == 1)
                ins.then_inc(msq_used, 1)

            for c in range(GLU_B * GLU_C):
                b = c // GLU_C
                if c < GLU_C:
                    pe.wait_ge(ylo_ready, c + 1)
                chunk(GLU_C0 + c, c, of(xs, 2 * (c % GLU_C)), blk=GLU_B0 + b if c % GLU_C == 0 else None,
                      last=c % GLU_C == GLU_C - 1)
                if c == GLU_C - 1:
                    for j in range(4):
                        sum_sq(4, j, 0)
            for j in range(4):
                sum_sq(5, j, 4)

            for c in range(OUT_C):
                pe.wait_ge(mlo_ready, c + 1)
                chunk(OUT_C0 + c, c, of(xs, (2 * c + KS) % KD), blk=OUT_B0 if c == 0 else None, last=c == OUT_C - 1)
            mod_group(MID, 0, start=True)
            with pe.Fori(1, OUT_B) as b:
                for c in range(OUT_C):
                    chunk(b * OUT_C + (OUT_C0 + c), c, of(xs, (2 * c + KS) % KD), blk=b + OUT_B0 if c == 0 else None,
                          last=c == OUT_C - 1)
                pe.wait_ge(mod_ready, b + MID.g0)
                mod_group(MID, b, start=True)
            pe.wait_ge(mr_done, 2)
            for j in range(KD // 2):
                pe.wait_ge(fsq_ready, j + 1)
                for q in range(2):
                    ins = mm(ps(4, 0, T), ones[:, :], msq[:, q, :], start=j + q == 0, stop=j == KD // 2 - 1 and q == 1)
                ins.then_inc(fss_ready if j == KD // 2 - 1 else fsq_used, 1)

            def up_block(b):
                for c in range(UP_C):
                    chunk(b * UP_C + (UP_C0 + c), c, of(xs, 2 * c), blk=b + UP_B0 if c == 0 else None, last=c == UP_C - 1)

            for c in range(UP_C):
                pe.wait_ge(flo_ready, c + 1)
                chunk(UP_C0 + c, c, of(xs, 2 * c), blk=UP_B0 if c == 0 else None, last=c == UP_C - 1)
            for c in range(UP_C):
                chunk(UP_C + UP_C0 + c, c, of(xs, 2 * c), blk=UP_B0 + 1 if c == 0 else None, last=c == UP_C - 1)
            pe.wait_ge(mod_ready, UPG.g0)
            mod_group(UPG, 0, start=True)
            with pe.Fori(1, 4) as g:
                up_block(g * 2)
                up_block(g * 2 + 1)
                pe.wait_ge(mod_ready, g + UPG.g0)
                mod_group(UPG, g, start=True)
            with pe.Fori(8, UP_B) as b:
                up_block(b)

            def rows_out(b, par):
                pe.wait_ge(o_ready, b + 1)
                pe.wait_ge(ot_ready, b * 2 + 2)
                for i in range(2):
                    for f in range(FB):
                        ins = nc.tensor.transpose(ps(6 + i, f * P, P), h_out[:, par, f, i * P:(i + 1) * P], ident[:, :])
                    ins.then_inc(ot_ps, 1)

            with pe.Fori(0, DN_B // 2) as pair:
                for par in range(2):
                    b = pair * 2 + par
                    for c in range(DN_C):
                        m = par * DN_C + c
                        pe.wait_ge(hid_lo, c + 1)
                        chunk(pair * (2 * DN_C) + (DN_C0 + m), m, of(hid, 2 * c), blk=b + DN_B0 if c == 0 else None,
                              last=c == DN_C - 1)
                    rows_out(b, par)

        @block.vector
        def _(dve):
            v = nc.vector
            n = [0]

            def link(ins):
                n[0] += 1
                ins.then_inc(dve_chain, 1)
                dve.wait_ge(dve_chain, n[0])

            dve.sem_inc(acc_free, FB)
            dve.sem_inc(bu_used, 2)
            dve.sem_inc(attn_ready, 1)
            dve.sem_inc(y_ready, 1)
            dve.sem_inc(ot_ready, 2)

            def ada_chunks(ph, i, c0=0, c1=ADA_C, buf=0):
                first = isinstance(i, int) and i == 0
                if c0 == 0:
                    if ph is not PRE:
                        dve.wait_ge(ada_sum, i + ph.g0)
                    elif not isinstance(i, int) or i >= 2:
                        dve.wait_ge(ada_sum, i - 1)
                for c in range(c0, c1):
                    if c in ph.tensor:
                        continue
                    slot, full, value = ada_slot(ph, i, c)
                    dve.wait_ge(full, value)
                    for t in range(CK):
                        kt = CK * c + t
                        src, col, dst = slot[:, t, :], cs[:, kt:kt + 1], ada_acc[:, buf, :]
                        if kt == 0:
                            v.tensor_scalar(dst, src, col, None, ALU.mult).then_inc(ada_mac, 1)
                        else:
                            dve.wait_ge(ada_mac, ph.used(i, c)[1] - CK + t)
                            v.scalar_tensor_tensor(dst, src, col, dst, ALU.mult, ALU.add).then_inc(ada_mac, 1)

            def ada_mods(ph, i):
                dve.wait_ge(ada_sum, i + (ph.g0 + 1))
                dve.wait_ge(cs_ready, 1)
                cols = ds((i + ph.g0) * FB, FB)
                v.tensor_tensor(mods[:, cols], vec1[:, cols], ps(7, 0, FB), ALU.add).then_inc(mod_ready, 1)

            dve.wait_ge(cs_ready, 1)
            def newton(r, scratch, total, e):
                link(v.scalar_tensor_tensor(scratch, total, e, r, ALU.add, ALU.mult))
                link(v.tensor_tensor(scratch, scratch, r, ALU.mult))
                link(v.tensor_scalar(scratch, scratch, -0.5, 1.5, ALU.mult, ALU.add))
                return v.tensor_tensor(r, r, scratch, ALU.mult)

            dve.wait_ge(vec_ready, 2)
            den, den_im = tiny[:, 23, :], tiny[:, 22, :]
            link(v.tensor_tensor(den, vec2[:, 40:72], vec2[:, 40:72], ALU.mult))
            link(v.tensor_tensor(den_im, vec2[:, 72:104], vec2[:, 72:104], ALU.mult))
            link(v.tensor_tensor(den, den, den_im, ALU.add))
            v.reciprocal(den, den).then_inc(den_ready, 1)
            ada_chunks(PRE, 0)
            ada_chunks(PRE, 1, buf=1)
            dve.wait_ge(rx_ready, 1)
            link(newton(rstd[:, :], nrm[:, :], ps(4, 0, T), D * EPS))
            dve.wait_ge(ssx_ready, 1)
            for j in range(4):
                link(v.tensor_tensor(x_n[:, 4 * j:4 * j + 4, :], resid[:, 4 * j:4 * j + 4, :],
                                     rstd[:, :].unsqueeze(1).to_broadcast([P, 4, T]), ALU.mult))
            with dve.Fori(1, PRE.count // 2) as pair:
                for q in range(2):
                    ada_chunks(PRE, pair * 2 + q, buf=q)
            dve.wait_ge(ada_sum, PRE.count)
            link(v.tensor_tensor(mods[:, 0:PRE.count * FB], vec1[:, 0:PRE.count * FB], ps(7, 0, PRE.count * FB), ALU.add))
            dve.sem_inc(mod_ready, PRE.count)
            def modulate(dst, gain, scale):
                link(v.tensor_scalar(dst, gain, math.sqrt(D), None, ALU.mult, ALU.bypass))
                link(v.scalar_tensor_tensor(dst, scale, 1.0, dst, ALU.add, ALU.mult))

            modulate(a_mix[:, :], vec1[:, 112:128], mods[:, KD:2 * KD])
            for j in range(5):
                if j < 4:
                    for kt in range(4 * j, 4 * j + 4):
                        v.tensor_scalar(x_n[:, kt, :], x_n[:, kt, :], a_mix[:, kt:kt + 1], mods[:, kt:kt + 1],
                                        ALU.mult, ALU.add).then_inc(xf_ready if kt % 4 == 3 else dve_const, 1)
                if j:
                    dve.wait_ge(xhi_ready, j)
                    sl = slice(4 * j - 4, 4 * j)
                    v.tensor_tensor(xs[:, sl, T:2 * T], x_n[:, sl, :], xs[:, sl, 0:T].bitcast(f32), ALU.subtract).then_inc(xlo_ready, 1)

            def bank_wait(f, blk, end_chunk):
                if f < FB - 1:
                    dve.wait_ge(acc_ready, blk * (FB - 1) + (f + 1))
                else:
                    dve.wait_ge(chunk_done, end_chunk + SPL)

            def halves(bank):
                return ps(bank).rearrange("p (h t) -> p t h", h=2)

            def projected(b):
                for f in range(FB):
                    bank_wait(f, b, b * IN_C + IN_C)
                    v.tensor_reduce(uqkv[:, ds(b * FB + f, 1), :].rearrange("p o t -> p (o t)"), halves(f), AX.X, ALU.add).then_inc(acc_free, 1)

            ada_chunks(INP, 0)
            projected(0)
            dve.wait_ge(lam_ready, 1)
            dve.wait_ge(b_in, 32)
            f_re = tiny[:, 2, :].unsqueeze(2).to_broadcast([P, ST, GH])
            f_im = tiny[:, 3, :].unsqueeze(2).to_broadcast([P, ST, GH])
            b0, b1 = btmp[:, 0, :, :], btmp[:, 1, :, :]
            link(v.tensor_tensor(b0, b_raw[:, 0, :, :], f_re, ALU.mult))
            link(v.tensor_tensor(b1, b_raw[:, 1, :, :], f_im, ALU.mult))
            link(v.tensor_tensor(b_bar[:, 0, :, :], b0, b1, ALU.subtract))
            link(v.tensor_tensor(b0, b_raw[:, 1, :, :], f_re, ALU.mult))
            link(v.tensor_tensor(b1, b_raw[:, 0, :, :], f_im, ALU.mult))
            v.tensor_tensor(b_bar[:, 1, :, :], b0, b1, ALU.add).then_inc(bbar_ready, 1)
            dve.wait_ge(bbar_ready, 1)

            ada_mods(INP, 0)
            with dve.Fori(1, IN_B) as b:
                ada_chunks(INP, b)
                projected(b)
                ada_mods(INP, b)

            dve.wait_ge(tab_ready, 1)
            gains = vec2[:, 104:106]
            link(v.tensor_scalar(gains[:, 0:1], gains[:, 0:1], math.sqrt(2), None, ALU.mult, ALU.bypass))
            link(v.tensor_scalar(gains[:, 1:2], gains[:, 1:2], math.sqrt(2 * DH), None, ALU.mult, ALU.bypass))
            NCH = 15

            def s5_tile(ft, i):
                tile = ft * 4 + i
                base = tile * NCH
                k = [0]

                def step(ins):
                    k[0] += 1
                    ins.then_inc(s5_chain, 1)

                def need(m):
                    dve.wait_ge(s5_chain, base + m)

                tb = [tabs[:, q, ds(tile, 1), :].rearrange("p o t -> p (o t)") for q in range(2)]
                cosb, nsinb = (x.unsqueeze(1).to_broadcast([P, NC, TC]) for x in tb)
                chunked = lambda ap: ap.rearrange("p (c t) -> p c t", c=NC)
                bre, bim = chunked(ps(4 + i % 2, 0, T)), chunked(ps(4 + i % 2, T, T))
                dm = [chunked(dem[:, q, :]) for q in range(4)]
                vre, vim = v_y[:, 0, :], v_y[:, 1, :]
                dve.wait_ge(bu_ready, tile + 1)
                step(v.tensor_tensor(dm[0], bre, cosb, ALU.mult))
                step(v.tensor_tensor(dm[1], bim, nsinb, ALU.mult))
                step(v.tensor_tensor(dm[2], bim, cosb, ALU.mult))
                v.tensor_tensor(dm[3], bre, nsinb, ALU.mult).then_inc(bu_used, 1)
                need(2)
                step(v.tensor_tensor(vre, dem[:, 0, :], dem[:, 1, :], ALU.subtract))
                dve.wait_ge(bu_used, tile + 3)
                step(v.tensor_tensor(vim, dem[:, 2, :], dem[:, 3, :], ALU.add))
                rr = vec2[:, ds(tile + 40, 1)].to_broadcast([P, TC])
                need(4)
                step(v.tensor_tensor_scan(vre[:, 0:TC], rr, vre[:, 0:TC], 0.0, ALU.mult, ALU.add))
                need(5)
                step(v.tensor_tensor_scan(vim[:, 0:TC], rr, vim[:, 0:TC], 0.0, ALU.mult, ALU.add))
                c128, s128 = tb[0][:, TC - 1:TC], tb[1][:, TC - 1:TC]
                lre, lim = vre[:, TC - 1:TC], vim[:, TC - 1:TC]
                need(6)
                step(v.tensor_scalar(carry[:, 1:2], lre, s128, None, ALU.mult, ALU.bypass))
                need(7)
                step(v.tensor_scalar(carry[:, 0:1], lim, s128, None, ALU.mult, ALU.bypass))
                need(8)
                step(v.scalar_tensor_tensor(carry[:, 3:4], lim, c128, carry[:, 1:2], ALU.mult, ALU.subtract))
                need(9)
                step(v.scalar_tensor_tensor(carry[:, 2:3], lre, c128, carry[:, 0:1], ALU.mult, ALU.add))
                need(10)
                step(v.tensor_tensor_scan(vim[:, TC:T], rr, vim[:, TC:T], carry[:, 3:4], ALU.mult, ALU.add))
                need(11)
                step(v.tensor_tensor_scan(vre[:, TC:T], rr, vre[:, TC:T], carry[:, 2:3], ALU.mult, ALU.add))
                dve.wait_ge(rem_used, tile + 1)
                yre, yim = chunked(vre), chunked(vim)
                rm = [chunked(rem[:, q, :]) for q in range(4)]
                need(12)
                step(v.tensor_tensor(rm[1], yim, nsinb, ALU.mult))
                step(v.tensor_tensor(rm[3], yim, cosb, ALU.mult))
                need(13)
                v.scalar_tensor_tensor(rm[2], yre, -1.0, nsinb, ALU.mult, ALU.mult)
                v.tensor_tensor(rm[0], yre, cosb, ALU.mult).then_inc(rem_ready, 1)
                assert k[0] == NCH, k

            def qk_vr(ft):
                dve.wait_ge(qr_ready, ft + 1)
                v.scalar_tensor_tensor(qk_a[:, :, :], ps(7).rearrange("p (m t) -> p m t", m=2), DH * EPS, qk_r[:, :, :],
                                       ALU.add, ALU.mult).then_inc(qt_ready, 1)

            def qk_norm(ft):
                dve.wait_ge(qrn_ready, ft + 1)
                for m in range(2):
                    ins = v.scalar_tensor_tensor(qk_n[:, m, :].unsqueeze(1), uqkv[:, ds(ft + KS * (m + 1), 1), :], gains[:, m:m + 1],
                                                 qk_r[:, m, :].unsqueeze(1), ALU.mult, ALU.mult)
                    ins.then_inc(qkn_ready if m else dve_const, 1)

            def s5_out(ft):
                dve.wait_ge(rem_used, ft * 4 + 5)
                ut = uqkv[:, ds(ft, 1), :].rearrange("p o t -> p (o t)")
                v.scalar_tensor_tensor(ut, ut, vec2[:, ds(ft + 32, 1)], ps(6, 0, T), ALU.mult, ALU.add).then_inc(y_ready, 1)

            def mixer(ft, first=False, last=False):
                s5_tile(ft, 0)
                if not first:
                    s5_out(ft - 1)
                s5_tile(ft, 1)
                if not last:
                    qk_vr(ft + 1)
                dve.wait_ge(ln_ready, ft + 1)
                v.scalar_tensor_tensor(sp[:, :, :, :].rearrange("p h m t -> p h (m t)"), acc[:, 0:2, 0:384], 0.0,
                                       sp[:, :, :, :].rearrange("p h m t -> p h (m t)"), ALU.max, ALU.add).then_inc(sp_ready, 1)
                s5_tile(ft, 2)
                if not last:
                    qk_norm(ft + 1)
                s5_tile(ft, 3)

            dve.sem_inc(rem_used, 1)
            qk_vr(0)
            qk_norm(0)
            mixer(0, first=True)
            mixer(1)
            with dve.Fori(1, KS // 2 - 1) as pair:
                for par in range(2):
                    mixer(pair * 2 + par)
            mixer(KS - 2)
            mixer(KS - 1, last=True)
            s5_out(KS - 1)

            for j in range(4):
                dve.wait_ge(yhi_ready, j + 1)
                sl = slice(2 * j, 2 * j + 2)
                v.tensor_tensor(xs[:, sl, T:2 * T], uqkv[:, sl, :], xs[:, sl, 0:T].bitcast(f32), ALU.subtract).then_inc(ylo_ready, 1)
            dve.wait_ge(mr_ready, 1)
            newton(rs2[:, 1, 0, :], rs2[:, 1, 1, :], ps(4, 0, T), SW * EPS).then_inc(mr_done, 1)
            for j in range(4):
                b = j // 2
                if j:
                    dve.wait_ge(sig_ready, j)
                for q in range(2):
                    f = (2 * j + q) % FB
                    bank_wait(f, GLU_B0 + b, GLU_C0 + (b + 1) * GLU_C)
                    v.tensor_reduce(glu_z[:, q, :], halves(f), AX.X, ALU.add).then_inc(acc_free, 1)
                dve.wait_ge(sig_ready, j + 1)
                sl = slice(2 * j, 2 * j + 2)
                v.tensor_tensor(uqkv[:, sl, :], uqkv[:, sl, :], glu_s[:, :, :], ALU.mult).then_inc(y2_ready, 1)
            gw = vec2[:, 16:32]
            link(v.tensor_scalar(gw, gw, math.sqrt(SW), None, ALU.mult, ALU.bypass))

            def mixed(j):
                if j < 8:
                    t0 = (2 * j + KS) % KD
                    kind = 1 if j < 4 else 0
                    if j == 0:
                        dve.wait_ge(mr_done, 1)
                    if j == 4:
                        dve.wait_ge(mr_ready, 2)
                        newton(rs2[:, 0, 0, :], rs2[:, 0, 1, :], ps(5, 0, T), SW * EPS).then_inc(mr_done, 1)
                        dve.wait_ge(mr_done, 2)
                    if j:
                        dve.wait_ge(mlo_ready, j)
                    for q in range(2):
                        v.scalar_tensor_tensor(mix_f[:, q, :], uqkv[:, t0 + q, :], gw[:, t0 + q:t0 + q + 1], rs2[:, kind, 0, :],
                                               ALU.mult, ALU.mult).then_inc(mf_ready if q else dve_const, 1)
                    dve.wait_ge(mhi_ready, j + 1)
                    v.tensor_tensor(xs[:, t0:t0 + 2, T:2 * T], mix_f[:, :, :], xs[:, t0:t0 + 2, 0:T].bitcast(f32),
                                    ALU.subtract).then_inc(mlo_ready, 1)

            for j in range(8):
                mixed(j)

            for b in range(OUT_B):
                ada_chunks(MID, b)
                for f in range(FB):
                    kt = b * FB + f
                    bank_wait(f, OUT_B0 + b, OUT_C0 + (b + 1) * OUT_C)
                    v.tensor_reduce(act_tmp[:, f % 2, :], halves(f), AX.X, ALU.add).then_inc(acc_free, 1)
                    dve.wait_ge(acc_free, FB + (OUT_B0 + b) * FB + f + 1)
                    v.scalar_tensor_tensor(resid[:, kt, :], act_tmp[:, f % 2, :], mods[:, 2 * KD + kt:2 * KD + kt + 1], resid[:, kt, :],
                                           ALU.mult, ALU.add).then_inc(h_ready, 1)
                ada_mods(MID, b)
            modulate(a_ffn[:, :], vec2[:, 0:16], mods[:, 4 * KD:5 * KD])
            dve.wait_ge(fr_ready, 1)
            link(newton(rstd[:, :], rs2[:, 0, 1, :], ps(4, 0, T), D * EPS))
            for j in range(KD // 2):
                if j:
                    dve.wait_ge(flo_ready, j)
                for q in range(2):
                    kt = 2 * j + q
                    link(v.scalar_tensor_tensor(ffn_f[:, q, :], resid[:, kt, :], a_ffn[:, kt:kt + 1], rstd[:, :], ALU.mult, ALU.mult))
                    v.tensor_scalar(ffn_f[:, q, :], ffn_f[:, q, :], mods[:, 3 * KD + kt:3 * KD + kt + 1], None,
                                    ALU.add, ALU.bypass).then_inc(ff_ready if q else dve_const, 1)
                dve.wait_ge(fhi_ready, j + 1)
                v.tensor_tensor(xs[:, 2 * j:2 * j + 2, T:2 * T], ffn_f[:, :, :], xs[:, 2 * j:2 * j + 2, 0:T].bitcast(f32),
                                ALU.subtract).then_inc(flo_ready, 1)

            def hidden(b):
                end = b * UP_C + (UP_C0 + UP_C)
                blk = b + UP_B0
                for f in range(FB):
                    bank_wait(f, blk, end)
                    ins = v.tensor_reduce(ps(4 + f // 2, (f % 2) * T, T), halves(f), AX.X, ALU.add)
                    ins.then_inc(acc_free, 1)
                dve.wait_ge(g_act, b + 1)
                dve.wait_ge(acc_free, blk * FB + (FB + 4))
                v.tensor_tensor(act_tmp[:, :, :], ps(5).rearrange("p (m t) -> p m t", m=2), act_tmp[:, :, :], ALU.mult).then_inc(h_prod, 1)
                dve.wait_ge(hid_hi, b + 1)
                dve.wait_ge(cs_ready, 1)
                tl = ds(b * 2, 2)
                v.tensor_tensor(hid[:, tl, T:2 * T], act_tmp[:, :, :], hid[:, tl, 0:T].bitcast(f32), ALU.subtract).then_inc(hid_lo, 1)

            with dve.Fori(0, 4) as g:
                ada_chunks(UPG, g, 0, 4)
                hidden(g * 2)
                ada_chunks(UPG, g, 4, 8)
                hidden(g * 2 + 1)
                ada_mods(UPG, g)
            with dve.Fori(8, UP_B) as b:
                hidden(b)

            with dve.Fori(0, DN_B // 2) as pair:
                for par in range(2):
                    for f in range(FB):
                        blk = pair * 2 + par
                        kt = blk * FB + f
                        bank_wait(f, blk + DN_B0, blk * DN_C + (DN_C0 + DN_C))
                        v.tensor_reduce(act_tmp[:, f % 2, :], halves(f), AX.X, ALU.add).then_inc(acc_free, 1)
                        dve.wait_ge(ot_ps, blk * 2 + 2)
                        dve.wait_ge(acc_free, blk * FB + (FB + DN_B0 * FB + f + 1))
                        v.scalar_tensor_tensor(h_out[:, par, f:f + 1, :], act_tmp[:, f % 2, :].unsqueeze(1),
                                               mods[:, ds(kt + 5 * KD, 1)], resid[:, ds(kt, 1), :],
                                               ALU.mult, ALU.add).then_inc(o_ready if f == FB - 1 else dve_const, 1)


_VEC = ["c", "b_ada", "g_mix", "log_dt", "q_gain", "k_gain", "g_ssm_out", "g_attn_out", "g_ffn"]
_MAT = ["x", "w_ada", "w_in", "a_re", "a_im", "b_re", "b_im", "c_re", "c_im", "d_skip", "w_glu", "w_out",
        "w_gate", "w_up", "w_down"]


def kernel(**inputs):
    import numpy as _np
    import concourse.bacc as _bacc
    from concourse import mybir as _mybir
    from concourse.bass_utils import run_bass_kernel_spmd as _run

    nc = _bacc.Bacc("TRN2", target_bir_lowering=False, num_devices=1)
    arrays, args = {}, {}
    for name in _VEC + _MAT:
        v = _np.ascontiguousarray(inputs[name])
        v = v.reshape(v.shape[1:])
        arrays[f"in_{name}"] = v
        args[name] = nc.dram_tensor(f"in_{name}", v.shape, _mybir.dt.from_np(v.dtype), kind="ExternalInput").ap()
    args["out"] = nc.dram_tensor("out_h", (T, D), _mybir.dt.float32, kind="ExternalOutput").ap()
    build(nc, args)
    r = _run(nc, [arrays], core_ids=[0])
    return r.results[0]["out_h"].reshape(1, T, D)
```

```python
import math
from contextlib import ExitStack

import numpy as np
import concourse.bass as bass
from concourse import mybir

P = 128
D = 2048
T = 256
KD = D // P
SW = 1024
KS = SW // P
GROUPS, GH, NS = 64, 16, 64
ST = GROUPS * NS // P
DH = 64
FF = 5632
KF = FF // P
NMOD = 6 * D
EPS = 1e-6
TC = 128
NC = T // TC
CK, CW = 2, 512
RAW, SPL, ADA = 8, 4, 4
FB = CW // P

IN_B, IN_C = 4 * SW // CW, KD // CK
GLU_B, GLU_C = SW // CW, KS // CK
OUT_B, OUT_C = D // CW, KD // CK
UP_B, UP_C = 2 * FF // CW, KD // CK
DN_B, DN_C = D // CW, KF // CK
GLU_C0 = IN_B * IN_C
OUT_C0 = GLU_C0 + GLU_B * GLU_C
UP_C0 = OUT_C0 + OUT_B * OUT_C
DN_C0 = UP_C0 + UP_B * UP_C
GLU_B0 = IN_B
OUT_B0 = GLU_B0 + GLU_B
UP_B0 = OUT_B0 + OUT_B
DN_B0 = UP_B0 + UP_B
ADA_G = NMOD // CW
ADA_C = KD // CK
ADA_T = (3, 6)


class Ada:

    def __init__(self, g0, count, shared, before=None):
        self.g0, self.count = g0, count
        self.tensor = ADA_T if shared else ()
        self.vper, self.tper = CK * (ADA_C - len(self.tensor)), len(self.tensor)
        self.v0 = before.v0 + before.count * before.vper if before else 0
        self.t0 = before.t0 + before.count * before.tper if before else 0

    def used(self, i, c):
        if c in self.tensor:
            return True, i * self.tper + (self.t0 + sum(x <= c for x in self.tensor))
        return False, i * self.vper + (self.v0 + CK * sum(x not in self.tensor for x in range(c + 1)))


PRE = Ada(0, 2 * D // CW, True)
INP = Ada(PRE.count, IN_B, False, PRE)
MID = Ada(INP.g0 + INP.count, OUT_B, False, INP)
UPG = Ada(MID.g0 + MID.count, 4, False, MID)


def build(nc, a):
    f32, f32r, bf16, i32 = mybir.dt.float32, mybir.dt.float32r, mybir.dt.bfloat16, mybir.dt.int32
    ALU, ACT, AX = mybir.AluOpType, mybir.ActivationFunctionType, mybir.AxisListType
    ds = bass.ds

    def chunks(w):
        return w.rearrange("(c t p) n -> c p t n", t=CK, p=P)

    w_in, w_glu, w_out = chunks(a["w_in"]), chunks(a["w_glu"]), chunks(a["w_out"])
    w_gate, w_up, w_down = chunks(a["w_gate"]), chunks(a["w_up"]), chunks(a["w_down"])
    w_ada = chunks(a["w_ada"])

    ctx = ExitStack()
    with ctx:
        def sb(name, shape, dt=f32):
            return ctx.enter_context(nc.sbuf_tensor(name, shape, dt))

        def sem(name):
            return ctx.enter_context(nc.semaphore(name))

        raw = sb("raw", [P, RAW, CK, CW])
        hi = sb("hi", [P, SPL, CK, CW], f32r)
        lo_at = (nc.sbuf_base + 31) // 32 * 32
        lo = sb("lo", [P, SPL, CK, CW], f32r)
        resid = sb("resid", [P, KD, T])
        xs_at = (nc.sbuf_base + 31) // 32 * 32
        xs = sb("xs", [P, KD, 2 * T], f32r)
        ar_at = (nc.sbuf_base + 31) // 32 * 32
        hid = sb("hid", [P, KF, 2 * T], f32r)
        ident = sb("ident", [P, P])
        ones = sb("ones", [P, P])
        head_ones = sb("head_ones", [P, P])
        neg_tri = sb("neg_tri", [P, P])
        neg_ones = sb("neg_ones", [P, P])
        ident_b = sb("ident_b", [P, P], bf16)
        mask_b = sb("mask_b", [P, P], bf16)
        vec1 = sb("vec1", [P, P])
        vec2 = sb("vec2", [P, 106])
        mods = sb("mods", [P, NMOD // P])
        a_mix = sb("a_mix", [P, KD])
        a_ffn = sb("a_ffn", [P, KD])
        cs = sb("cs", [P, KD])
        eps = sb("eps", [P, 5])
        grp = sb("grp", [P, 2])
        rstd = sb("rstd", [P, T])
        act_tmp = sb("act_tmp", [P, 2, T])

        def over(name, base, at, shape, dt=f32):
            return nc.alloc_sbuf_tensor_at(name, shape, dt, offset=base + 4 * at)

        tabs = over("tabs", ar_at, 0, [P, 2, ST, TC])
        uqkv = over("uqkv", ar_at, 8192, [P, 32, T])
        b_bar = over("b_bar", ar_at, 16384, [P, 2, ST, GH])
        ada_acc = over("ada_acc", ar_at, 17408, [P, 2, CW])
        ada_raw = over("ada_raw", ar_at, 18432, [P, ADA, CK, CW])
        x_tok = over("x_tok", ar_at, 8192, [P, 2, D])
        x_n = over("x_n", ar_at, 8192, [P, KD, T])
        b_raw = over("b_raw", ar_at, 12288, [P, 2, ST, GH])
        rows = over("rows", ar_at, 13312, [P, 2, P])
        ldt = over("ldt", ar_at, 13568, [P, GROUPS])
        tiny = over("tiny", ar_at, 13632, [P, 24, ST])
        tiny_i = over("tiny_i", ar_at, 14400, [P, ST], i32)
        nrm = over("nrm", ar_at, 14432, [P, T])
        sqx = over("sqx", ar_at, 14720, [P, 2, 2, T])
        ptiny = over("ptiny", ar_at, 15744, [P, 2, ST])
        btmp = over("btmp", ar_at, 10240, [P, 2, ST, GH])
        ptmp = over("ptmp", lo_at, 0, [P, 2, ST, TC // 2])
        pre_raw = over("pre_raw", xs_at, 0, [P, ADA_C, CK, CW])
        c_raw = over("c_raw", xs_at, 0, [P, KS, 2, NS])
        bx = over("bx", xs_at, 1024, [P, 2, 4, 2, GH])
        cx = over("cx", xs_at, 1280, [P, 2, 2, NS])
        bc = over("bc", xs_at, 1536, [P, 2, 4, P])
        v_y = over("v_y", xs_at, 2560, [P, 2, 2, T])
        carry = over("carry", xs_at, 4096, [P, 4])
        rem = over("rem", xs_at, 4128, [P, 2, 4, T])
        u_st = over("u_st", xs_at, 6176, [P, 2, T])
        qk_n = over("qk_n", xs_at, 3584, [P, 2, T])
        v_st = over("v_st", xs_at, 6688, [P, T])
        qk_a = over("qk_a", xs_at, 6944, [P, 2, T])
        qk_r = over("qk_r", xs_at, 7456, [P, 2, T])
        sp = over("sp", ar_at, 18432, [P, 2, 3, P])
        w_t = over("w_t", ar_at, 19200, [P, 2, 3, P])
        v_t = over("v_t", ar_at, 19968, [P, 2, 2, P])
        dem = over("dem", ar_at, 20480, [P, 2, 4, T])
        glu_z = over("glu_z", ar_at, 12288, [P, 2, T])
        glu_s = over("glu_s", ar_at, 12800, [P, 2, T])
        mix_f = over("mix_f", ar_at, 13312, [P, 2, 2, T])
        msq = over("msq", ar_at, 14336, [P, 2, 2, T])
        rs2 = over("rs2", ar_at, 15360, [P, 2, 2, T])
        ffn_f = over("ffn_f", ar_at, 8192, [P, 2, 2, T])
        out_s = over("out_s", xs_at, 0, [P, 2, 2, CW])
        h_out = over("h_out", xs_at, 2048, [P, 2, FB, T])

        acc = ctx.enter_context(nc.psum_tensor("acc", [P, 8, 512], f32))

        def ps(bank, lo_=0, n=512):
            return acc[:, bank, lo_:lo_ + n]

        rows_in, x_in, b_in, c_in, out_done = sem("rows_in"), sem("x_in"), sem("b_in"), sem("c_in"), sem("out_done")
        raw_full = [sem(f"raw_full{s}") for s in range(RAW)]
        pre_full = [sem(f"pre_full{c}") for c in range(ADA_C)]
        ada_full = [sem(f"ada_full{s}") for s in range(ADA)]
        hi_ready, lo_ready = sem("hi_ready"), sem("lo_ready")
        chunk_done = sem("chunk_done")
        acc_ready = sem("acc_ready")
        acc_free = sem("acc_free")
        ada_mac, ada_pe = sem("ada_mac"), sem("ada_pe")
        ada_sum, mod_ready = sem("ada_sum"), sem("mod_ready")
        cols_ready = sem("cols_ready")
        dve_step = sem("dve_step")
        rows_t, vec_ready, cs_ready, lam_ready = sem("rows_t"), sem("vec_ready"), sem("cs_ready"), sem("lam_ready")
        dve_chain, pool_chain, act_chain = sem("dve_chain"), sem("pool_chain"), sem("act_chain")
        tab_ready, bbar_ready, den_ready = sem("tab_ready"), sem("bbar_ready"), sem("den_ready")
        xt_ps, xt_ready, sqx_ready, ssx_ready = sem("xt_ps"), sem("xt_ready"), sem("sqx_ready"), sem("ssx_ready")
        sqx_used, rx_ready = sem("sqx_used"), sem("rx_ready")
        xf_ready, xhi_ready, xlo_ready = sem("xf_ready"), sem("xhi_ready"), sem("xlo_ready")
        bcx_ready, bc_ps, bc_ready, u_ready = sem("bcx_ready"), sem("bc_ps"), sem("bc_ready"), sem("u_ready")
        bu_ready, bu_used, v_ready, s5_chain = sem("bu_ready"), sem("bu_used"), sem("v_ready"), sem("s5_chain")
        rem_ready, rem_used, y_ready = sem("rem_ready"), sem("rem_used"), sem("y_ready")
        qsq_ready, qss_ready, qr_ready, qn_chain = sem("qsq_ready"), sem("qss_ready"), sem("qr_ready"), sem("qn_chain")
        qt_ready, qrn_ready, qkn_ready = sem("qt_ready"), sem("qrn_ready"), sem("qkn_ready")
        vst_ready, vt_ps, vt_ready = sem("vst_ready"), sem("vt_ps"), sem("vt_ready")
        z_ready, ln_ready, sp_ready, zs_ready, w_ready = sem("z_ready"), sem("ln_ready"), sem("sp_ready"), sem("zs_ready"), sem("w_ready")
        act_z = sem("act_z")
        av_ready, attn_ready = sem("av_ready"), sem("attn_ready")
        gelu_ready, yhi_ready, ylo_ready = sem("gelu_ready"), sem("yhi_ready"), sem("ylo_ready")
        sig_ready, y2_ready = sem("sig_ready"), sem("y2_ready")
        msq_ready, msq_used, mr_ready = sem("msq_ready"), sem("msq_used"), sem("mr_ready")
        mr_done = sem("mr_done")
        mf_ready, mhi_ready, mlo_ready = sem("mf_ready"), sem("mhi_ready"), sem("mlo_ready")
        h_ready, fsq_ready, fsq_used, fss_ready, fr_ready = sem("h_ready"), sem("fsq_ready"), sem("fsq_used"), sem("fss_ready"), sem("fr_ready")
        ff_ready, fhi_ready, flo_ready = sem("ff_ready"), sem("fhi_ready"), sem("flo_ready")
        g_act, h_prod, hid_hi, hid_lo = sem("g_act"), sem("h_prod"), sem("hid_hi"), sem("hid_lo")
        o_ready, ot_ps, ot_ready = sem("o_ready"), sem("ot_ps"), sem("ot_ready")

        block = ctx.enter_context(nc.Block())

        def store(eng, b):
            for i in range(2):
                eng.wait_ge(ot_ready, 2 * b + i + 3)
                eng.dma_start(a["out"][i * P:(i + 1) * P, b * CW:(b + 1) * CW], out_s[:, b % 2, i, :]).then_inc(out_done, 16)

        def ada_slot(ph, i, c):
            if ph is PRE:
                return pre_raw[:, c, :, :], pre_full[c], i * 16 + 16
            return ada_raw[:, c % ADA, :, :], ada_full[c % ADA], \
                (i + (ph.g0 - PRE.count)) * (16 * ADA_C // ADA) + 16 * (c // ADA + 1)

        @block.sync
        def _(sp_):
            def ada_chunk(ph, i, c):
                ring = ADA_C if ph is PRE else ADA
                first = isinstance(i, int) and i == 0
                if c < ring and ph in (MID, UPG):
                    sp_.wait_ge(ada_mac, ph.v0)
                    sp_.wait_ge(ada_pe, ph.t0)
                if c >= ring or not first:
                    tensor, value = ph.used(i, c - ring) if c >= ring else ph.used(i - 1, c - ring + ADA_C)
                    sp_.wait_ge(ada_pe if tensor else ada_mac, value)
                dst, full = (pre_raw[:, c, :, :], pre_full[c]) if ph is PRE else (ada_raw[:, c % ADA, :, :], ada_full[c % ADA])
                sp_.dma_start(dst, w_ada[c, :, :, ds((i + ph.g0) * CW, CW)]).then_inc(full, 16)

            def row(i, at, n, src):
                sp_.dma_start(rows[at:at + n, i, :], src).then_inc(rows_in, 16)

            row(0, 0, 96, a["b_ada"].rearrange("(r c) -> r c", c=P))
            row(0, 96, 16, a["c"].rearrange("(r c) -> r c", c=P))
            row(0, 112, 16, a["g_mix"].rearrange("(r c) -> r c", c=P))
            row(1, 0, 16, a["g_ffn"].rearrange("(r c) -> r c", c=P))
            row(1, 16, 8, a["g_ssm_out"].rearrange("(r c) -> r c", c=P))
            row(1, 24, 8, a["g_attn_out"].rearrange("(r c) -> r c", c=P))
            row(1, 32, 8, a["d_skip"].rearrange("(r g) h -> r (g h)", g=8))
            row(1, 40, 32, a["a_re"].rearrange("(r g) n -> r (g n)", g=2))
            row(1, 72, 32, a["a_im"].rearrange("(r g) n -> r (g n)", g=2))
            for i, name in enumerate(("q_gain", "k_gain")):
                sp_.dma_start(rows[104 + i:105 + i, 1, :].rearrange("o (g n) -> o g n", g=2),
                              a[name].rearrange("(o g n) -> o g n", o=1, g=1).to_broadcast([1, 2, DH])
                              ).then_inc(rows_in, 16)
            sp_.dma_start(ldt[:, :], a["log_dt"].rearrange("(o n) -> o n", o=1).to_broadcast([P, GROUPS])
                          ).then_inc(rows_in, 16)
            for i in range(2):
                sp_.dma_start(x_tok[:, i, :], a["x"][i * P:(i + 1) * P, :]).then_inc(x_in, 16)
            for c in range(ADA_C):
                ada_chunk(PRE, 0, c)
            for i, name in enumerate(("b_re", "b_im")):
                sp_.dma_start(b_raw[:, i, :, :], a[name].rearrange("(t g) n h -> (g n) t h", g=2)).then_inc(b_in, 16)
            with sp_.Fori(1, PRE.count) as g:
                for c in range(ADA_C):
                    ada_chunk(PRE, g, c)
            for c in range(IN_C):
                sp_.dma_start(raw[:, c, :, :], w_in[c, :, :, 0:CW]).then_inc(raw_full[c], 16)
            for c in range(ADA_C):
                ada_chunk(INP, 0, c)
            with sp_.Fori(1, IN_B) as b:
                for c in range(IN_C):
                    sp_.wait_ge(lo_ready, b * IN_C + c - RAW + 1)
                    sp_.dma_start(raw[:, c, :, :], w_in[c, :, :, ds(b * CW, CW)]).then_inc(raw_full[c], 16)
                    ada_chunk(INP, b, c)
            for c in range(GLU_B * GLU_C):
                if c == SPL:
                    sp_.wait_ge(chunk_done, SPL + GLU_C0)
                    for i, name in enumerate(("c_re", "c_im")):
                        sp_.dma_start(c_raw[:, :, i, :], a[name].rearrange("(f g) h n -> (g h) f n", f=KS)).then_inc(c_in, 16)
                sp_.wait_ge(lo_ready, GLU_C0 + c - RAW + 1)
                sp_.dma_start(raw[:, c % RAW, :, :],
                              w_glu[c % GLU_C, :, :, (c // GLU_C) * CW:(c // GLU_C + 1) * CW]).then_inc(raw_full[c % RAW], 16)
            for n in range(OUT_B * OUT_C):
                b, c = divmod(n, OUT_C)
                sp_.wait_ge(lo_ready, OUT_C0 + n - RAW + 1)
                sp_.dma_start(raw[:, c, :, :], w_out[(c + KS // CK) % OUT_C, :, :, b * CW:(b + 1) * CW]).then_inc(raw_full[c], 16)
                if n == OUT_C - 1:
                    sp_.wait_ge(attn_ready, KS + 1)
                    for c_ in range(ADA_C):
                        ada_chunk(MID, 0, c_)
                elif b:
                    ada_chunk(MID, b, c)

            def up_block(b):
                for c in range(UP_C):
                    sp_.wait_ge(lo_ready, b * UP_C + (UP_C0 + c - RAW + 1))
                    for w, cols in ((w_gate, (0, 256)), (w_up, (256, 512))):
                        sp_.dma_start(raw[:, c, :, cols[0]:cols[1]], w[c, :, :, ds(b * 256, 256)]).then_inc(raw_full[c], 16)

            with sp_.Fori(0, 4) as g:
                for half in range(2):
                    up_block(g * 2 + half)
                    for c in range(ADA_C // 2 * half, ADA_C // 2 * (half + 1)):
                        ada_chunk(UPG, g, c)
            with sp_.Fori(8, UP_B) as b:
                up_block(b)
            for b in range(DN_B):
                for c in range(DN_C):
                    n = b * DN_C + c
                    sp_.wait_ge(lo_ready, DN_C0 + n - RAW + 1)
                    sp_.dma_start(raw[:, n % RAW, :, :], w_down[c, :, :, b * CW:(b + 1) * CW]).then_inc(raw_full[n % RAW], 16)
                if b >= 1:
                    store(sp_, b - 1)
            store(sp_, DN_B - 1)
            sp_.wait_ge(out_done, 16 * 2 * DN_B)

        @block.gpsimd
        def _(pool):
            n = [0]

            def link(ins):
                n[0] += 1
                ins.then_inc(pool_chain, 1)
                pool.wait_ge(pool_chain, n[0])

            g = nc.gpsimd
            link(g.memset(ident[:, :], 0.0))
            link(g.affine_select(out=ident[:, :], in_=ident[:, :], compare_op=ALU.not_equal, fill=1.0, base=0,
                                 pattern=[[-1, P]], channel_multiplier=1))
            g.memset(ones[:, :], 1.0).then_inc(cols_ready, 1)
            link(g.memset(neg_ones[:, :], -1.0))
            link(g.affine_select(out=neg_tri[:, :], in_=neg_ones[:, :], compare_op=ALU.is_ge, fill=0.0, base=0,
                                 pattern=[[-1, P]], channel_multiplier=1))
            link(g.affine_select(out=head_ones[:, 0:DH], in_=ones[:, 0:DH], compare_op=ALU.is_ge, fill=0.0, base=DH - 1,
                                 pattern=[[0, DH]], channel_multiplier=-1))
            link(g.affine_select(out=head_ones[:, DH:P], in_=ones[:, DH:P], compare_op=ALU.is_ge, fill=0.0, base=-DH,
                                 pattern=[[0, DH]], channel_multiplier=1))
            link(g.tensor_copy(ident_b[:, :], ident[:, :]))
            link(g.memset(mask_b[:, :], -1e30))
            link(g.affine_select(out=mask_b[:, :], in_=mask_b[:, :], compare_op=ALU.is_ge, fill=0.0, base=0,
                                 pattern=[[-1, P]], channel_multiplier=1))
            link(g.memset(grp[:, :], 1.0))
            for q in range(6, -1, -1):
                link(g.affine_select(out=grp[:, 1:2], in_=grp[:, 1:2], compare_op=ALU.is_ge, fill=float(q % 2),
                                     base=-16 * (q + 1), pattern=[[0, 1]], channel_multiplier=1))
            link(g.tensor_tensor(grp[:, 0:1], ones[:, 0:1], grp[:, 1:2], ALU.subtract))
            for i, v in enumerate((D * EPS, DH * EPS, SW * EPS, -0.5 * math.log(2))):
                link(g.memset(eps[:, i:i + 1], v))
            g.memset(eps[:, 4:5], 1.5).then_inc(cols_ready, 1)

            pool.wait_ge(vec_ready, 2)
            tn = [4]

            def new():
                tn[0] += 1
                assert tn[0] <= 21
                return tiny[:, tn[0] - 1, :]

            def ts(o, i_, s1, s2, o1, o2):
                link(g.tensor_scalar(o, i_, s1, s2, o1, o2))

            def tt(o, i0, i1, op):
                link(g.tensor_tensor(o, i0, i1, op))

            def stt(o, i0, s1, i1, o1, o2):
                link(g.tensor_scalar(tiny[:, 21, :], i0, s1, None, o1, ALU.bypass))
                link(g.tensor_tensor(o, tiny[:, 21, :], i1, o2))

            MAGIC = 12582912.0
            LN2_HI, LN2_LO = 0.693359375, -2.12194440e-4
            kf, fr, ex, sc = new(), new(), new(), new()

            def expm1(x, em1):
                ts(kf, x, 1.4426950408889634, MAGIC, ALU.mult, ALU.add)
                ts(kf, kf, MAGIC, 126.0, ALU.subtract, ALU.min)
                ts(kf, kf, -126.0, None, ALU.max, ALU.bypass)
                stt(fr, kf, -LN2_HI, x, ALU.mult, ALU.add)
                stt(fr, kf, -LN2_LO, fr, ALU.mult, ALU.add)
                ts(ex, fr, 1 / 5040, None, ALU.mult, ALU.bypass)
                for c_ in (1 / 720, 1 / 120, 1 / 24, 1 / 6, 0.5, 1.0):
                    stt(ex, ex, c_, fr, ALU.add, ALU.mult)
                ts(tiny_i[:, :], kf, 127.0, 8388608.0, ALU.add, ALU.mult)
                link(g.tensor_copy(sc, tiny_i[:, :].bitcast(f32)))
                tt(ex, ex, sc, ALU.mult)
                stt(em1, sc, -1.0, ex, ALU.add, ALU.add)

            a_re, a_im = vec2[:, 40:72], vec2[:, 72:104]
            dt_ = new()
            for q in range(2):
                rq = slice(DH * q, DH * (q + 1))
                link(g.tensor_copy(dt_[rq, :], ldt[rq, q::2]))
            expm1(dt_, dt_)
            ts(dt_, dt_, 1.0, None, ALU.add, ALU.bypass)
            em, th, cm, sn, z2, zz = new(), new(), new(), new(), new(), new()
            tt(em, a_re, dt_, ALU.mult)
            expm1(em, em)
            tt(th, a_im, dt_, ALU.mult)
            ts(kf, th, 1 / (2 * math.pi), MAGIC, ALU.mult, ALU.add)
            ts(kf, kf, MAGIC, None, ALU.subtract, ALU.bypass)
            C1 = 6.28125
            C2 = float(np.float32(math.floor((2 * math.pi - C1) * 2 ** 21) / 2 ** 21))
            C3 = 2 * math.pi - C1 - C2
            for c_ in (C1, C2, C3):
                stt(th, kf, -c_, th, ALU.mult, ALU.add)
            ts(th, th, 0.5, None, ALU.mult, ALU.bypass)
            tt(z2, th, th, ALU.mult)
            ts(sn, z2, 1 / math.factorial(13), None, ALU.mult, ALU.bypass)
            for k_ in (11, 9, 7, 5, 3):
                stt(sn, sn, (-1.0) ** (k_ // 2) / math.factorial(k_), z2, ALU.add, ALU.mult)
            stt(sn, sn, 1.0, th, ALU.add, ALU.mult)
            ts(cm, z2, -1 / math.factorial(14), None, ALU.mult, ALU.bypass)
            for k_ in (12, 10, 8, 6, 4, 2):
                stt(cm, cm, (-1.0) ** (k_ // 2) / math.factorial(k_), z2, ALU.add, ALU.mult)
            tt(zz, sn, sn, ALU.mult)
            ts(zz, zz, -2.0, None, ALU.mult, ALU.bypass)
            stt(cm, cm, 1.0, sn, ALU.add, ALU.mult)
            ts(sn, cm, 2.0, None, ALU.mult, ALU.bypass)
            ts(tiny[:, 0, :], zz, 1.0, None, ALU.add, ALU.bypass)
            ts(tiny[:, 1, :], sn, -1.0, None, ALU.mult, ALU.bypass)
            re_, im_, t0, den = new(), new(), new(), tiny[:, 23, :]
            tt(re_, em, tiny[:, 0, :], ALU.mult)
            tt(re_, re_, zz, ALU.add)
            stt(im_, em, 1.0, sn, ALU.add, ALU.mult)
            pool.wait_ge(den_ready, 1)
            tt(tiny[:, 2, :], re_, a_re, ALU.mult)
            tt(t0, im_, a_im, ALU.mult)
            tt(tiny[:, 2, :], tiny[:, 2, :], t0, ALU.add)
            tt(tiny[:, 2, :], tiny[:, 2, :], den, ALU.mult)
            tt(tiny[:, 3, :], im_, a_re, ALU.mult)
            tt(t0, re_, a_im, ALU.mult)
            tt(tiny[:, 3, :], tiny[:, 3, :], t0, ALU.subtract)
            tt(tiny[:, 3, :], tiny[:, 3, :], den, ALU.mult)
            decay = vec2[:, 40:72]
            g.tensor_scalar(decay, em, 1.0, None, ALU.add, ALU.bypass).then_inc(lam_ready, 1)


            cosp, sinp = tabs[:, 0, :, :], tabs[:, 1, :, :]

            def unit(j):
                c_, s_ = cosp[:, :, j], sinp[:, :, j]
                t0, t1 = ptiny[:, 0, :], ptiny[:, 1, :]
                link(g.tensor_tensor(t0, c_, c_, ALU.mult))
                link(g.tensor_tensor(t1, s_, s_, ALU.mult))
                link(g.tensor_tensor(t0, t0, t1, ALU.add))
                link(g.tensor_scalar(t0, t0, -0.5, 1.5, ALU.mult, ALU.add))
                link(g.tensor_tensor(c_, c_, t0, ALU.mult))
                link(g.tensor_tensor(s_, s_, t0, ALU.mult))

            link(g.tensor_copy(cosp[:, :, 0], tiny[:, 0, :]))
            link(g.tensor_copy(sinp[:, :, 0], tiny[:, 1, :]))
            unit(0)
            w = 1
            while w < TC:
                p0, p1 = ptmp[:, 0, :, 0:w], ptmp[:, 1, :, 0:w]
                c0, s0, c1, s1 = cosp[:, :, 0:w], sinp[:, :, 0:w], cosp[:, :, w:2 * w], sinp[:, :, w:2 * w]
                cn, sn = (x[:, :, w - 1:w].to_broadcast([P, ST, w]) for x in (cosp, sinp))
                link(g.tensor_tensor(p0, c0, cn, ALU.mult))
                link(g.tensor_tensor(p1, s0, sn, ALU.mult))
                link(g.tensor_tensor(c1, p0, p1, ALU.subtract))
                link(g.tensor_tensor(p0, c0, sn, ALU.mult))
                link(g.tensor_tensor(p1, s0, cn, ALU.mult))
                link(g.tensor_tensor(s1, p0, p1, ALU.add))
                w *= 2
                unit(w - 1)
            pool.sem_inc(tab_ready, 1)

            def low(value, slot, s):
                pool.wait_ge(hi_ready, value + 1)
                g.tensor_tensor(lo[:, s, :, :], raw[:, slot, :, :], hi[:, s, :, :].bitcast(f32), ALU.subtract).then_inc(lo_ready, 1)

            with pool.Fori(0, IN_B) as b:
                for c in range(IN_C):
                    low(b * IN_C + c, c % RAW, c % SPL)

            pool.wait_ge(chunk_done, SPL + GLU_C0)
            pool.wait_ge(c_in, 32)
            link(g.tensor_scalar(c_raw[:, :, 1, :], c_raw[:, :, 1, :], -1.0, None, ALU.mult))
            pool.wait_ge(bbar_ready, 1)

            def bc_blocks(ft):
                pool.wait_ge(bc_ps, ft + 1)
                pool.wait_ge(cols_ready, 2)
                for q in range(2):
                    g.tensor_tensor(bx[:, :, :, q, :], b_bar[:, :, ds(ft * 4, 4), :],
                                    head_ones[:, 127 * q:127 * q + 1].unsqueeze(2).unsqueeze(3).to_broadcast([P, 2, 4, GH]),
                                    ALU.mult).then_inc(bcx_ready, 1)
                for q in range(2):
                    g.tensor_tensor(cx[:, :, q, :], c_raw[:, ds(ft, 1), :, :].rearrange("p o r n -> p (o r) n"),
                                          grp[:, q:q + 1].unsqueeze(2).to_broadcast([P, 2, NS]), ALU.mult).then_inc(bcx_ready, 1)

            def refine(ft):
                pool.wait_ge(qt_ready, ft + 1)
                g.tensor_tensor(qk_a[:, :, :], qk_a[:, :, :], qk_r[:, :, :], ALU.mult).then_inc(qn_chain, 1)
                pool.wait_ge(qn_chain, ft * 2 + 1)
                g.tensor_tensor(qk_a[:, :, :], eps[:, 4:5].unsqueeze(2).to_broadcast([P, 2, T]), qk_a[:, :, :],
                                ALU.subtract).then_inc(qn_chain, 1)
                pool.wait_ge(qn_chain, ft * 2 + 2)
                g.tensor_tensor(qk_r[:, :, :], qk_r[:, :, :], qk_a[:, :, :], ALU.mult).then_inc(qrn_ready, 1)

            def turned(tile, par):
                pool.wait_ge(bu_used, tile + 3)
                g.tensor_tensor(v_y[:, par, 0, :], dem[:, par, 0, :], dem[:, par, 1, :], ALU.subtract).then_inc(v_ready, 1)
                g.tensor_tensor(v_y[:, par, 1, :], dem[:, par, 2, :], dem[:, par, 3, :], ALU.add).then_inc(v_ready, 1)

            bc_blocks(0)
            refine(0)
            turned(0, 0)
            with pool.Fori(0, KS - 2) as ft:
                bc_blocks(ft + 1)
                turned(ft * 4 + 1, 1)
                turned(ft * 4 + 2, 0)
                turned(ft * 4 + 3, 1)
                refine(ft + 1)
                turned(ft * 4 + 4, 0)
            ft = KS - 2
            bc_blocks(ft + 1)
            for i in range(1, 5):
                turned(ft * 4 + i, i % 2)
                low(GLU_C0 + i - 1, i - 1, i - 1)
                if i == 3:
                    refine(ft + 1)
            for i in range(1, 4):
                turned(4 * (KS - 1) + i, i % 2)

            for c in range(SPL, RAW):
                low(GLU_C0 + c, c, c % SPL)
            for first, count in ((OUT_C0, OUT_B), (UP_C0, UP_B), (DN_C0, DN_B * DN_C // RAW)):
                with pool.Fori(0, count) as b:
                    for c in range(RAW):
                        low(b * RAW + (first + c), c, c % SPL)

        @block.scalar
        def _(act):
            s = nc.scalar
            n = [0]

            def link(ins):
                n[0] += 1
                ins.then_inc(act_chain, 1)
                act.wait_ge(act_chain, n[0])

            def high(value, c, full):
                act.wait_ge(raw_full[c], full)
                act.wait_ge(chunk_done, value + 1)
                s.activation(hi[:, c % SPL, :, :], raw[:, c, :, :], ACT.Copy).then_inc(hi_ready, 1)

            act.wait_ge(rows_t, 1)
            s.activation(vec1[:, :], ps(0, 0, P), ACT.Copy).then_inc(vec_ready, 1)
            act.wait_ge(rows_t, 2)
            s.activation(vec2[:, :], ps(1, 0, 106), ACT.Copy).then_inc(vec_ready, 1)
            act.wait_ge(vec_ready, 2)
            s.activation(cs[:, :], vec1[:, 96:112], ACT.Silu).then_inc(cs_ready, 1)

            act.wait_ge(cols_ready, 2)
            for j in range(KD // 2):
                act.wait_ge(xt_ps, j + 1)
                s.activation(resid[:, 2 * j:2 * j + 2, :], ps(j % 4), ACT.Copy).then_inc(xt_ready, 1)
                if j >= 2:
                    act.wait_ge(sqx_used, j - 1)
                act.wait_ge(xt_ready, j + 1)
                s.activation(sqx[:, j % 2, :, :], resid[:, 2 * j:2 * j + 2, :], ACT.Square).then_inc(sqx_ready, 1)
            act.wait_ge(ssx_ready, 1)
            link(s.activation(rstd[:, :], ps(4, 0, T), ACT.Ln, bias=eps[:, 0:1]))
            s.activation(rstd[:, :], rstd[:, :], ACT.Exp, scale=-0.5).then_inc(rx_ready, 1)

            for c in range(SPL):
                high(c, c, 16)
            for j in range(4):
                act.wait_ge(xf_ready, j + 1)
                s.activation(xs[:, 4 * j:4 * j + 4, 0:T], x_n[:, 4 * j:4 * j + 4, :], ACT.Copy).then_inc(xhi_ready, 1)
            for c in range(SPL, IN_C):
                high(c, c, 16)
            with act.Fori(1, IN_B) as b:
                for c in range(IN_C):
                    high(b * IN_C + c, c, b * 16 + 16)

            for c in range(SPL):
                high(GLU_C0 + c, c, 16 * (GLU_C0 // RAW + 1))

            heads = uqkv[:, :, :].rearrange("p (m f) t -> p m f t", m=4)
            act.wait_ge(acc_free, FB + IN_B * FB)
            act.wait_ge(chunk_done, SPL + GLU_C0)

            def copies(ft, par):
                s.activation(u_st[:, par, :].unsqueeze(1), uqkv[:, ds(ft, 1), :], ACT.Copy).then_inc(u_ready, 1)
                s.activation(v_st[:, :].unsqueeze(1), uqkv[:, ds(ft + 3 * KS, 1), :], ACT.Copy).then_inc(vst_ready, 1)
                if not (isinstance(ft, int) and ft == 0):
                    act.wait_ge(qrn_ready, ft)
                s.activation(qk_a[:, :, :].unsqueeze(2), heads[:, 1:3, ds(ft, 1), :], ACT.Square).then_inc(qsq_ready, 1)

            def bc_copy(ft, par):
                act.wait_ge(bc_ps, ft + 2)
                s.activation(bc[:, par, :, :], ps(2), ACT.Copy).then_inc(bc_ready, 1)

            def norm_ln(ft):
                act.wait_ge(qss_ready, ft + 1)
                if not (isinstance(ft, int) and ft == 0):
                    act.wait_ge(qkn_ready, ft)
                s.activation(qk_r[:, :, :], ps(7), ACT.Ln, bias=eps[:, 1:2]).then_inc(act_z, 1)

            def norm_exp(ft, links):
                act.wait_ge(act_z, links)
                s.activation(qk_r[:, :, :], qk_r[:, :, :], ACT.Exp, bias=eps[:, 3:4], scale=-0.5).then_inc(qr_ready, 1)

            def v_copy(ft, par):
                act.wait_ge(vt_ps, ft + 1)
                s.activation(v_t[:, par, :, :], ps(2, 0, T), ACT.Copy).then_inc(vt_ready, 1)

            def mixer(ft, par, last=False):
                z = acc[:, 0:2, 0:384]
                spv = sp[:, :, :, :].rearrange("p h m t -> p h (m t)")
                if not last:
                    copies(ft + 1, 1 - par)
                act.wait_ge(z_ready, ft + 1)
                s.activation(spv, z, ACT.Abs).then_inc(act_z, 1)
                act.wait_ge(act_z, ft * 3 + 2)
                s.activation(spv, spv, ACT.Exp, scale=-1.0).then_inc(act_z, 1)
                act.wait_ge(act_z, ft * 3 + 3)
                s.activation(spv, spv, ACT.Ln, bias=1.0).then_inc(ln_ready, 1)
                if not last:
                    norm_ln(ft + 1)
                    bc_copy(ft + 1, 1 - par)
                    norm_exp(ft + 1, ft * 3 + 4)
                    v_copy(ft + 1, 1 - par)
                act.wait_ge(zs_ready, ft + 1)
                s.activation(w_t[:, :, :, :].rearrange("p h m t -> p h (m t)"), z, ACT.Exp).then_inc(w_ready, 1)
                act.wait_ge(av_ready, ft * 2 + 3)
                s.activation(uqkv[:, ds(ft + KS, 1), :], ps(3, 0, T).unsqueeze(1), ACT.Copy).then_inc(attn_ready, 1)

            act.wait_ge(cols_ready, 2)
            copies(0, 0)
            norm_ln(0)
            norm_exp(0, 1)
            bc_copy(0, 0)
            v_copy(0, 0)
            mixer(0, 0)
            mixer(1, 1)
            with act.Fori(1, KS // 2 - 1) as pair:
                for par in range(2):
                    mixer(pair * 2 + par, par)
            mixer(KS - 2, 0)
            mixer(KS - 1, 1, last=True)

            def square(j, src):
                if j >= 2:
                    act.wait_ge(msq_used, j - 1)
                s.activation(msq[:, j % 2, :, :], src, ACT.Square).then_inc(msq_ready, 1)

            def mixed_high(j):
                t0 = (2 * j + KS) % KD
                act.wait_ge(mf_ready, j + 1)
                s.activation(xs[:, t0:t0 + 2, 0:T], mix_f[:, j % 2, :, :], ACT.Copy).then_inc(mhi_ready, 1)

            def gelu(j):
                act.wait_ge(y_ready, 2 * j + 3)
                s.activation(uqkv[:, 2 * j:2 * j + 2, :], uqkv[:, 2 * j:2 * j + 2, :], ACT.Gelu_apprx_tanh).then_inc(gelu_ready, 1)

            act.wait_ge(attn_ready, KS + 1)
            for j in range(4):
                square(j, uqkv[:, KS + 2 * j:KS + 2 * j + 2, :])
            for j in range(4):
                gelu(j)
            for j in range(4):
                act.wait_ge(gelu_ready, j + 1)
                s.activation(xs[:, 2 * j:2 * j + 2, 0:T], uqkv[:, 2 * j:2 * j + 2, :], ACT.Copy).then_inc(yhi_ready, 1)
            act.wait_ge(msq_used, 4)
            link(s.activation(rs2[:, 1, 0, :], ps(4, 0, T), ACT.Ln, bias=eps[:, 2:3]))
            s.activation(rs2[:, 1, 0, :], rs2[:, 1, 0, :], ACT.Exp, scale=-0.5).then_inc(mr_ready, 1)
            for c in range(SPL, GLU_B * GLU_C):
                high(GLU_C0 + c, c, 16 * (GLU_C0 // RAW + 1))
                mixed_high(c - SPL)
            for j in range(4):
                if j == 2:
                    for c in range(SPL):
                        high(OUT_C0 + c, c, 16 * (OUT_C0 // RAW + 1))
                act.wait_ge(acc_free, FB + GLU_B0 * FB + 2 * j + 2)
                s.activation(glu_s[:, :, :], glu_z[:, :, :], ACT.Sigmoid).then_inc(sig_ready, 1)
                act.wait_ge(y2_ready, j + 1)
                square(4 + j, uqkv[:, 2 * j:2 * j + 2, :])
            act.wait_ge(msq_used, 8)
            link(s.activation(rs2[:, 0, 0, :], ps(5, 0, T), ACT.Ln, bias=eps[:, 2:3]))
            s.activation(rs2[:, 0, 0, :], rs2[:, 0, 0, :], ACT.Exp, scale=-0.5).then_inc(mr_ready, 1)
            for j in range(4, 8):
                mixed_high(j)
                high(OUT_C0 + j, j, 16 * (OUT_C0 // RAW + 1))

            def h_square(j2, q):
                act.wait_ge(h_ready, j2 * 4 + (2 * q + 2))
                act.wait_ge(fsq_used, j2 * 2 + (q + 1))
                s.activation(msq[:, q, :, :], resid[:, ds(j2 * 4 + 2 * q, 2), :], ACT.Square).then_inc(fsq_ready, 1)

            with act.Fori(1, OUT_B) as b:
                for c in range(OUT_C):
                    high(b * OUT_C + (OUT_C0 + c), c, b * 16 + 16 * (OUT_C0 // RAW + 1))
                    if c in (4, 6):
                        h_square(b - 1, c // 2 - 2)

            UP_FULL = 16 * (UP_C0 // RAW)
            for c in range(SPL):
                high(UP_C0 + c, c, UP_FULL + 32)
            for q in range(2):
                h_square(OUT_B - 1, q)
            act.wait_ge(fss_ready, 1)
            link(s.activation(rstd[:, :], ps(4, 0, T), ACT.Ln, bias=eps[:, 0:1]))
            s.activation(rstd[:, :], rstd[:, :], ACT.Exp, scale=-0.5).then_inc(fr_ready, 1)
            for j in range(KD // 2):
                act.wait_ge(ff_ready, j + 1)
                s.activation(xs[:, 2 * j:2 * j + 2, 0:T], ffn_f[:, j % 2, :, :], ACT.Copy).then_inc(fhi_ready, 1)
                if SPL <= j + 1 < UP_C:
                    high(UP_C0 + j + 1, j + 1, UP_FULL + 32)

            def hidden_silu(blk):
                act.wait_ge(acc_free, blk * FB + (FB + UP_B0 * FB + 2))
                s.activation(act_tmp[:, :, :], ps(4), ACT.Silu).then_inc(g_act, 1)

            def hidden_high(blk, tile):
                act.wait_ge(h_prod, blk + 1)
                act.wait_ge(cols_ready, 2)
                s.activation(hid[:, tile, 0:T], act_tmp[:, :, :], ACT.Copy).then_inc(hid_hi, 1)

            with act.Fori(1, UP_B) as b:
                for c in range(UP_C):
                    high(b * UP_C + (UP_C0 + c), c, b * 32 + (UP_FULL + 32))
                    if c == 3:
                        hidden_silu(b - 1)
                    if c == 5:
                        hidden_high(b - 1, ds(b * 2 - 2, 2))
            DN_FULL = UP_FULL + 32 * UP_B
            for m in range(SPL):
                high(DN_C0 + m, m, DN_FULL + 16)
            hidden_silu(UP_B - 1)
            hidden_high(UP_B - 1, slice(KF - 2, KF))

            def out_copy(b):
                for i in range(2):
                    act.wait_ge(ot_ps, 2 * b + i + 5)
                    if b >= 2:
                        act.wait_ge(out_done, 32 * (b - 1))
                    s.activation(out_s[:, b % 2, i, :], ps(6 + i), ACT.Copy).then_inc(ot_ready, 1)

            for b in range(DN_B):
                for c in range(DN_C):
                    m = b * DN_C + c
                    if m >= SPL:
                        high(DN_C0 + m, m % RAW, DN_FULL + 16 * (m // RAW + 1))
                    if b and c == 12:
                        out_copy(b - 1)
            out_copy(DN_B - 1)

        @block.tensor
        def _(pe):
            mm = nc.tensor.matmul
            pe.sem_inc(chunk_done, SPL)
            pe.sem_inc(bc_ps, 1)
            pe.sem_inc(av_ready, 1)
            pe.sem_inc(fsq_used, 2)
            pe.sem_inc(ot_ps, 4)

            def chunk(value, c, rhs, blk=None, last=False):
                pe.wait_ge(lo_ready, value + 1)
                for f in range(FB):
                    if blk is not None:
                        pe.wait_ge(acc_free, blk * FB + f + 1)
                    for t in range(CK):
                        w_ = slice(f * P, (f + 1) * P)
                        mm(ps(f), hi[:, c % SPL, t, w_], rhs(t, 2 * T), start=blk is not None and t == 0, stop=False)
                        ins = mm(ps(f, 0, T), lo[:, c % SPL, t, w_], rhs(t, T), start=False, stop=last and t == CK - 1)
                    if last and f < FB - 1:
                        ins.then_inc(acc_ready, 1)
                ins.then_inc(chunk_done, 1)

            def of(src, kt):
                return lambda t, n: src[:, kt + t, 0:n]

            def ada_direct(ph, i, c, col=0, start=False):
                src, full, value = ada_slot(ph, i, c)
                pe.wait_ge(full, value)
                for t in range(CK):
                    for j in range(FB):
                        ins = mm(acc[:, 7, ds(col + j, 1)], src[:, t, j * P:(j + 1) * P], cs[:, CK * c + t:CK * c + t + 1],
                                 start=start and t + j == 0, stop=False, skip_group_check=True)
                ins.then_inc(ada_pe, 1)

            def mod_group(ph, i, buf=0, col=0, start=False):
                pe.wait_ge(ada_mac, i * ph.vper + (ph.v0 + ph.vper))
                for j in range(FB):
                    ins = mm(acc[:, 7, ds(col + j, 1)], ada_acc[:, buf, j * P:(j + 1) * P], ones[:, 0:1],
                             start=start and j == 0, stop=True, skip_group_check=True)
                ins.then_inc(ada_sum, 1)

            pe.wait_ge(cols_ready, 1)
            pe.wait_ge(rows_in, 16 * 12)
            nc.tensor.transpose(ps(0, 0, P), rows[:, 0, :], ident[:, :]).then_inc(rows_t, 1)
            nc.tensor.transpose(ps(1, 0, 106), rows[0:106, 1, :], ident[0:106, 0:106]).then_inc(rows_t, 1)
            pe.wait_ge(cols_ready, 2)
            pe.wait_ge(vec_ready, 2)
            pe.wait_ge(x_in, 32)
            def x_squares(j):
                pe.wait_ge(sqx_ready, j + 1)
                for q in range(2):
                    ins = mm(ps(4, 0, T), ones[:, :], sqx[:, j % 2, q, :], start=j + q == 0, stop=j == KD // 2 - 1 and q == 1)
                ins.then_inc(ssx_ready if j == KD // 2 - 1 else sqx_used, 1)

            for j in range(KD // 2):
                if j >= 4:
                    pe.wait_ge(xt_ready, j - 3)
                for q in range(2):
                    for i in range(2):
                        kt = 2 * j + q
                        ins = nc.tensor.transpose(ps(j % 4, (2 * q + i) * P, P), x_tok[:, i, kt * P:(kt + 1) * P], ident[:, :])
                ins.then_inc(xt_ps, 1)
                if j >= 2:
                    x_squares(j - 2)
                if j == 0:
                    pe.wait_ge(cs_ready, 1)
                if j in PRE.tensor:
                    ada_direct(PRE, 0, j, start=j == PRE.tensor[0])
            x_squares(KD // 2 - 2)
            x_squares(KD // 2 - 1)
            mod_group(PRE, 0)

            def pre_group(g, buf):
                for c in PRE.tensor:
                    ada_direct(PRE, g, c, g * FB)
                mod_group(PRE, g, buf, g * FB)

            pre_group(1, 1)
            with pe.Fori(1, PRE.count // 2) as pair:
                for q in range(2):
                    pre_group(pair * 2 + q, q)

            for c in range(IN_C):
                pe.wait_ge(xlo_ready, c // 2 + 1)
                chunk(c, c, of(xs, 2 * c), blk=0 if c == 0 else None, last=c == IN_C - 1)
            pe.wait_ge(mod_ready, INP.g0)
            mod_group(INP, 0, start=True)
            with pe.Fori(1, IN_B) as b:
                for c in range(IN_C):
                    chunk(b * IN_C + c, c, of(xs, 2 * c), blk=b if c == 0 else None, last=c == IN_C - 1)
                pe.wait_ge(mod_ready, b + INP.g0)
                mod_group(INP, b, start=True)

            pe.wait_ge(acc_free, FB + IN_B * FB)
            pe.wait_ge(tab_ready, 1)

            def bu(par, i, ft):
                pe.wait_ge(bu_used, ft * 4 + (i + 1))
                r = slice(32 * i, 32 * i + 32)
                for q in range(2):
                    ins = mm(ps(4 + i % 2, q * T, T), bc[r, par, q, :], u_st[r, par, :], start=q == 0, stop=True, skip_group_check=True)
                ins.then_inc(bu_ready, 1)

            def c_y(par, i, ft):
                pe.wait_ge(rem_ready, ft * 4 + (i + 1))
                for q in range(4):
                    ins = mm(acc[32 * i:32 * i + 32, 6, 0:T], bc[:, par, 2 + q // 2, 32 * i:32 * i + 32], rem[:, i % 2, q, :],
                             start=q == 0, stop=q == 3)
                ins.then_inc(rem_used, 1)

            def scores(h):
                hr = slice(DH * h, DH * h + DH)
                zz = lambda a_, n_: ps(h, a_, n_)
                mm(zz(0, 256), qk_n[hr, 1, 0:P], qk_n[hr, 0, :], start=True, stop=False, skip_group_check=True)
                mm(zz(256, P), qk_n[hr, 1, P:T], qk_n[hr, 0, P:T], start=False, stop=False, skip_group_check=True)
                mm(zz(0, P), ident_b[:, :], mask_b[:, :], start=False, stop=False, skip_group_check=True)
                return mm(zz(256, P), ident_b[:, :], mask_b[:, :], start=False, stop=True, skip_group_check=True)

            def keep(h):
                mm(ps(h, 0, 256), neg_tri[:, :], sp[:, h, 0:2, :], start=False, stop=False, skip_group_check=True)
                mm(ps(h, P, P), neg_ones[:, :], sp[:, h, 2, :], start=False, stop=False, skip_group_check=True)
                return mm(ps(h, 256, P), neg_tri[:, :], sp[:, h, 2, :], start=False, stop=True, skip_group_check=True)

            def values(h, par):
                hr = slice(DH * h, DH * h + DH)
                mm(acc[hr, 3, 0:T], v_t[:, par, 0, hr], w_t[:, h, 0:2, :], start=True, stop=False)
                mm(acc[hr, 3, P:T], v_t[:, par, 1, hr], w_t[:, h, 2, :], start=False, stop=True).then_inc(av_ready, 1)

            def prepare(ft, par):
                later = not (isinstance(ft, int) and ft == 0)
                if later:
                    pe.wait_ge(qt_ready, ft)
                pe.wait_ge(qsq_ready, ft + 1)
                mm(ps(7), head_ones[:, :], qk_a[:, :, :], start=True, stop=True).then_inc(qss_ready, 1)
                if later:
                    bu(1 - par, 3, ft - 1)
                    pe.wait_ge(vt_ready, ft)
                pe.wait_ge(bcx_ready, ft * 4 + 4)
                for q in range(2):
                    nc.tensor.transpose(ps(2, q * P, P), bx[:, q, :, :, :].rearrange("p i g h -> p (i g h)"), ident[:, :])
                for q in range(2):
                    ins = nc.tensor.transpose(ps(2, (2 + q) * P, P), cx[:, q, :, :].rearrange("p g n -> p (g n)"), ident[:, :])
                ins.then_inc(bc_ps, 1)

            def value_rows(ft):
                pe.wait_ge(vst_ready, ft + 1)
                pe.wait_ge(bc_ready, ft + 1)
                for i in range(2):
                    ins = nc.tensor.transpose(ps(2, i * P, P), v_st[:, i * P:(i + 1) * P], ident[:, :])
                ins.then_inc(vt_ps, 1)

            def sum_sq(bank, j, j0):
                pe.wait_ge(msq_ready, j0 + j + 1)
                for q in range(2):
                    ins = mm(ps(bank, 0, T), ones[:, :], msq[:, (j0 + j) % 2, q, :], start=j + q == 0, stop=j == 3 and q == 1)
                ins.then_inc(msq_used, 1)

            def mixer(ft, par, last=False):
                bu(par, 2, ft)
                pe.wait_ge(qkn_ready, ft + 1)
                pe.wait_ge(w_ready, ft + 1)
                scores(0)
                scores(1).then_inc(z_ready, 1)
                if last:
                    bu(par, 3, ft)
                else:
                    prepare(ft + 1, 1 - par)
                pe.wait_ge(y_ready, ft + 1)
                c_y(par, 0, ft)
                if not last:
                    value_rows(ft + 1)
                c_y(par, 1, ft)
                if not last:
                    pe.wait_ge(u_ready, ft + 2)
                    bu(1 - par, 0, ft + 1)
                pe.wait_ge(sp_ready, ft + 1)
                keep(0)
                keep(1).then_inc(zs_ready, 1)
                pe.wait_ge(w_ready, ft + 2)
                pe.wait_ge(vt_ready, ft + 1)
                pe.wait_ge(attn_ready, ft + 1)
                for h in range(2):
                    values(h, par)
                c_y(par, 2, ft)
                if not last:
                    bu(1 - par, 1, ft + 1)
                else:
                    pe.wait_ge(bu_used, KS * 4 + 1)
                    for j in range(3):
                        sum_sq(4, j, 0)
                c_y(par, 3, ft)
                if last:
                    sum_sq(4, 3, 0)

            pe.sem_inc(w_ready, 1)
            pe.wait_ge(mod_ready, MID.g0)
            prepare(0, 0)
            value_rows(0)
            pe.wait_ge(u_ready, 1)
            bu(0, 0, 0)
            bu(0, 1, 0)
            mixer(0, 0)
            mixer(1, 1)
            with pe.Fori(1, KS // 2 - 1) as pair:
                for par in range(2):
                    mixer(pair * 2 + par, par)
            mixer(KS - 2, 0)
            mixer(KS - 1, 1, last=True)

            for c in range(GLU_B * GLU_C):
                b = c // GLU_C
                if c < GLU_C:
                    pe.wait_ge(ylo_ready, c + 1)
                chunk(GLU_C0 + c, c, of(xs, 2 * (c % GLU_C)), blk=GLU_B0 + b if c % GLU_C == 0 else None,
                      last=c % GLU_C == GLU_C - 1)
            sum_sq(5, 0, 4)
            sum_sq(5, 1, 4)

            def h_sum(j2, q, first=False, last=False):
                pe.wait_ge(fsq_ready, j2 * 2 + (q + 1))
                for i in range(2):
                    ins = mm(ps(4, 0, T), ones[:, :], msq[:, q, i, :], start=first and i == 0, stop=last and i == 1)
                ins.then_inc(fss_ready if last else fsq_used, 1)

            def out_block(b):
                for c in range(OUT_C):
                    chunk(b * OUT_C + (OUT_C0 + c), c, of(xs, (2 * c + KS) % KD), blk=b + OUT_B0 if c == 0 else None,
                          last=c == OUT_C - 1)
                pe.wait_ge(mod_ready, b + MID.g0)
                mod_group(MID, b, start=True)

            for c in range(OUT_C):
                pe.wait_ge(mlo_ready, c + 1)
                chunk(OUT_C0 + c, c, of(xs, (2 * c + KS) % KD), blk=OUT_B0 if c == 0 else None, last=c == OUT_C - 1)
                if c == 0:
                    sum_sq(5, 2, 4)
                    sum_sq(5, 3, 4)
            mod_group(MID, 0, start=True)
            out_block(1)
            pe.wait_ge(mr_done, 2)
            for q in range(2):
                h_sum(0, q, first=q == 0)
            with pe.Fori(2, OUT_B) as b:
                out_block(b)
                for q in range(2):
                    h_sum(b - 1, q)
            for q in range(2):
                h_sum(OUT_B - 1, q, last=q == 1)

            def up_block(b):
                for c in range(UP_C):
                    chunk(b * UP_C + (UP_C0 + c), c, of(xs, 2 * c), blk=b + UP_B0 if c == 0 else None, last=c == UP_C - 1)

            for c in range(UP_C):
                pe.wait_ge(flo_ready, c + 1)
                chunk(UP_C0 + c, c, of(xs, 2 * c), blk=UP_B0 if c == 0 else None, last=c == UP_C - 1)
            for c in range(UP_C):
                chunk(UP_C + UP_C0 + c, c, of(xs, 2 * c), blk=UP_B0 + 1 if c == 0 else None, last=c == UP_C - 1)
            pe.wait_ge(mod_ready, UPG.g0)
            mod_group(UPG, 0, start=True)
            with pe.Fori(1, 4) as g:
                up_block(g * 2)
                up_block(g * 2 + 1)
                pe.wait_ge(mod_ready, g + UPG.g0)
                mod_group(UPG, g, start=True)
            with pe.Fori(8, UP_B) as b:
                up_block(b)

            def rows_out(b, par):
                pe.wait_ge(o_ready, b + 1)
                pe.wait_ge(ot_ready, b * 2 + 2)
                for i in range(2):
                    for f in range(FB):
                        ins = nc.tensor.transpose(ps(6 + i, f * P, P), h_out[:, par, f, i * P:(i + 1) * P], ident[:, :])
                    ins.then_inc(ot_ps, 1)

            with pe.Fori(0, DN_B // 2) as pair:
                for par in range(2):
                    b = pair * 2 + par
                    for c in range(DN_C):
                        m = par * DN_C + c
                        pe.wait_ge(hid_lo, c + 1)
                        chunk(pair * (2 * DN_C) + (DN_C0 + m), m, of(hid, 2 * c), blk=b + DN_B0 if c == 0 else None,
                              last=c == DN_C - 1)
                        if par and c == 7:
                            rows_out(b - 1, 0)
                rows_out(pair * 2 + 1, 1)

        @block.vector
        def _(dve):
            v = nc.vector
            n = [0]

            def link(ins):
                n[0] += 1
                ins.then_inc(dve_chain, 1)
                dve.wait_ge(dve_chain, n[0])

            dve.sem_inc(acc_free, FB)
            dve.sem_inc(bu_used, 2)
            dve.sem_inc(attn_ready, 1)
            dve.sem_inc(y_ready, 1)
            dve.sem_inc(ot_ready, 2)

            def ada_chunks(ph, i, c0=0, c1=ADA_C, buf=0):
                first = isinstance(i, int) and i == 0
                if c0 == 0:
                    if ph is not PRE:
                        dve.wait_ge(ada_sum, i + ph.g0)
                    elif not isinstance(i, int) or i >= 2:
                        dve.wait_ge(ada_sum, i - 1)
                for c in range(c0, c1):
                    if c in ph.tensor:
                        continue
                    slot, full, value = ada_slot(ph, i, c)
                    dve.wait_ge(full, value)
                    for t in range(CK):
                        kt = CK * c + t
                        src, col, dst = slot[:, t, :], cs[:, kt:kt + 1], ada_acc[:, buf, :]
                        if kt == 0:
                            v.tensor_scalar(dst, src, col, None, ALU.mult).then_inc(ada_mac, 1)
                        else:
                            dve.wait_ge(ada_mac, ph.used(i, c)[1] - CK + t)
                            v.scalar_tensor_tensor(dst, src, col, dst, ALU.mult, ALU.add).then_inc(ada_mac, 1)

            def ada_mods(ph, i):
                dve.wait_ge(ada_sum, i + (ph.g0 + 1))
                dve.wait_ge(cs_ready, 1)
                cols = ds((i + ph.g0) * FB, FB)
                v.tensor_tensor(mods[:, cols], vec1[:, cols], ps(7, 0, FB), ALU.add).then_inc(mod_ready, 1)

            dve.wait_ge(cs_ready, 1)
            def newton(r, scratch, total, e):
                link(v.scalar_tensor_tensor(scratch, total, e, r, ALU.add, ALU.mult))
                link(v.tensor_tensor(scratch, scratch, r, ALU.mult))
                link(v.tensor_scalar(scratch, scratch, -0.5, 1.5, ALU.mult, ALU.add))
                return v.tensor_tensor(r, r, scratch, ALU.mult)

            dve.wait_ge(vec_ready, 2)
            den, den_im = tiny[:, 23, :], tiny[:, 22, :]
            link(v.tensor_tensor(den, vec2[:, 40:72], vec2[:, 40:72], ALU.mult))
            link(v.tensor_tensor(den_im, vec2[:, 72:104], vec2[:, 72:104], ALU.mult))
            link(v.tensor_tensor(den, den, den_im, ALU.add))
            v.reciprocal(den, den).then_inc(den_ready, 1)
            ada_chunks(PRE, 0)
            ada_chunks(PRE, 1, buf=1)
            dve.wait_ge(rx_ready, 1)
            link(newton(rstd[:, :], nrm[:, :], ps(4, 0, T), D * EPS))
            dve.wait_ge(ssx_ready, 1)
            for j in range(4):
                link(v.tensor_tensor(x_n[:, 4 * j:4 * j + 4, :], resid[:, 4 * j:4 * j + 4, :],
                                     rstd[:, :].unsqueeze(1).to_broadcast([P, 4, T]), ALU.mult))
            with dve.Fori(1, PRE.count // 2) as pair:
                for q in range(2):
                    ada_chunks(PRE, pair * 2 + q, buf=q)
            dve.wait_ge(ada_sum, PRE.count)
            link(v.tensor_tensor(mods[:, 0:PRE.count * FB], vec1[:, 0:PRE.count * FB], ps(7, 0, PRE.count * FB), ALU.add))
            dve.sem_inc(mod_ready, PRE.count)
            def modulate(dst, gain, scale):
                link(v.tensor_scalar(dst, gain, math.sqrt(D), None, ALU.mult, ALU.bypass))
                link(v.scalar_tensor_tensor(dst, scale, 1.0, dst, ALU.add, ALU.mult))

            modulate(a_mix[:, :], vec1[:, 112:128], mods[:, KD:2 * KD])
            for j in range(5):
                if j < 4:
                    for kt in range(4 * j, 4 * j + 4):
                        v.tensor_scalar(x_n[:, kt, :], x_n[:, kt, :], a_mix[:, kt:kt + 1], mods[:, kt:kt + 1],
                                        ALU.mult, ALU.add).then_inc(xf_ready if kt % 4 == 3 else dve_step, 1)
                if j:
                    dve.wait_ge(xhi_ready, j)
                    sl = slice(4 * j - 4, 4 * j)
                    v.tensor_tensor(xs[:, sl, T:2 * T], x_n[:, sl, :], xs[:, sl, 0:T].bitcast(f32), ALU.subtract).then_inc(xlo_ready, 1)

            def bank_wait(f, blk, end_chunk):
                if f < FB - 1:
                    dve.wait_ge(acc_ready, blk * (FB - 1) + (f + 1))
                else:
                    dve.wait_ge(chunk_done, end_chunk + SPL)

            def halves(bank):
                return ps(bank).rearrange("p (h t) -> p t h", h=2)

            def projected(b):
                for f in range(FB):
                    bank_wait(f, b, b * IN_C + IN_C)
                    v.tensor_reduce(uqkv[:, ds(b * FB + f, 1), :].rearrange("p o t -> p (o t)"), halves(f), AX.X, ALU.add).then_inc(acc_free, 1)

            ada_chunks(INP, 0)
            projected(0)
            dve.wait_ge(lam_ready, 1)
            dve.wait_ge(b_in, 32)
            f_re = tiny[:, 2, :].unsqueeze(2).to_broadcast([P, ST, GH])
            f_im = tiny[:, 3, :].unsqueeze(2).to_broadcast([P, ST, GH])
            b0, b1 = btmp[:, 0, :, :], btmp[:, 1, :, :]
            link(v.tensor_tensor(b0, b_raw[:, 0, :, :], f_re, ALU.mult))
            link(v.tensor_tensor(b1, b_raw[:, 1, :, :], f_im, ALU.mult))
            link(v.tensor_tensor(b_bar[:, 0, :, :], b0, b1, ALU.subtract))
            link(v.tensor_tensor(b0, b_raw[:, 1, :, :], f_re, ALU.mult))
            link(v.tensor_tensor(b1, b_raw[:, 0, :, :], f_im, ALU.mult))
            v.tensor_tensor(b_bar[:, 1, :, :], b0, b1, ALU.add).then_inc(bbar_ready, 1)
            dve.wait_ge(bbar_ready, 1)

            ada_mods(INP, 0)
            with dve.Fori(1, IN_B) as b:
                ada_chunks(INP, b)
                projected(b)
                ada_mods(INP, b)

            dve.wait_ge(tab_ready, 1)
            gains = vec2[:, 104:106]
            link(v.tensor_scalar(gains[:, 0:1], gains[:, 0:1], math.sqrt(2), None, ALU.mult, ALU.bypass))
            link(v.tensor_scalar(gains[:, 1:2], gains[:, 1:2], math.sqrt(2 * DH), None, ALU.mult, ALU.bypass))
            NCH = 8

            def chunked(ap):
                return ap.rearrange("p (c t) -> p c t", c=NC)

            def table(tile):
                tb = [tabs[:, q, ds(tile, 1), :].rearrange("p o t -> p (o t)") for q in range(2)]
                return tb, [x.unsqueeze(1).to_broadcast([P, NC, TC]) for x in tb]

            def s5_turn(ft, i):
                tile = ft * 4 + i
                _, (cosb, nsinb) = table(tile)
                bre, bim = chunked(ps(4 + i % 2, 0, T)), chunked(ps(4 + i % 2, T, T))
                dm = [chunked(dem[:, i % 2, q, :]) for q in range(4)]
                dve.wait_ge(bu_ready, tile + 1)
                v.tensor_tensor(dm[0], bre, cosb, ALU.mult)
                v.tensor_tensor(dm[1], bim, nsinb, ALU.mult)
                v.tensor_tensor(dm[2], bim, cosb, ALU.mult)
                v.tensor_tensor(dm[3], bre, nsinb, ALU.mult).then_inc(bu_used, 1)

            def s5_scan(ft, i):
                tile = ft * 4 + i
                base = tile * NCH
                k = [0]

                def step(ins):
                    k[0] += 1
                    ins.then_inc(s5_chain, 1)

                def need(m):
                    dve.wait_ge(s5_chain, base + m)

                tb, (cosb, nsinb) = table(tile)
                vre, vim = v_y[:, i % 2, 0, :], v_y[:, i % 2, 1, :]
                rr = vec2[:, ds(tile + 40, 1)].to_broadcast([P, TC])
                dve.wait_ge(v_ready, tile * 2 + 2)
                step(v.tensor_tensor_scan(vre[:, 0:TC], rr, vre[:, 0:TC], 0.0, ALU.mult, ALU.add))
                step(v.tensor_tensor_scan(vim[:, 0:TC], rr, vim[:, 0:TC], 0.0, ALU.mult, ALU.add))
                c128, s128 = tb[0][:, TC - 1:TC], tb[1][:, TC - 1:TC]
                lre, lim = vre[:, TC - 1:TC], vim[:, TC - 1:TC]
                need(1)
                step(v.tensor_scalar(carry[:, 1:2], lre, s128, None, ALU.mult, ALU.bypass))
                need(2)
                step(v.tensor_scalar(carry[:, 0:1], lim, s128, None, ALU.mult, ALU.bypass))
                need(3)
                step(v.scalar_tensor_tensor(carry[:, 3:4], lim, c128, carry[:, 1:2], ALU.mult, ALU.subtract))
                need(4)
                step(v.scalar_tensor_tensor(carry[:, 2:3], lre, c128, carry[:, 0:1], ALU.mult, ALU.add))
                need(5)
                step(v.tensor_tensor_scan(vim[:, TC:T], rr, vim[:, TC:T], carry[:, 3:4], ALU.mult, ALU.add))
                need(6)
                step(v.tensor_tensor_scan(vre[:, TC:T], rr, vre[:, TC:T], carry[:, 2:3], ALU.mult, ALU.add))
                dve.wait_ge(rem_used, tile + 1)
                yre, yim = chunked(vre), chunked(vim)
                rm = [chunked(rem[:, i % 2, q, :]) for q in range(4)]
                need(7)
                v.tensor_tensor(rm[1], yim, nsinb, ALU.mult)
                v.tensor_tensor(rm[3], yim, cosb, ALU.mult)
                need(8)
                v.scalar_tensor_tensor(rm[2], yre, -1.0, nsinb, ALU.mult, ALU.mult)
                v.tensor_tensor(rm[0], yre, cosb, ALU.mult).then_inc(rem_ready, 1)
                assert k[0] == NCH, k

            def qk_vr(ft):
                dve.wait_ge(qr_ready, ft + 1)
                v.scalar_tensor_tensor(qk_a[:, :, :], ps(7).rearrange("p (m t) -> p m t", m=2), DH * EPS, qk_r[:, :, :],
                                       ALU.add, ALU.mult).then_inc(qt_ready, 1)

            def qk_norm(ft):
                dve.wait_ge(qrn_ready, ft + 1)
                for m in range(2):
                    ins = v.scalar_tensor_tensor(qk_n[:, m, :].unsqueeze(1), uqkv[:, ds(ft + KS * (m + 1), 1), :], gains[:, m:m + 1],
                                                 qk_r[:, m, :].unsqueeze(1), ALU.mult, ALU.mult)
                    ins.then_inc(qkn_ready if m else dve_step, 1)

            def s5_out(ft):
                dve.wait_ge(rem_used, ft * 4 + 6)
                ut = uqkv[:, ds(ft, 1), :].rearrange("p o t -> p (o t)")
                v.scalar_tensor_tensor(ut, ut, vec2[:, ds(ft + 32, 1)], ps(6, 0, T), ALU.mult, ALU.add).then_inc(y_ready, 1)

            def mixer(ft, first=False, last=False):
                s5_turn(ft, 1)
                s5_scan(ft, 0)
                if not first:
                    s5_out(ft - 1)
                s5_turn(ft, 2)
                s5_scan(ft, 1)
                dve.wait_ge(ln_ready, ft + 1)
                v.scalar_tensor_tensor(sp[:, :, :, :].rearrange("p h m t -> p h (m t)"), acc[:, 0:2, 0:384], 0.0,
                                       sp[:, :, :, :].rearrange("p h m t -> p h (m t)"), ALU.max, ALU.add).then_inc(sp_ready, 1)
                s5_turn(ft, 3)
                if not last:
                    qk_vr(ft + 1)
                s5_scan(ft, 2)
                if not last:
                    qk_norm(ft + 1)
                    s5_turn(ft + 1, 0)
                s5_scan(ft, 3)

            dve.sem_inc(rem_used, 2)
            qk_vr(0)
            s5_turn(0, 0)
            qk_norm(0)
            mixer(0, first=True)
            mixer(1)
            with dve.Fori(1, KS // 2 - 1) as pair:
                for par in range(2):
                    mixer(pair * 2 + par)
            mixer(KS - 2)
            mixer(KS - 1, last=True)
            s5_out(KS - 1)

            for j in range(4):
                dve.wait_ge(yhi_ready, j + 1)
                sl = slice(2 * j, 2 * j + 2)
                v.tensor_tensor(xs[:, sl, T:2 * T], uqkv[:, sl, :], xs[:, sl, 0:T].bitcast(f32), ALU.subtract).then_inc(ylo_ready, 1)
            gw = vec2[:, 16:32]
            link(v.tensor_scalar(gw, gw, math.sqrt(SW), None, ALU.mult, ALU.bypass))
            dve.wait_ge(mr_ready, 1)
            link(newton(rs2[:, 1, 0, :], rs2[:, 1, 1, :], ps(4, 0, T), SW * EPS))
            dve.sem_inc(mr_done, 1)

            def mixed(j, kind):
                if j >= 2:
                    dve.wait_ge(mlo_ready, j - 1)
                t0 = (2 * j + KS) % KD
                for q in range(2):
                    v.scalar_tensor_tensor(mix_f[:, j % 2, q, :], uqkv[:, t0 + q, :], gw[:, t0 + q:t0 + q + 1], rs2[:, kind, 0, :],
                                           ALU.mult, ALU.mult).then_inc(mf_ready if q else dve_step, 1)

            def mixed_low(j):
                t0 = (2 * j + KS) % KD
                dve.wait_ge(mf_ready, j + 1)
                dve.wait_ge(mhi_ready, j + 1)
                v.tensor_tensor(xs[:, t0:t0 + 2, T:2 * T], mix_f[:, j % 2, :, :], xs[:, t0:t0 + 2, 0:T].bitcast(f32),
                                ALU.subtract).then_inc(mlo_ready, 1)

            def mix(first, kind):
                mixed(first, kind)
                for j in range(first, first + 4):
                    if j < first + 3:
                        mixed(j + 1, kind)
                    mixed_low(j)

            mix(0, 1)
            for j in range(4):
                b = j // 2
                if j:
                    dve.wait_ge(sig_ready, j)
                for q in range(2):
                    f = (2 * j + q) % FB
                    bank_wait(f, GLU_B0 + b, GLU_C0 + (b + 1) * GLU_C)
                    v.tensor_reduce(glu_z[:, q, :], halves(f), AX.X, ALU.add).then_inc(acc_free, 1)
                dve.wait_ge(sig_ready, j + 1)
                sl = slice(2 * j, 2 * j + 2)
                v.tensor_tensor(uqkv[:, sl, :], uqkv[:, sl, :], glu_s[:, :, :], ALU.mult).then_inc(y2_ready, 1)
            dve.wait_ge(y2_ready, 4)
            dve.wait_ge(mr_ready, 2)
            link(newton(rs2[:, 0, 0, :], rs2[:, 0, 1, :], ps(5, 0, T), SW * EPS))
            dve.sem_inc(mr_done, 1)
            mix(4, 0)

            for b in range(OUT_B):
                ada_chunks(MID, b)
                for f in range(FB):
                    kt = b * FB + f
                    bank_wait(f, OUT_B0 + b, OUT_C0 + (b + 1) * OUT_C)
                    v.tensor_reduce(act_tmp[:, f % 2, :], halves(f), AX.X, ALU.add).then_inc(acc_free, 1)
                    dve.wait_ge(acc_free, FB + (OUT_B0 + b) * FB + f + 1)
                    v.scalar_tensor_tensor(resid[:, kt, :], act_tmp[:, f % 2, :], mods[:, 2 * KD + kt:2 * KD + kt + 1], resid[:, kt, :],
                                           ALU.mult, ALU.add).then_inc(h_ready, 1)
                ada_mods(MID, b)
            modulate(a_ffn[:, :], vec2[:, 0:16], mods[:, 4 * KD:5 * KD])
            dve.wait_ge(fr_ready, 1)
            link(newton(rstd[:, :], rs2[:, 0, 1, :], ps(4, 0, T), D * EPS))
            def ffn_in(j):
                if j >= 2:
                    dve.wait_ge(flo_ready, j - 1)
                for q in range(2):
                    kt = 2 * j + q
                    ins = v.scalar_tensor_tensor(ffn_f[:, j % 2, q, :], resid[:, kt, :], a_ffn[:, kt:kt + 1], rstd[:, :], ALU.mult, ALU.mult)
                    link(ins)
                for q in range(2):
                    kt = 2 * j + q
                    v.tensor_scalar(ffn_f[:, j % 2, q, :], ffn_f[:, j % 2, q, :], mods[:, 3 * KD + kt:3 * KD + kt + 1], None,
                                    ALU.add, ALU.bypass).then_inc(ff_ready if q else dve_step, 1)

            ffn_in(0)
            for j in range(KD // 2):
                if j < KD // 2 - 1:
                    ffn_in(j + 1)
                dve.wait_ge(ff_ready, j + 1)
                dve.wait_ge(fhi_ready, j + 1)
                v.tensor_tensor(xs[:, 2 * j:2 * j + 2, T:2 * T], ffn_f[:, j % 2, :, :], xs[:, 2 * j:2 * j + 2, 0:T].bitcast(f32),
                                ALU.subtract).then_inc(flo_ready, 1)

            def hidden(b):
                end = b * UP_C + (UP_C0 + UP_C)
                blk = b + UP_B0
                for f in range(FB):
                    bank_wait(f, blk, end)
                    ins = v.tensor_reduce(ps(4 + f // 2, (f % 2) * T, T), halves(f), AX.X, ALU.add)
                    ins.then_inc(acc_free, 1)
                dve.wait_ge(g_act, b + 1)
                dve.wait_ge(acc_free, blk * FB + (FB + 4))
                v.tensor_tensor(act_tmp[:, :, :], ps(5).rearrange("p (m t) -> p m t", m=2), act_tmp[:, :, :], ALU.mult).then_inc(h_prod, 1)
                dve.wait_ge(hid_hi, b + 1)
                dve.wait_ge(cs_ready, 1)
                tl = ds(b * 2, 2)
                v.tensor_tensor(hid[:, tl, T:2 * T], act_tmp[:, :, :], hid[:, tl, 0:T].bitcast(f32), ALU.subtract).then_inc(hid_lo, 1)

            with dve.Fori(0, 4) as g:
                ada_chunks(UPG, g, 0, 4)
                hidden(g * 2)
                ada_chunks(UPG, g, 4, 8)
                hidden(g * 2 + 1)
                ada_mods(UPG, g)
            with dve.Fori(8, UP_B) as b:
                hidden(b)

            with dve.Fori(0, DN_B // 2) as pair:
                for par in range(2):
                    for f in range(FB):
                        blk = pair * 2 + par
                        kt = blk * FB + f
                        bank_wait(f, blk + DN_B0, blk * DN_C + (DN_C0 + DN_C))
                        v.tensor_reduce(act_tmp[:, f % 2, :], halves(f), AX.X, ALU.add).then_inc(acc_free, 1)
                        dve.wait_ge(ot_ps, blk * 2 + 2)
                        dve.wait_ge(acc_free, blk * FB + (FB + DN_B0 * FB + f + 1))
                        v.scalar_tensor_tensor(h_out[:, par, f:f + 1, :], act_tmp[:, f % 2, :].unsqueeze(1),
                                               mods[:, ds(kt + 5 * KD, 1)], resid[:, ds(kt, 1), :],
                                               ALU.mult, ALU.add).then_inc(o_ready if f == FB - 1 else dve_step, 1)


_VEC = ["c", "b_ada", "g_mix", "log_dt", "q_gain", "k_gain", "g_ssm_out", "g_attn_out", "g_ffn"]
_MAT = ["x", "w_ada", "w_in", "a_re", "a_im", "b_re", "b_im", "c_re", "c_im", "d_skip", "w_glu", "w_out",
        "w_gate", "w_up", "w_down"]


def kernel(**inputs):
    import numpy as _np
    import concourse.bacc as _bacc
    from concourse import mybir as _mybir
    from concourse.bass_utils import run_bass_kernel_spmd as _run

    nc = _bacc.Bacc("TRN2", target_bir_lowering=False, num_devices=1)
    arrays, args = {}, {}
    for name in _VEC + _MAT:
        v = _np.ascontiguousarray(inputs[name])
        v = v.reshape(v.shape[1:])
        arrays[f"in_{name}"] = v
        args[name] = nc.dram_tensor(f"in_{name}", v.shape, _mybir.dt.from_np(v.dtype), kind="ExternalInput").ap()
    args["out"] = nc.dram_tensor("out_h", (T, D), _mybir.dt.float32, kind="ExternalOutput").ap()
    build(nc, args)
    r = _run(nc, [arrays], core_ids=[0])
    return r.results[0]["out_h"].reshape(1, T, D)
```
